# Optimizing a Trainium2 kernel written in Bass

```python
import jax
import jax.numpy as jnp
from jax import lax
import numpy as np
import math
import jax, jax.numpy as jnp

D_MODEL = 1024
BATCH = 1
SEQ = 512
DEPTH = 2

N_GROUPS = 4
HEADS = 4
HEAD_DIM = 64
D_GROUP = HEADS * HEAD_DIM
D_MIX = N_GROUPS * D_GROUP
D_FF = 2816
Q_BLOCK = 128
ROPE_THETA = 10000.0
MLA_Q_RANK = 256
MLA_KV_RANK = 128
MLA_D_NOPE = 64
MLA_D_ROPE = 32
MLA_D_V = 64
NSA_CMP_LEN = 32
NSA_CMP_STRIDE = 16
NSA_SEL_LEN = 64
NSA_N_SEL = 8
NSA_N_INIT = 1
NSA_N_LOCAL = 2
NSA_WINDOW = 512
DSA_TOPK = 256
DSA_IDX_HEADS = 8
DSA_IDX_DIM = 32
DN_ALPHA = (2.0 * DEPTH) ** 0.25
DN_BETA = (8.0 * DEPTH) ** -0.25
LN_EPS = 1e-5
RMS_EPS = 1e-6
NEG_INF = -1e30
FORCE_SCORE = 1e4

IN_SPLITS = (
    ('mla_cq', MLA_Q_RANK), ('mla_ckv', MLA_KV_RANK), ('mla_krope', MLA_D_ROPE),
    ('nsa_q', D_GROUP), ('nsa_k_cmp', HEAD_DIM), ('nsa_v_cmp', HEAD_DIM),
    ('nsa_k_slc', HEAD_DIM), ('nsa_v_slc', HEAD_DIM), ('nsa_k_win', HEAD_DIM),
    ('nsa_v_win', HEAD_DIM), ('nsa_gate', 3 * HEADS),
    ('dsa_q', D_GROUP), ('dsa_k', HEAD_DIM), ('dsa_v', HEAD_DIM),
    ('idx_q', DSA_IDX_HEADS * DSA_IDX_DIM), ('idx_k', DSA_IDX_DIM), ('idx_w', DSA_IDX_HEADS),
    ('sb_q', D_GROUP), ('sb_k', D_GROUP), ('sb_v', D_GROUP),
)
D_IN = sum(w for _, w in IN_SPLITS)


def layer_norm(x, g, b):
    xf = x.astype(jnp.float32)
    mu = jnp.mean(xf, -1, keepdims=True)
    var = jnp.mean(jnp.square(xf - mu), -1, keepdims=True)
    return ((xf - mu) * lax.rsqrt(var + LN_EPS) * g + b).astype(x.dtype)

def rms_norm(x, g):
    xf = x.astype(jnp.float32)
    return (xf * lax.rsqrt(jnp.mean(xf * xf, -1, keepdims=True) + RMS_EPS) * g).astype(x.dtype)

def swiglu(x, w1, w3, w2):
    return (jax.nn.silu(x @ w1) * (x @ w3)) @ w2

def rope_tables(seq, dim):
    inv = ROPE_THETA ** (-jnp.arange(0, dim, 2, dtype=jnp.float32) / dim)
    ang = jnp.arange(seq, dtype=jnp.float32)[:, None] * inv[None, :]
    return jnp.cos(ang), jnp.sin(ang)

def apply_rope(z, cos, sin):
    shape = (cos.shape[0],) + (1,) * (z.ndim - 3) + (cos.shape[1],)
    c = cos.reshape(shape).astype(z.dtype)
    s = sin.reshape(shape).astype(z.dtype)
    z1, z2 = jnp.split(z, 2, axis=-1)
    return jnp.concatenate([z1 * c - z2 * s, z1 * s + z2 * c], axis=-1)

def masked_softmax(s, mask):
    s = jnp.where(mask, s, NEG_INF)
    e = jnp.where(mask, jnp.exp(s - jnp.max(s, -1, keepdims=True)), 0.0)
    return e / jnp.maximum(jnp.sum(e, -1, keepdims=True), 1e-30)

def unblock(y):
    nb, b, qb = y.shape[:3]
    return jnp.moveaxis(y, 0, 1).reshape((b, nb * qb) + y.shape[3:])

def split_columns(h):
    parts = {}
    off = 0
    for name, width in IN_SPLITS:
        parts[name] = h[..., off:off + width]
        off += width
    return parts

def mla_mixer(c_q, c_kv, k_rope, q_norm_g, w_uq, kv_norm_g, w_ukv, cos_r, sin_r):
    B, S, _ = c_q.shape
    q = (rms_norm(c_q, q_norm_g) @ w_uq).reshape(B, S, HEADS, MLA_D_NOPE + MLA_D_ROPE)
    q_nope = q[..., :MLA_D_NOPE]
    q_pe = apply_rope(q[..., MLA_D_NOPE:], cos_r, sin_r)
    kv = (rms_norm(c_kv, kv_norm_g) @ w_ukv).reshape(B, S, HEADS, MLA_D_NOPE + MLA_D_V)
    k_nope = kv[..., :MLA_D_NOPE]
    v = kv[..., MLA_D_NOPE:]
    k_pe = apply_rope(k_rope, cos_r, sin_r)
    scale = (MLA_D_NOPE + MLA_D_ROPE) ** -0.5
    k_pos = jnp.arange(S)

    def block(i):
        q0 = i * Q_BLOCK
        qn = lax.dynamic_slice_in_dim(q_nope, q0, Q_BLOCK, 1)
        qp = lax.dynamic_slice_in_dim(q_pe, q0, Q_BLOCK, 1)
        s = jnp.einsum('bqhd,bkhd->bhqk', qn, k_nope) + jnp.einsum('bqhd,bkd->bhqk', qp, k_pe)
        q_pos = q0 + jnp.arange(Q_BLOCK)
        p = masked_softmax(s.astype(jnp.float32) * scale, k_pos[None, :] <= q_pos[:, None])
        return jnp.einsum('bhqk,bkhd->bqhd', p.astype(v.dtype), v)

    return unblock(lax.map(block, jnp.arange(S // Q_BLOCK))).reshape(B, S, D_GROUP)

def nsa_mixer(q, k_cmp, v_cmp, k_slc, v_slc, k_win, v_win, gate_logits,
              cmp_pos, wk1, wk2, wv1, wv2, cos_h, sin_h):
    B, S, _ = q.shape
    q = apply_rope(q.reshape(B, S, HEADS, HEAD_DIM), cos_h, sin_h)
    k_cmp = apply_rope(k_cmp, cos_h, sin_h)
    k_slc = apply_rope(k_slc, cos_h, sin_h)
    k_win = apply_rope(k_win, cos_h, sin_h)
    scale = HEAD_DIM ** -0.5
    t_pos = jnp.arange(S)

    n_cmp = (S - NSA_CMP_LEN) // NSA_CMP_STRIDE + 1
    tok = np.arange(n_cmp)[:, None] * NSA_CMP_STRIDE + np.arange(NSA_CMP_LEN)[None, :]

    def compress(z, w1, w2):
        blk = (z[:, tok] + cmp_pos).reshape(B, n_cmp, NSA_CMP_LEN * HEAD_DIM)
        return jax.nn.gelu(blk @ w1) @ w2

    kc = compress(k_cmp, wk1, wk2)
    vc = compress(v_cmp, wv1, wv2)
    s_c = jnp.einsum('bshd,bnd->bhsn', q, kc).astype(jnp.float32) * scale
    p_c = masked_softmax(s_c, tok[:, -1][None, :] <= t_pos[:, None])
    o_cmp = jnp.einsum('bhsn,bnd->bshd', p_c.astype(vc.dtype), vc)

    n_slc = S // NSA_SEL_LEN
    slc_start = np.arange(n_slc) * NSA_SEL_LEN
    overlap = ((tok[:, :1] <= slc_start[None, :] + NSA_SEL_LEN - 1)
               & (tok[:, -1:] >= slc_start[None, :])).astype(np.float32)
    imp = jnp.einsum('bhsn,nj->bsj', p_c, jnp.asarray(overlap))
    cur = (t_pos // NSA_SEL_LEN)[:, None]
    jb = jnp.arange(n_slc)[None, :]
    forced = (jb < NSA_N_INIT) | ((jb <= cur) & (jb > cur - NSA_N_LOCAL))
    imp = jnp.where(forced, FORCE_SCORE, jnp.where(jb <= cur, imp, NEG_INF))
    n_top = min(NSA_N_SEL, n_slc)
    _, sel = lax.top_k(imp, n_top)
    k_blk = k_slc.reshape(B, n_slc, NSA_SEL_LEN, HEAD_DIM)
    v_blk = v_slc.reshape(B, n_slc, NSA_SEL_LEN, HEAD_DIM)
    kw = jnp.pad(k_win, ((0, 0), (NSA_WINDOW, 0), (0, 0)))
    vw = jnp.pad(v_win, ((0, 0), (NSA_WINDOW, 0), (0, 0)))
    b_idx = jnp.arange(B)[:, None, None]
    n_sel_tok = n_top * NSA_SEL_LEN

    def block(i):
        q0 = i * Q_BLOCK
        qb = lax.dynamic_slice_in_dim(q, q0, Q_BLOCK, 1)
        q_pos = q0 + jnp.arange(Q_BLOCK)
        idx = lax.dynamic_slice_in_dim(sel, q0, Q_BLOCK, 1)
        kg = k_blk[b_idx, idx].reshape(B, Q_BLOCK, n_sel_tok, HEAD_DIM)
        vg = v_blk[b_idx, idx].reshape(B, Q_BLOCK, n_sel_tok, HEAD_DIM)
        g_pos = (idx[..., None] * NSA_SEL_LEN + jnp.arange(NSA_SEL_LEN)).reshape(B, Q_BLOCK, n_sel_tok)
        s = jnp.einsum('bqhd,bqkd->bhqk', qb, kg).astype(jnp.float32) * scale
        p = masked_softmax(s, (g_pos <= q_pos[None, :, None])[:, None])
        o_s = jnp.einsum('bhqk,bqkd->bqhd', p.astype(vg.dtype), vg)
        kb = lax.dynamic_slice_in_dim(kw, q0, NSA_WINDOW + Q_BLOCK, 1)
        vb = lax.dynamic_slice_in_dim(vw, q0, NSA_WINDOW + Q_BLOCK, 1)
        w_pos = q0 - NSA_WINDOW + jnp.arange(NSA_WINDOW + Q_BLOCK)
        dist = q_pos[:, None] - w_pos[None, :]
        s = jnp.einsum('bqhd,bkd->bhqk', qb, kb).astype(jnp.float32) * scale
        p = masked_softmax(s, (dist >= 0) & (dist < NSA_WINDOW) & (w_pos[None, :] >= 0))
        o_w = jnp.einsum('bhqk,bkd->bqhd', p.astype(vb.dtype), vb)
        return o_s, o_w

    o_slc, o_win = lax.map(block, jnp.arange(S // Q_BLOCK))
    o_slc = unblock(o_slc)
    o_win = unblock(o_win)
    g = jax.nn.sigmoid(gate_logits).reshape(B, S, 3, HEADS)[..., None]
    o = g[:, :, 0] * o_cmp + g[:, :, 1] * o_slc + g[:, :, 2] * o_win
    return o.reshape(B, S, D_GROUP)

def dsa_mixer(q, k, v, q_idx, k_idx, w_idx, cos_h, sin_h, cos_i, sin_i):
    B, S, _ = q.shape
    q = apply_rope(q.reshape(B, S, HEADS, HEAD_DIM), cos_h, sin_h)
    k = apply_rope(k, cos_h, sin_h)
    q_idx = apply_rope(q_idx.reshape(B, S, DSA_IDX_HEADS, DSA_IDX_DIM), cos_i, sin_i)
    k_idx = apply_rope(k_idx, cos_i, sin_i)
    w_idx = w_idx.astype(jnp.float32) * (DSA_IDX_HEADS * DSA_IDX_DIM) ** -0.5
    scale = HEAD_DIM ** -0.5
    n_top = min(DSA_TOPK, S // 4)
    k_pos = jnp.arange(S)
    b_idx = jnp.arange(B)[:, None, None]

    def block(i):
        q0 = i * Q_BLOCK
        q_pos = q0 + jnp.arange(Q_BLOCK)
        qi = lax.dynamic_slice_in_dim(q_idx, q0, Q_BLOCK, 1)
        wi = lax.dynamic_slice_in_dim(w_idx, q0, Q_BLOCK, 1)
        rel = jax.nn.relu(jnp.einsum('bqhd,bsd->bqhs', qi, k_idx).astype(jnp.float32))
        score = jnp.einsum('bqh,bqhs->bqs', wi, rel)
        score = jnp.where(k_pos[None, None, :] <= q_pos[None, :, None], score, NEG_INF)
        _, idx = lax.top_k(score, n_top)
        kg = k[b_idx, idx]
        vg = v[b_idx, idx]
        qb = lax.dynamic_slice_in_dim(q, q0, Q_BLOCK, 1)
        s = jnp.einsum('bqhd,bqkd->bhqk', qb, kg).astype(jnp.float32) * scale
        p = masked_softmax(s, (idx <= q_pos[None, :, None])[:, None])
        return jnp.einsum('bhqk,bqkd->bqhd', p.astype(vg.dtype), vg)

    return unblock(lax.map(block, jnp.arange(S // Q_BLOCK))).reshape(B, S, D_GROUP)

def stick_breaking_mixer(q, k, v):
    B, S, _ = q.shape
    q = q.reshape(B, S, HEADS, HEAD_DIM)
    k = k.reshape(B, S, HEADS, HEAD_DIM)
    v = v.reshape(B, S, HEADS, HEAD_DIM)
    scale = HEAD_DIM ** -0.5
    k_pos = jnp.arange(S)

    def block(i):
        q0 = i * Q_BLOCK
        qb = lax.dynamic_slice_in_dim(q, q0, Q_BLOCK, 1)
        q_pos = q0 + jnp.arange(Q_BLOCK)
        z = jnp.einsum('bqhd,bkhd->bhqk', qb, k).astype(jnp.float32) * scale
        mask = k_pos[None, :] < q_pos[:, None]
        log_1m = jnp.where(mask, jax.nn.log_sigmoid(-z), 0.0)
        after = lax.cumsum(log_1m, axis=3, reverse=True) - log_1m
        a = jnp.where(mask, jnp.exp(jax.nn.log_sigmoid(z) + after), 0.0)
        return jnp.einsum('bhqk,bkhd->bqhd', a.astype(v.dtype), v)

    return unblock(lax.map(block, jnp.arange(S // Q_BLOCK))).reshape(B, S, D_GROUP)

def hybrid_mixer(x, w_in, mla_q_norm, mla_w_uq, mla_kv_norm, mla_w_ukv, nsa_cmp_pos,
                 nsa_cmp_wk1, nsa_cmp_wk2, nsa_cmp_wv1, nsa_cmp_wv2, group_norm_g, w_out,
                 cos_h, sin_h, cos_r, sin_r, cos_i, sin_i):
    B, S, _ = x.shape
    h = split_columns(x @ w_in)
    y_a = mla_mixer(h['mla_cq'], h['mla_ckv'], h['mla_krope'], mla_q_norm, mla_w_uq,
                    mla_kv_norm, mla_w_ukv, cos_r, sin_r)
    y_b = nsa_mixer(h['nsa_q'], h['nsa_k_cmp'], h['nsa_v_cmp'], h['nsa_k_slc'], h['nsa_v_slc'],
                    h['nsa_k_win'], h['nsa_v_win'], h['nsa_gate'], nsa_cmp_pos,
                    nsa_cmp_wk1, nsa_cmp_wk2, nsa_cmp_wv1, nsa_cmp_wv2, cos_h, sin_h)
    y_c = dsa_mixer(h['dsa_q'], h['dsa_k'], h['dsa_v'], h['idx_q'], h['idx_k'], h['idx_w'],
                    cos_h, sin_h, cos_i, sin_i)
    y_d = stick_breaking_mixer(h['sb_q'], h['sb_k'], h['sb_v'])
    y = jnp.concatenate([y_a, y_b, y_c, y_d], axis=-1).reshape(B, S, N_GROUPS, D_GROUP)
    y = rms_norm(y, group_norm_g.reshape(N_GROUPS, D_GROUP)).reshape(B, S, D_MIX)
    return y @ w_out

def first_inputs(seed: int = 0) -> dict:
    key = jax.random.key(seed)
    keys = jax.random.split(key, 32)
    counter = [0]

    def nrm(shape, scale):
        k = keys[counter[0]]
        counter[0] += 1
        return jax.random.normal(k, shape, jnp.float32) * scale

    def gain(shape):
        return 1.0 + nrm(shape, 0.02)

    L, D = DEPTH, D_MODEL
    return {
        'x': nrm((BATCH, SEQ, D), 1.0),
        'ln1_g': gain((L, D)),
        'ln1_b': nrm((L, D), 0.02),
        'ffn1_w1': nrm((L, D, D_FF), D ** -0.5),
        'ffn1_w3': nrm((L, D, D_FF), D ** -0.5),
        'ffn1_w2': nrm((L, D_FF, D), DN_BETA * D_FF ** -0.5),
        'w_in': nrm((L, D, D_IN), D ** -0.5),
        'mla_q_norm': gain((L, MLA_Q_RANK)),
        'mla_w_uq': nrm((L, MLA_Q_RANK, HEADS * (MLA_D_NOPE + MLA_D_ROPE)), MLA_Q_RANK ** -0.5),
        'mla_kv_norm': gain((L, MLA_KV_RANK)),
        'mla_w_ukv': nrm((L, MLA_KV_RANK, HEADS * (MLA_D_NOPE + MLA_D_V)), MLA_KV_RANK ** -0.5),
        'nsa_cmp_pos': nrm((L, NSA_CMP_LEN, HEAD_DIM), 0.1),
        'nsa_cmp_wk1': nrm((L, NSA_CMP_LEN * HEAD_DIM, HEAD_DIM), (NSA_CMP_LEN * HEAD_DIM) ** -0.5),
        'nsa_cmp_wk2': nrm((L, HEAD_DIM, HEAD_DIM), HEAD_DIM ** -0.5),
        'nsa_cmp_wv1': nrm((L, NSA_CMP_LEN * HEAD_DIM, HEAD_DIM), (NSA_CMP_LEN * HEAD_DIM) ** -0.5),
        'nsa_cmp_wv2': nrm((L, HEAD_DIM, HEAD_DIM), HEAD_DIM ** -0.5),
        'group_norm_g': gain((L, D_MIX)),
        'w_out': nrm((L, D_MIX, D), DN_BETA * D_MIX ** -0.5),
        'ln2_g': gain((L, D)),
        'ln2_b': nrm((L, D), 0.02),
        'ffn2_w1': nrm((L, D, D_FF), D ** -0.5),
        'ffn2_w3': nrm((L, D, D_FF), D ** -0.5),
        'ffn2_w2': nrm((L, D_FF, D), DN_BETA * D_FF ** -0.5),
        'ln3_g': gain((L, D)),
        'ln3_b': nrm((L, D), 0.02),
    }

def first_block(x, ln1_g, ln1_b, ffn1_w1, ffn1_w3, ffn1_w2, w_in, mla_q_norm, mla_w_uq,
              mla_kv_norm, mla_w_ukv, nsa_cmp_pos, nsa_cmp_wk1, nsa_cmp_wk2, nsa_cmp_wv1,
              nsa_cmp_wv2, group_norm_g, w_out, ln2_g, ln2_b, ffn2_w1, ffn2_w3, ffn2_w2,
              ln3_g, ln3_b):
    S = x.shape[1]
    cos_h, sin_h = rope_tables(S, HEAD_DIM)
    cos_r, sin_r = rope_tables(S, MLA_D_ROPE)
    cos_i, sin_i = rope_tables(S, DSA_IDX_DIM)
    for l in range(DEPTH):
        x = layer_norm(DN_ALPHA * x + 0.5 * swiglu(x, ffn1_w1[l], ffn1_w3[l], ffn1_w2[l]),
                       ln1_g[l], ln1_b[l])
        y = hybrid_mixer(x, w_in[l], mla_q_norm[l], mla_w_uq[l], mla_kv_norm[l], mla_w_ukv[l],
                         nsa_cmp_pos[l], nsa_cmp_wk1[l], nsa_cmp_wk2[l], nsa_cmp_wv1[l],
                         nsa_cmp_wv2[l], group_norm_g[l], w_out[l],
                         cos_h, sin_h, cos_r, sin_r, cos_i, sin_i)
        x = layer_norm(DN_ALPHA * x + y, ln2_g[l], ln2_b[l])
        x = layer_norm(DN_ALPHA * x + 0.5 * swiglu(x, ffn2_w1[l], ffn2_w3[l], ffn2_w2[l]),
                       ln3_g[l], ln3_b[l])
    return x


DEPTH_2 = 1

SSM_EXPAND = 2
SSM_D_INNER = SSM_EXPAND * D_MODEL
SSM_HEAD_DIM = 64
SSM_HEADS = SSM_D_INNER // SSM_HEAD_DIM
SSM_GROUPS = 4
SSM_HEADS_PER_GROUP = SSM_HEADS // SSM_GROUPS
SSM_D_STATE = 128
SSM_CONV = 4
SSM_CHUNK = 128
SSM_BC_DIM = SSM_GROUPS * SSM_D_STATE
SSM_CONV_DIM = SSM_D_INNER + 2 * SSM_BC_DIM
SSM_NORM_GROUP = SSM_D_INNER // SSM_GROUPS
SSM_DT_MIN = 0.001
SSM_DT_MAX = 0.1

LRU_WIDTH = 1280
LRU_BLOCKS = 10
LRU_BLOCK = LRU_WIDTH // LRU_BLOCKS
LRU_CONV = 4
LRU_C = 8.0

FFN_HIDDEN = -(-8 * D_MODEL // (3 * 256)) * 256


N_GATES = 2 * D_MODEL
IN_PROJ_DIM = N_GATES + SSM_D_INNER + SSM_CONV_DIM + SSM_HEADS + 2 * LRU_WIDTH
IN_SPLITS_2 = (
    N_GATES,
    N_GATES + SSM_D_INNER,
    N_GATES + SSM_D_INNER + SSM_CONV_DIM,
    N_GATES + SSM_D_INNER + SSM_CONV_DIM + SSM_HEADS,
    N_GATES + SSM_D_INNER + SSM_CONV_DIM + SSM_HEADS + LRU_WIDTH,
)


def rmsnorm(x, w, eps=RMS_EPS):
    xf = x.astype(jnp.float32)
    y = xf * lax.rsqrt(jnp.mean(xf * xf, axis=-1, keepdims=True) + eps)
    return (y * w.astype(jnp.float32)).astype(x.dtype)

def causal_dwconv(u, w, b):
    k_width = w.shape[0]
    length = u.shape[1]
    up = jnp.pad(u, ((0, 0), (k_width - 1, 0), (0, 0)))
    out = b + up[:, 0:length] * w[0]
    for k in range(1, k_width):
        out = out + up[:, k:k + length] * w[k]
    return out

def segsum_exp(cs):
    t = cs.shape[-1]
    mask = jnp.tril(jnp.ones((t, t), dtype=bool))
    diff = cs[..., :, None] - cs[..., None, :]
    return jnp.exp(jnp.where(mask, diff, -jnp.inf))

def ssd_chunked(xdt, dA, bm, cm):
    b, length, g, r, p = xdt.shape
    n = bm.shape[-1]
    l = SSM_CHUNK
    c = length // l
    xdt = xdt.reshape(b, c, l, g, r, p)
    dA = dA.reshape(b, c, l, g, r)
    bm = bm.reshape(b, c, l, g, n)
    cm = cm.reshape(b, c, l, g, n)

    cs = jnp.cumsum(dA, axis=2)
    lmat = segsum_exp(jnp.moveaxis(cs, 2, -1))
    cb = jnp.einsum('bclgn,bcsgn->bcgls', cm, bm)
    y_diag = jnp.einsum('bcgls,bcgrls,bcsgrp->bclgrp', cb, lmat, xdt)
    decay_states = jnp.exp(cs[:, :, -1:] - cs)
    states = jnp.einsum('bclgn,bclgr,bclgrp->bcgrpn', bm, decay_states, xdt)
    chunk_tot = jnp.moveaxis(cs[:, :, -1], 1, -1)
    chunk_cs = jnp.cumsum(jnp.pad(chunk_tot, ((0, 0), (0, 0), (0, 0), (1, 0))), axis=-1)
    decay_chunk = segsum_exp(chunk_cs)
    states = jnp.concatenate([jnp.zeros_like(states[:, :1]), states], axis=1)
    states_in = jnp.einsum('bgrzc,bcgrpn->bzgrpn', decay_chunk[..., :-1, :], states)
    y_off = jnp.einsum('bclgn,bcgrpn,bclgr->bclgrp', cm, states_in, jnp.exp(cs))
    return (y_diag + y_off).reshape(b, length, g, r, p)

def mamba2_mixer(z, xbc, dt_raw, conv_w, conv_b, dt_bias, a_log, d_skip, norm_w):
    b, length, _ = z.shape
    f32 = jnp.float32
    xbc = jax.nn.silu(causal_dwconv(xbc, conv_w, conv_b))
    xs, bm, cm = jnp.split(xbc, [SSM_D_INNER, SSM_D_INNER + SSM_BC_DIM], axis=-1)
    dt = jax.nn.softplus(dt_raw.astype(f32) + dt_bias.astype(f32))
    a = -jnp.exp(a_log.astype(f32))
    g, r, p, n = SSM_GROUPS, SSM_HEADS_PER_GROUP, SSM_HEAD_DIM, SSM_D_STATE
    xs_h = xs.astype(f32).reshape(b, length, g, r, p)
    dt_h = dt.reshape(b, length, g, r)
    y = ssd_chunked(xs_h * dt_h[..., None], dt_h * a.reshape(g, r),
                    bm.astype(f32).reshape(b, length, g, n),
                    cm.astype(f32).reshape(b, length, g, n))
    y = y + xs_h * d_skip.astype(f32).reshape(g, r, 1)
    y = y.reshape(b, length, SSM_D_INNER) * jax.nn.silu(z.astype(f32))
    yg = y.reshape(b, length, SSM_GROUPS, SSM_NORM_GROUP)
    yg = yg * lax.rsqrt(jnp.mean(yg * yg, axis=-1, keepdims=True) + RMS_EPS)
    y = yg.reshape(b, length, SSM_D_INNER) * norm_w.astype(f32)
    return y.astype(z.dtype)

def rglru_mixer(xl, yl, conv_w, conv_b, w_r, b_r, w_i, b_i, lam):
    b, length, _ = xl.shape
    f32 = jnp.float32
    u = causal_dwconv(xl, conv_w, conv_b)
    ub = u.reshape(b, length, LRU_BLOCKS, LRU_BLOCK)
    r_gate = jax.nn.sigmoid((jnp.einsum('blhi,hij->blhj', ub, w_r).reshape(b, length, LRU_WIDTH) + b_r).astype(f32))
    i_gate = jax.nn.sigmoid((jnp.einsum('blhi,hij->blhj', ub, w_i).reshape(b, length, LRU_WIDTH) + b_i).astype(f32))
    log_a = -LRU_C * r_gate * jax.nn.softplus(-lam.astype(f32))
    a_t = jnp.exp(log_a)
    b_t = jnp.sqrt(-jnp.expm1(2.0 * log_a)) * (i_gate * u.astype(f32))

    def combine(left, right):
        a1, b1 = left
        a2, b2 = right
        return a1 * a2, a2 * b1 + b2

    _, h = lax.associative_scan(combine, (a_t, b_t), axis=1)
    out = h * jax.nn.gelu(yl.astype(f32), approximate=True)
    return out.astype(xl.dtype)

def second_inputs(seed: int = 0) -> dict:
    key = jax.random.key(seed)
    ks = jax.random.split(key, 32)
    f32 = jnp.float32
    nrm = lambda k, shape, scale: jax.random.normal(k, shape, f32) * scale
    L = DEPTH_2

    x = jax.random.normal(ks[0], (BATCH, SEQ, D_MODEL), f32)
    norm1_w = 1.0 + nrm(ks[1], (L, D_MODEL), 0.05)
    w_in = nrm(ks[2], (L, D_MODEL, IN_PROJ_DIM), D_MODEL ** -0.5)
    b_branch_gate = nrm(ks[3], (L, N_GATES), 0.1)

    ssm_conv_w = nrm(ks[4], (L, SSM_CONV, SSM_CONV_DIM), SSM_CONV ** -0.5)
    ssm_conv_b = nrm(ks[5], (L, SSM_CONV_DIM), 0.02)
    u = jax.random.uniform(ks[6], (L, SSM_HEADS), f32)
    dt0 = jnp.exp(u * (math.log(SSM_DT_MAX) - math.log(SSM_DT_MIN)) + math.log(SSM_DT_MIN))
    dt0 = jnp.maximum(dt0, 1e-4)
    ssm_dt_bias = dt0 + jnp.log(-jnp.expm1(-dt0))
    ssm_a_log = jnp.log(jax.random.uniform(ks[7], (L, SSM_HEADS), f32, 1.0, 16.0))
    ssm_d = 1.0 + nrm(ks[8], (L, SSM_HEADS), 0.1)
    ssm_norm_w = 1.0 + nrm(ks[9], (L, SSM_D_INNER), 0.05)
    w_out_ssm = nrm(ks[10], (L, SSM_D_INNER, D_MODEL), SSM_D_INNER ** -0.5)

    lru_conv_w = nrm(ks[11], (L, LRU_CONV, LRU_WIDTH), LRU_CONV ** -0.5)
    lru_conv_b = nrm(ks[12], (L, LRU_WIDTH), 0.02)
    lru_w_r = nrm(ks[13], (L, LRU_BLOCKS, LRU_BLOCK, LRU_BLOCK), LRU_BLOCK ** -0.5)
    lru_b_r = nrm(ks[14], (L, LRU_WIDTH), 0.02)
    lru_w_i = nrm(ks[15], (L, LRU_BLOCKS, LRU_BLOCK, LRU_BLOCK), LRU_BLOCK ** -0.5)
    lru_b_i = nrm(ks[16], (L, LRU_WIDTH), 0.02)
    a0 = jax.random.uniform(ks[17], (L, LRU_WIDTH), f32, 0.9, 0.999)
    s0 = a0 ** (1.0 / LRU_C)
    lru_lambda = jnp.log(s0) - jnp.log1p(-s0)
    w_out_lru = nrm(ks[18], (L, LRU_WIDTH, D_MODEL), LRU_WIDTH ** -0.5)

    w_out = nrm(ks[19], (L, D_MODEL, D_MODEL), D_MODEL ** -0.5)
    norm2_w = 1.0 + nrm(ks[20], (L, D_MODEL), 0.05)
    w_ffn_in = nrm(ks[21], (L, D_MODEL, 2 * FFN_HIDDEN), D_MODEL ** -0.5)
    w_ffn_out = nrm(ks[22], (L, FFN_HIDDEN, D_MODEL), FFN_HIDDEN ** -0.5)
    norm_f_w = 1.0 + nrm(ks[23], (D_MODEL,), 0.05)

    return {
        "x": x, "norm1_w": norm1_w, "w_in": w_in, "b_branch_gate": b_branch_gate,
        "ssm_conv_w": ssm_conv_w, "ssm_conv_b": ssm_conv_b, "ssm_dt_bias": ssm_dt_bias,
        "ssm_a_log": ssm_a_log, "ssm_d": ssm_d, "ssm_norm_w": ssm_norm_w, "w_out_ssm": w_out_ssm,
        "lru_conv_w": lru_conv_w, "lru_conv_b": lru_conv_b, "lru_w_r": lru_w_r, "lru_b_r": lru_b_r,
        "lru_w_i": lru_w_i, "lru_b_i": lru_b_i, "lru_lambda": lru_lambda, "w_out_lru": w_out_lru,
        "w_out": w_out, "norm2_w": norm2_w, "w_ffn_in": w_ffn_in, "w_ffn_out": w_ffn_out,
        "norm_f_w": norm_f_w,
    }

def second_block(x, norm1_w, w_in, b_branch_gate, ssm_conv_w, ssm_conv_b, ssm_dt_bias, ssm_a_log,
              ssm_d, ssm_norm_w, w_out_ssm, lru_conv_w, lru_conv_b, lru_w_r, lru_b_r, lru_w_i,
              lru_b_i, lru_lambda, w_out_lru, w_out, norm2_w, w_ffn_in, w_ffn_out, norm_f_w):
    h = x
    for l in range(DEPTH_2):
        hn = rmsnorm(h, norm1_w[l])
        proj = hn @ w_in[l]
        gates, z, xbc, dt_raw, lru_x, lru_y = jnp.split(proj, IN_SPLITS_2, axis=-1)
        gates = jax.nn.sigmoid(gates + b_branch_gate[l])
        g_ssm, g_lru = jnp.split(gates, 2, axis=-1)
        y_ssm = mamba2_mixer(z, xbc, dt_raw, ssm_conv_w[l], ssm_conv_b[l], ssm_dt_bias[l],
                             ssm_a_log[l], ssm_d[l], ssm_norm_w[l]) @ w_out_ssm[l]
        y_lru = rglru_mixer(lru_x, lru_y, lru_conv_w[l], lru_conv_b[l], lru_w_r[l], lru_b_r[l],
                            lru_w_i[l], lru_b_i[l], lru_lambda[l]) @ w_out_lru[l]
        h = h + (g_ssm * y_ssm + g_lru * y_lru) @ w_out[l]
        hn = rmsnorm(h, norm2_w[l])
        gate, up = jnp.split(hn @ w_ffn_in[l], 2, axis=-1)
        h = h + (jax.nn.silu(gate) * up) @ w_ffn_out[l]
    return rmsnorm(h, norm_f_w)


def setup_inputs(seed=0):
    out = dict(first_inputs(seed))
    for name, value in second_inputs(seed + 1).items():
        if name != "x":
            out[name + "_2"] = value
    return out


def reference(
    x, ln1_g, ln1_b, ffn1_w1, ffn1_w3, ffn1_w2, w_in, mla_q_norm, mla_w_uq, mla_kv_norm,
    mla_w_ukv, nsa_cmp_pos, nsa_cmp_wk1, nsa_cmp_wk2, nsa_cmp_wv1, nsa_cmp_wv2, group_norm_g,
    w_out, ln2_g, ln2_b, ffn2_w1, ffn2_w3, ffn2_w2, ln3_g, ln3_b, norm1_w_2, w_in_2,
    b_branch_gate_2, ssm_conv_w_2, ssm_conv_b_2, ssm_dt_bias_2, ssm_a_log_2, ssm_d_2,
    ssm_norm_w_2, w_out_ssm_2, lru_conv_w_2, lru_conv_b_2, lru_w_r_2, lru_b_r_2, lru_w_i_2,
    lru_b_i_2, lru_lambda_2, w_out_lru_2, w_out_2, norm2_w_2, w_ffn_in_2, w_ffn_out_2,
    norm_f_w_2,
):
    x = first_block(
        x, ln1_g, ln1_b, ffn1_w1, ffn1_w3, ffn1_w2, w_in, mla_q_norm, mla_w_uq, mla_kv_norm,
        mla_w_ukv, nsa_cmp_pos, nsa_cmp_wk1, nsa_cmp_wk2, nsa_cmp_wv1, nsa_cmp_wv2,
        group_norm_g, w_out, ln2_g, ln2_b, ffn2_w1, ffn2_w3, ffn2_w2, ln3_g, ln3_b,
    )
    return second_block(
        x, norm1_w_2, w_in_2, b_branch_gate_2, ssm_conv_w_2, ssm_conv_b_2, ssm_dt_bias_2,
        ssm_a_log_2, ssm_d_2, ssm_norm_w_2, w_out_ssm_2, lru_conv_w_2, lru_conv_b_2, lru_w_r_2,
        lru_b_r_2, lru_w_i_2, lru_b_i_2, lru_lambda_2, w_out_lru_2, w_out_2, norm2_w_2,
        w_ffn_in_2, w_ffn_out_2, norm_f_w_2,
    )


_drawn_inputs = setup_inputs


def setup_inputs(seed=0):
    import zlib

    import numpy as np

    out = dict(_drawn_inputs(seed))
    spreads = {}
    factors = {'mla_q_norm': 6.572,
     'mla_kv_norm': 4.177,
     'group_norm_g': 2.876,
     'ssm_conv_b_2': 4.273,
     'lru_b_r_2': 29.215,
     'lru_b_i_2': 8.0,
     'ssm_norm_w_2': 2.695,
     'lru_conv_b_2': 3.137}
    for name, (base, spread) in spreads.items():
        noise = np.random.default_rng([zlib.crc32(name.encode()), seed]).standard_normal(out[name].shape)
        drawn = base * np.exp(spread * noise) if base else spread * noise
        out[name] = jnp.asarray(drawn.astype(out[name].dtype))
    for name, factor in factors.items():
        out[name] = (out[name] * factor).astype(out[name].dtype)
    return out
```

```python
from contextlib import ExitStack

import numpy as np

import concourse.bass as bass
from concourse import mybir

F32 = mybir.dt.float32
F32R = mybir.dt.float32r
BF16 = mybir.dt.bfloat16
ALU = mybir.AluOpType
ACT = mybir.ActivationFunctionType
AXX = mybir.AxisListType.X

P = 128
SEQ = 512
D = 1024
DT = D // P
FF = 2816
FT = FF // P
DEPTH = 2
ALPHA = (2.0 * DEPTH) ** 0.25
LN_EPS = 1e-5
RMS_EPS = 1e-6
NEG = -1e30
TAKEN = -3e38
HD = 64
HEADS = 4
QB = SEQ // P
TOPK = min(256, SEQ // 4)
NCMP = (SEQ - 32) // 16 + 1
IDXH = 8

RAW = 4
HALF = 2
SLOT = 11 * P

CQ, CKV, KROPE, NSAQ, KCMP, VCMP, KSLC, KWIN, DSAQ, DSAK, IDXQ, IDXK, SBQ, SBK = 0, 2, 3, 4, 6, 7, 8, 9, 10, 12, 13, 15, 16, 18
HT = 20
VSLC, VWIN, GATE, DSAV, IDXW, SBV = 0, 64, 128, 140, 204, 212
TW = 468

KB = 1024
A_X, A_XH, A_XL, A_RAW, A_WHI, A_WLO = 0, 16 * KB, 32 * KB, 48 * KB, 48 * KB + RAW * SLOT * 4, 48 * KB + (RAW + HALF) * SLOT * 4
A_CONST = A_RAW + (RAW + 2 * HALF) * SLOT * 4
CONST_NAMES = ["ident", "negd", "negs", "cmpm", "negl", "strict", "ntri", "nones", "ones", "sw64", "sw32", "triu"]
N_BF16 = 5
NCONST = len(CONST_NAMES) * P + 4 * SEQ + 8
A_PAR = A_CONST + NCONST * 4
PG1, PB1, PG2, PB2, PG3, PB3, PQN, PKVN, PGN, PPOS = 0, 8, 16, 24, 32, 40, 48, 50, 51, 59
NPAR = 75
RN1, RN2, RNF, RBG, RLAM, RDTB, RALOG = 0, 8, 16, 24, 40, 50, 51
NPAR2 = 52
GCW, GCB, GD, GN = 0, 24, 30, 34
NPG = 40
A_KB = A_PAR + 128 * 4
A_WORK = A_KB + N_BF16 * P * 2


def tiles_of(w):
    k, m = w.shape
    return w.reshape(k // P, P, m).transpose(1, 0, 2).reshape(P, -1)


def columns_of(v):
    return v.reshape(-1, P).T


def constants():
    i = np.arange(P)
    k, q = i[:, None], i[None, :]
    c = {}
    c["ident"] = (k == q) * 1.0
    c["negd"] = (q > k) * NEG
    c["strict"] = (k < q) * 1.0
    c["negs"] = (k >= q) * NEG
    c["ntri"] = (k >= q) * -1.0
    c["nones"] = -np.ones((P, P))
    c["ones"] = np.ones((P, P))
    c["sw64"] = ((k // 64 == q // 64) & ((k % 64 + 32) % 64 == q % 64)) * 1.0
    c["sw32"] = ((k // 32 == q // 32) & ((k % 32 + 16) % 32 == q % 32)) * 1.0
    n = np.arange(NCMP)
    m = np.zeros((P, P))
    for b in range(QB):
        m[:, b * NCMP:(b + 1) * NCMP] = (n[None, :] * 16 + 31 > (i + b * P)[:, None]) * NEG
    c["cmpm"] = m
    c["triu"] = (k <= q) * 1.0
    c["negl"] = (k > q) * NEG
    cols = [c[x].astype(np.float32) for x in CONST_NAMES]
    for dim in (64, 32):
        half = dim // 2
        inv = (np.float32(10000.0) ** (-np.arange(0, dim, 2, dtype=np.float32) / np.float32(dim))).astype(np.float32)
        ang = np.arange(SEQ, dtype=np.float32)[:, None] * inv[None, :]
        cos, sin = np.cos(ang).astype(np.float32).T, np.sin(ang).astype(np.float32).T
        reps = P // dim
        cols.append(np.tile(np.concatenate([cos, cos]), (reps, 1)))
        cols.append(np.tile(np.concatenate([-sin, sin]), (reps, 1)))
    eps = np.zeros((P, 8), np.float32)
    eps[:, 0], eps[:, 1] = LN_EPS, RMS_EPS
    cols.append(eps)
    return np.ascontiguousarray(np.concatenate(cols, axis=1))


def mixer_columns():
    widths = [256, 128, 32, 256, 64, 64, 64, 64, 64, 64, 12, 256, 64, 64, 256, 32, 8, 256, 256, 256]
    names = "cq ckv krope nq kc vc ks vs kw vw gate dq dk dv iq ik iw sq sk sv".split()
    at, off = {}, 0
    for n, w in zip(names, widths):
        at[n] = np.arange(off, off + w)
        off += w
    feat = [at["cq"], at["ckv"], *[at["krope"]] * 4, at["nq"]]
    for n in ("kc", "vc", "ks", "kw"):
        feat += [at[n]] * 2
    feat += [at["dq"], at["dk"], at["dk"], at["iq"], *[at["ik"]] * 4, at["sq"], at["sk"]]
    tok = [at[n] for n in ("vs", "vw", "gate", "dv", "iw", "sv")]
    return np.concatenate(feat), np.concatenate(tok)


def layout(a):
    a = {k: np.asarray(v) for k, v in a.items()}
    out = {"xT": np.ascontiguousarray(a["x"][0].T.reshape(DT, P, SEQ).transpose(1, 0, 2).reshape(P, -1))}
    out["consts"] = constants()
    ups, downs = [], []

    def ffn(w1, w3, w2):
        up = []
        for t in range(FT):
            up += [tiles_of(w1[:, t * P:(t + 1) * P]), tiles_of(w3[:, t * P:(t + 1) * P])]
        ups.append(np.stack(up))
        down = []
        for d in range(DT):
            w = w2[:, d * P:(d + 1) * P]
            down += [tiles_of(w[:11 * P]), tiles_of(w[11 * P:])]
        downs.append(np.stack(down))

    for l in range(DEPTH):
        ffn(a["ffn1_w1"][l], a["ffn1_w3"][l], a["ffn1_w2"][l])
        ffn(a["ffn2_w1"][l], a["ffn2_w3"][l], a["ffn2_w2"][l])
    wf = a["w_ffn_in_2"][0]
    ffn(wf[:, :FF], wf[:, FF:], a["w_ffn_out_2"][0])
    out["ffn_up"], out["ffn_down"] = np.stack(ups), np.stack(downs)

    def outs(w):
        return [tiles_of(w[:, d * P:(d + 1) * P]) for d in range(w.shape[1] // P)]

    feat, tok = mixer_columns()
    out["mix_in"] = np.stack([np.stack(outs(a["w_in"][l][:, feat])) for l in range(DEPTH)])
    out["mix_tok"] = np.stack([tiles_of(a["w_in"][l][:, tok]) for l in range(DEPTH)])
    out["mix_out"] = np.stack([np.stack(outs(a["w_out"][l])) for l in range(DEPTH)])
    out["mla_uq"] = np.stack([tiles_of(a["mla_w_uq"][l]) for l in range(DEPTH)])
    ukv = a["mla_w_ukv"].reshape(DEPTH, P, HEADS, 2, 64).transpose(0, 1, 3, 2, 4)
    out["mla_ukv"] = np.ascontiguousarray(ukv.reshape(DEPTH, P, 512))

    def cmp1(w):
        return w.reshape(2, 16, 64, 64).transpose(0, 2, 1, 3).reshape(P, 1024)

    out["cmp1"] = np.stack([np.concatenate([cmp1(a["nsa_cmp_wk1"][l]), cmp1(a["nsa_cmp_wv1"][l])], 1) for l in range(DEPTH)])
    out["cmp2"] = np.concatenate([a["nsa_cmp_wk2"], a["nsa_cmp_wk2"], a["nsa_cmp_wv2"]], 2)
    pars = []
    for l in range(DEPTH):
        c = [columns_of(a[n][l]) for n in ("ln1_g", "ln1_b", "ln2_g", "ln2_b", "ln3_g", "ln3_b", "mla_q_norm", "mla_kv_norm", "group_norm_g")]
        pos = a["nsa_cmp_pos"][l]
        c.append(np.concatenate([pos[:16].T, pos[16:].T]))
        pars.append(np.concatenate(c, 1))
    out["pars"] = np.stack(pars)
    w = a["w_in_2"][0]
    zo, xo, bo, co, to, lo, yo = 2048, 4096, 6144, 6656, 7168, 7200, 8480

    def tl(n):
        return tiles_of(w[:, n:n + P])

    out["ssm_dt"] = tiles_of(np.concatenate([w[:, to:to + 32], np.zeros((D, P - 32), np.float32)], 1))
    groups, pars_g = [], []
    cw, cbias = a["ssm_conv_w_2"][0], a["ssm_conv_b_2"][0]
    for g in range(4):
        conv = [bo + g * P, co + g * P] + [xo + (4 * g + j) * P for j in range(4)]
        rest = [zo + (4 * g + j) * P for j in range(4)] + [(2 * g + j) * P for j in range(2)]
        groups.append(np.stack([tl(n) for n in conv + rest]))
        cols = [cw[:, n - xo:n - xo + P].T for n in conv]
        cols += [cbias[n - xo:n - xo + P, None] for n in conv]
        cols += [np.repeat(a["ssm_d_2"][0, 8 * g + 2 * j:8 * g + 2 * j + 2], HD)[:, None] for j in range(4)]
        cols += [a["ssm_norm_w_2"][0, (4 * g + j) * P:(4 * g + j + 1) * P, None] for j in range(4)]
        cols += [a["b_branch_gate_2"][0, (2 * g + j) * P:(2 * g + j + 1) * P, None] for j in range(2)]
        pars_g.append(np.concatenate(cols, 1))
    out["ssm_in"], out["pars_g"] = np.stack(groups), np.stack(pars_g)
    wo = a["w_out_ssm_2"][0]
    out["ssm_out"] = np.stack([tiles_of(wo[hf * D:(hf + 1) * D, t * P:(t + 1) * P]) for t in range(DT) for hf in range(2)])
    out["lru_in"] = np.stack([tl(n + t * P) for t in range(10) for n in (lo, yo)])
    out["lru_ri"] = np.concatenate([a["lru_w_r_2"][0], a["lru_w_i_2"][0]], 2)
    cols = [a["lru_conv_w_2"][0], a["lru_conv_b_2"], a["lru_b_r_2"], a["lru_b_i_2"], np.zeros((1, 1280), np.float32)]
    out["lru_cols"] = np.concatenate(cols, 0).reshape(8, 10, P).transpose(1, 2, 0)
    out["lru_gate"] = np.stack([tl(D + t * P) for t in range(DT)])
    out["lru_out"] = np.stack(outs(a["w_out_lru_2"][0]))
    out["b2_out"] = np.stack(outs(a["w_out_2"][0]))
    p2 = np.zeros((P, NPAR2), np.float32)
    for at, v in ((RN1, a["norm1_w_2"][0]), (RN2, a["norm2_w_2"][0]), (RNF, a["norm_f_w_2"]), (RBG, a["b_branch_gate_2"][0]), (RLAM, a["lru_lambda_2"][0])):
        p2[:, at:at + v.size // P] = columns_of(v)
    p2[0:32, RDTB], p2[0:32, RALOG] = a["ssm_dt_bias_2"][0], a["ssm_a_log_2"][0]
    out["pars2"] = p2
    return {k: np.ascontiguousarray(v) for k, v in out.items()}


SHAPES = {
    "xT": [P, DT * SEQ], "consts": [P, NCONST], "ffn_up": [5, 2 * FT, P, D], "ffn_down": [5, 2 * DT, P, SLOT],
    "mix_in": [DEPTH, HT, P, D], "mix_tok": [DEPTH, P, DT * TW], "mix_out": [DEPTH, DT, P, D],
    "mla_uq": [DEPTH, P, 768], "mla_ukv": [DEPTH, P, 512], "cmp1": [DEPTH, P, 2048], "cmp2": [DEPTH, 64, 192],
    "pars": [DEPTH, P, NPAR], "ssm_dt": [P, D], "ssm_in": [4, 12, P, D], "pars_g": [4, P, NPG], "ssm_out": [16, P, D],
    "lru_in": [20, P, D], "lru_ri": [10, P, 2 * P], "lru_cols": [10, P, 8], "lru_gate": [DT, P, D], "lru_out": [DT, P, 10 * P],
    "b2_out": [DT, P, D], "pars2": [P, NPAR2],
}


class Core:

    def __init__(self, nc, ctx, dram, outT):
        self.nc, self.dram, self.outT = nc, dram, outT
        arena = ctx.enter_context(nc.sbuf_tensor("arena", [P, 212 * 1000 // 4], F32))
        self.base = 16512
        self.n = 0
        self.x = self.at("x", [P, DT, SEQ], F32, A_X)
        self.xh = self.at("xh", [P, DT, SEQ], F32R, A_XH)
        self.xl = self.at("xl", [P, DT, SEQ], F32R, A_XL)
        self.raw = self.at("raw", [P, RAW, SLOT], F32, A_RAW)
        self.whi = self.at("whi", [P, HALF, SLOT], F32R, A_WHI)
        self.wlo = self.at("wlo", [P, HALF, SLOT], F32R, A_WLO)
        self.consts = self.at("consts_sb", [P, NCONST], F32, A_CONST)
        self.par = self.at("par", [P, P], F32, A_PAR)
        self.k = {name: self.consts[:, n * P:(n + 1) * P] for n, name in enumerate(CONST_NAMES)}
        self.kb_all = self.at("consts_bf16", [P, N_BF16 * P], BF16, A_KB)
        self.kb = {name: self.kb_all[:, n * P:(n + 1) * P] for n, name in enumerate(CONST_NAMES[:N_BF16])}
        r = len(CONST_NAMES) * P
        self.cos64, self.sin64, self.cos32, self.sin32 = (self.consts[:, r + n * SEQ:r + (n + 1) * SEQ] for n in range(4))
        self.eps_ln, self.eps_rms = self.consts[:, NCONST - 8:NCONST - 7], self.consts[:, NCONST - 7:NCONST - 6]
        self.ps = ctx.enter_context(nc.psum_tensor("ps", [P, 8, SEQ], F32))

    def at(self, name, shape, dtype, offset):
        return self.nc.alloc_sbuf_tensor_at(name, shape, dtype, offset=self.base + offset)


class Phase:

    def __init__(self, core, ctx, name, sems):
        self.core, self.nc, self.name = core, core.nc, name
        names = [f"raw_in{r}" for r in range(RAW)] + ["hi_done", "lo_done", "slot_used"] + sems.split()
        self.handles, self.sems = [], {}
        for n in names:
            h = ctx.enter_context(core.nc.semaphore(f"{name}_{n}"))
            self.handles.append(h)
            self.sems[n] = h
        self.raw_in = [self.sems[f"raw_in{r}"] for r in range(RAW)]

    def __getitem__(self, name):
        return self.sems[name]

    def end(self):
        nums = sorted(h.num for h in self.handles)
        starts = [n for n in nums if n - 1 not in nums]
        for n in starts:
            self.nc.all_engine_barrier(sems_to_clear=range(n, next(k for k in range(n, n + 200) if k not in nums)))

    def load(self, sp, q, u, src, width, fresh=False):
        if not fresh:
            sp.wait_ge(self["lo_done"], 4 * q + u - (RAW - 1))
        sp.dma_start(self.core.raw[:, u, 0:width], src).then_inc(self.raw_in[u], 16)

    def hi(self, act, q, u, width):
        act.wait_ge(self.raw_in[u], 16 * q + 16)
        act.activation(self.core.whi[:, u % HALF, 0:width], self.core.raw[:, u, 0:width], ACT.Copy).then_inc(self["hi_done"], 1)

    def lo(self, dve, q, u, width):
        dve.wait_ge(self["hi_done"], 4 * q + u + 1)
        dve.tensor_tensor(self.core.wlo[:, u % HALF, 0:width], self.core.raw[:, u, 0:width],
                          self.core.whi[:, u % HALF, 0:width].bitcast(F32), ALU.subtract).then_inc(self["lo_done"], 1)

    def products(self, pe, q, u, out, xh, xl, k0, nk, first, last, ready=None):
        c = self.core
        pe.wait_ge(self["lo_done"], 4 * q + u + 1)
        for k in range(nk):
            w = slice(k * P, (k + 1) * P)
            h = u % HALF
            if ready is not None:
                pe.wait_ge(ready, k + 1)
            pe.matmul(out, c.whi[:, h, w], xh[:, k0 + k], start=first and k == 0, stop=False)
            pe.matmul(out, c.whi[:, h, w], xl[:, k0 + k], start=False, stop=False)
            mm = pe.matmul(out, c.wlo[:, h, w], xh[:, k0 + k], start=False, stop=last and k == nk - 1)
        mm.then_inc(self["slot_used"], 1)


def looped(engine, n, body, peel_first=0, peel_last=0):
    for i in range(peel_first):
        body(i)
    if n - peel_last > peel_first:
        with engine.Fori(peel_first, n - peel_last) as i:
            body(i)
    for i in range(n - peel_last, n):
        body(i)


def setup_phase(c):
    nc, d = c.nc, c.dram
    with ExitStack() as ctx:
        ph = Phase(c, ctx, "setup", "x_in consts_in kb_done xh_done xl_done")
        with nc.Block() as block:
            @block.sync
            def _(sp):
                sp.dma_start(c.x[:], d["xT"].rearrange("p (t n) -> p t n", t=DT)).then_inc(ph["x_in"], 16)
                sp.dma_start(c.consts[:], d["consts"]).then_inc(ph["consts_in"], 16)

            @block.scalar
            def _(act):
                act.wait_ge(ph["x_in"], 16)
                for t in range(DT):
                    act.activation(c.xh[:, t], c.x[:, t], ACT.Copy).then_inc(ph["xh_done"], 1)
                act.wait_ge(ph["consts_in"], 16)
                act.activation(c.kb_all[:], c.consts[:, 0:N_BF16 * P], ACT.Copy).then_inc(ph["kb_done"], 1)

            @block.vector
            def _(dve):
                for t in range(DT):
                    dve.wait_ge(ph["xh_done"], t + 1)
                    dve.tensor_tensor(c.xl[:, t], c.x[:, t], c.xh[:, t].bitcast(F32), ALU.subtract).then_inc(ph["xl_done"], 1)
                dve.wait_ge(ph["xl_done"], DT)
        ph.end()


NORM_SEMS = "mean_done xc_done sq_done sq_used std_done rstd_done xg_done xb_done xh_done xl_done"


class Norm:

    def __init__(self, ph, c, x_done, layer, g, b=None, tag="", final=False):
        self.ph, self.c, self.x_done, self.layer, self.g, self.b, self.final = ph, c, x_done, layer, g, b, final
        self.sq = c.at(f"{ph.name}_sq", [P, 2, SEQ], F32, A_WORK)
        self.std = c.at(f"{ph.name}_std", [P, SEQ], F32, A_WORK + 4 * KB)
        self.rstd = c.at(f"{ph.name}_rstd", [P, SEQ], F32, A_WORK + 6 * KB)
        self.t = c.at(f"{ph.name}_t", [P, DT, SEQ], F32, A_WORK + 8 * KB)

    def src(self, t):
        return self.c.x[:, t]

    def dst(self, t):
        return self.c.x[:, t] if self.layer else self.t[:, t]

    def pe(self, pe):
        ph, c = self.ph, self.c
        if self.layer:
            for t in range(DT):
                pe.wait_ge(self.x_done, t + 1)
                mm = pe.matmul(c.ps[:, 6], c.k["ones"], c.x[:, t], start=t == 0, stop=t == DT - 1)
            mm.then_inc(ph["mean_done"], 1)
        for t in range(DT):
            pe.wait_ge(ph["sq_done"], t + 1)
            pe.matmul(c.ps[:, 7], c.k["ones"], self.sq[:, t % 2], start=t == 0, stop=t == DT - 1).then_inc(ph["sq_used"], 1)

    def act(self, act):
        ph, c = self.ph, self.c
        for t in range(DT):
            act.wait_ge(ph["xc_done"] if self.layer else self.x_done, t + 1)
            if t >= 2:
                act.wait_ge(ph["sq_used"], t - 1)
            act.activation(self.sq[:, t % 2], c.x[:, t], ACT.Square).then_inc(ph["sq_done"], 1)
        act.wait_ge(ph["sq_used"], DT)
        act.activation(self.std[:], c.ps[:, 7], ACT.Sqrt, scale=1.0 / D,
                       bias=c.eps_ln if self.layer else c.eps_rms).then_inc(ph["std_done"], 1)
        for t in range(DT):
            act.wait_ge(ph["xg_done"], t + 1)
            if self.layer:
                act.activation(c.x[:, t], c.x[:, t], ACT.Identity, bias=c.par[:, self.b + t:self.b + t + 1]).then_inc(ph["xb_done"], 1)
                act.wait_ge(ph["xb_done"], t + 1)
            if not self.final:
                act.activation(c.xh[:, t], self.dst(t), ACT.Copy).then_inc(ph["xh_done"], 1)

    def dve(self, dve):
        ph, c = self.ph, self.c
        if self.layer:
            dve.wait_ge(ph["mean_done"], 1)
            for t in range(DT):
                dve.scalar_tensor_tensor(c.x[:, t], c.ps[:, 6], -1.0 / D, c.x[:, t], ALU.mult, ALU.add).then_inc(ph["xc_done"], 1)
        dve.wait_ge(ph["std_done"], 1)
        dve.reciprocal(self.rstd[:], self.std[:]).then_inc(ph["rstd_done"], 1)
        dve.wait_ge(ph["rstd_done"], 1)
        for t in range(DT):
            dve.scalar_tensor_tensor(self.dst(t), c.x[:, t], c.par[:, self.g + t:self.g + t + 1], self.rstd[:],
                                     ALU.mult, ALU.mult).then_inc(ph["xg_done"], 1)
            if not self.final and t >= 1:
                self.low(dve, t - 1)
        if not self.final:
            self.low(dve, DT - 1)

    def low(self, dve, t):
        ph, c = self.ph, self.c
        dve.wait_ge(ph["xh_done"], t + 1)
        dve.tensor_tensor(c.xl[:, t], self.dst(t), c.xh[:, t].bitcast(F32), ALU.subtract).then_inc(ph["xl_done"], 1)


def ffn_phase(c, name, f, g, b, res, half, layer, final=False, par_src=None):
    nc, d = c.nc, c.dram
    UP, DOWN = 2 * FT, 2 * DT
    with ExitStack() as ctx:
        ph = Phase(c, ctx, name, "gate_done prod_done hh_done hl_done bank_free yb_done res_done par_in out_done " + NORM_SEMS)
        hh = c.at(name + "_hh", [P, FT, SEQ], F32R, A_WORK)
        hl = c.at(name + "_hl", [P, FT, SEQ], F32R, A_WORK + FT * 2 * KB)
        gate = c.at(name + "_gate", [P, 2, SEQ], F32, A_WORK + FT * 4 * KB)
        norm = Norm(ph, c, ph["res_done"], layer, g, b, final=final)
        with nc.Block() as block:
            @block.sync
            def _(sp):
                sp.dma_start(c.par[:, 0:par_src.shape[-1]], par_src).then_inc(ph["par_in"], 16)

                def up(q, fresh=False):
                    for u in range(4):
                        ph.load(sp, q, u, d["ffn_up"][f, 4 * q + u], D, fresh)

                def down(j):
                    for u in range(4):
                        ph.load(sp, j + UP // 4, u, d["ffn_down"][f, 4 * j + u], SLOT)

                up(0, fresh=True)
                with sp.Fori(1, UP // 4) as q:
                    up(q)
                with sp.Fori(0, DOWN // 4) as j:
                    down(j)
                if final:
                    for t in range(DT):
                        sp.wait_ge(ph["xg_done"], t + 1)
                        sp.dma_start(c.outT[t * P:(t + 1) * P, :], norm.t[:, t]).then_inc(ph["out_done"], 16)
                    sp.wait_ge(ph["out_done"], 16 * DT)

            @block.tensor
            def _(pe):
                def up(q):
                    for u in range(4):
                        pe.wait_ge(ph["bank_free"], 2 * q + u // 2 + 1)
                        ph.products(pe, q, u, c.ps[:, u], c.xh, c.xl, 0, DT, True, True)

                def down(j):
                    for u in range(4):
                        t = u // 2
                        if u % 2 == 0:
                            pe.wait_ge(ph["bank_free"], UP // 2 + 2 * j + t + 1)
                        ph.products(pe, j + UP // 4, u, c.ps[:, 4 + t], hh, hl, 11 * (u % 2), 11, u % 2 == 0, u % 2 == 1)

                with pe.Fori(0, UP // 4) as q:
                    up(q)
                pe.wait_ge(ph["hl_done"], FT)
                with pe.Fori(0, DOWN // 4) as j:
                    down(j)
                norm.pe(pe)

            @block.scalar
            def _(act):
                def evacuate_up(q, u):
                    act.wait_ge(ph["slot_used"], 4 * q + u + 1)
                    if u % 2 == 0:
                        act.activation(gate[:, u // 2], c.ps[:, u], ACT.Silu).then_inc(ph["gate_done"], 1)
                    else:
                        p = 2 * q + u // 2
                        act.wait_ge(ph["prod_done"], p + 1)
                        act.activation(hh[:, p], gate[:, u // 2], ACT.Copy).then_inc(ph["hh_done"], 1)

                def evacuate_down(j, u):
                    act.wait_ge(ph["slot_used"], 4 * j + u + 1 + UP)
                    if u % 2 == 1:
                        act.wait_ge(ph["bank_free"], UP // 2 + 2 * j + u // 2 + 1)
                        act.activation(gate[:, u // 2], c.ps[:, 4 + u // 2], ACT.Copy, scale=half).then_inc(ph["yb_done"], 1)

                def up(q, last=False):
                    for u in range(4):
                        evacuate_up(q, u)
                        ph.hi(act, q + (u + 2) // 4, (u + 2) % 4, SLOT if last and u >= 2 else D)

                def down(j, last=False):
                    for u in range(4):
                        evacuate_down(j, u)
                        if not (last and u >= 2):
                            ph.hi(act, j + UP // 4 + (u + 2) // 4, (u + 2) % 4, SLOT)

                ph.hi(act, 0, 0, D)
                ph.hi(act, 0, 1, D)
                with act.Fori(0, UP // 4 - 1) as q:
                    up(q)
                up(UP // 4 - 1, last=True)
                with act.Fori(0, DOWN // 4 - 1) as j:
                    down(j)
                down(DOWN // 4 - 1, last=True)
                norm.act(act)

            @block.vector
            def _(dve):
                def evacuate_up(q, u):
                    if u % 2 == 1:
                        p = 2 * q + u // 2
                        dve.wait_ge(ph["slot_used"], 4 * q + u + 1)
                        dve.wait_ge(ph["gate_done"], p + 1)
                        dve.tensor_tensor(gate[:, u // 2], gate[:, u // 2], c.ps[:, u], ALU.mult).then_inc(ph["prod_done"], 1)
                        dve.wait_ge(ph["hh_done"], p + 1)
                        dve.tensor_tensor(hl[:, p], gate[:, u // 2], hh[:, p].bitcast(F32), ALU.subtract).then_inc(ph["hl_done"], 1)
                        dve.wait_ge(ph["hl_done"], p + 1)
                        dve.nop().then_inc(ph["bank_free"], 1)

                def evacuate_down(j, u):
                    if u % 2 == 1:
                        t = 2 * j + u // 2
                        dve.wait_ge(ph["yb_done"], t + 1)
                        dve.scalar_tensor_tensor(c.x[:, t], c.x[:, t], res, gate[:, u // 2], ALU.mult, ALU.add).then_inc(ph["res_done"], 1)
                        dve.wait_ge(ph["res_done"], t + 1)
                        dve.nop().then_inc(ph["bank_free"], 1)

                def up(q, last=False):
                    for u in range(4):
                        evacuate_up(q, u)
                        ph.lo(dve, q + (u + 2) // 4, (u + 2) % 4, SLOT if last and u >= 2 else D)

                def down(j, last=False):
                    for u in range(4):
                        evacuate_down(j, u)
                        if not (last and u >= 2):
                            ph.lo(dve, j + UP // 4 + (u + 2) // 4, (u + 2) % 4, SLOT)

                dve.nop().then_inc(ph["bank_free"], 2)
                ph.lo(dve, 0, 0, D)
                ph.lo(dve, 0, 1, D)
                with dve.Fori(0, UP // 4 - 1) as q:
                    up(q)
                up(UP // 4 - 1, last=True)
                with dve.Fori(0, DOWN // 4 - 1) as j:
                    down(j)
                down(DOWN // 4 - 1, last=True)
                dve.wait_ge(ph["par_in"], 16)
                norm.dve(dve)
        ph.end()


class Mixer:

    def __init__(self, c):
        W = A_WORK
        self.h = c.at("mix_h", [P, HT, SEQ], F32, W)
        self.tok = c.at("mix_tok_sb", [P, QB, TW], F32, W + 40 * KB)
        self.y = c.at("mix_y", [P, QB, D], F32, W + 48 * KB)
        self.qm = c.at("mla_q", [96, HEADS, SEQ], F32, A_XH)
        self.km = c.at("mla_k", [96, HEADS, SEQ], F32, A_XH + 8 * KB)
        self.vm = c.at("mla_v", [P, QB, HEADS * HD], F32, A_XL)
        self.kc = c.at("cmp_k", [P, NCMP], F32, A_XL + 12 * KB)
        self.vc = c.at("cmp_v", [NCMP, HD], F32, A_XL + 12 * KB + 256)


def mixer_projections(c, m, l):
    nc, d = c.nc, c.dram
    with ExitStack() as ctx:
        ph = Phase(c, ctx, "proj", "bank_free tokw_in tok_done tok_out gates_done")
        tw = c.at("tok_w", [P, DT, TW], F32, A_WORK + 64 * KB)
        with nc.Block() as block:
            @block.sync
            def _(sp):
                def four(q, fresh=False):
                    for u in range(4):
                        ph.load(sp, q, u, d["mix_in"][l, 4 * q + u], D, fresh)
                four(0, fresh=True)
                sp.dma_start(tw[:], d["mix_tok"][l].rearrange("p (t n) -> p t n", t=DT)).then_inc(ph["tokw_in"], 16)
                with sp.Fori(1, HT // 4) as q:
                    four(q)

            @block.tensor
            def _(pe):
                with pe.Fori(0, HT // 4) as q:
                    for u in range(4):
                        pe.wait_ge(ph["bank_free"], 4 * q + u + 1)
                        ph.products(pe, q, u, c.ps[:, u], c.xh, c.xl, 0, DT, True, True)
                pe.wait_ge(ph["tokw_in"], 16)
                for b in range(QB):
                    for t in range(DT):
                        mm = pe.matmul(c.ps[:, 4 + b, 0:TW], c.x[:, t, b * P:(b + 1) * P], tw[:, t], start=t == 0, stop=t == DT - 1)
                    mm.then_inc(ph["tok_done"], 1)

            @block.scalar
            def _(act):
                def four(q, last=False):
                    for u in range(4):
                        act.wait_ge(ph["slot_used"], 4 * q + u + 1)
                        act.activation(m.h[:, 4 * q + u], c.ps[:, u], ACT.Copy).then_inc(ph["bank_free"], 1)
                        if not (last and u >= 2):
                            ph.hi(act, q + (u + 2) // 4, (u + 2) % 4, D)
                act.nop().then_inc(ph["bank_free"], 4)
                ph.hi(act, 0, 0, D)
                ph.hi(act, 0, 1, D)
                with act.Fori(0, HT // 4 - 1) as q:
                    four(q)
                four(HT // 4 - 1, last=True)
                for b in range(QB):
                    act.wait_ge(ph["tok_out"], b + 1)
                    gate = m.tok[:, b, GATE:GATE + 3 * HEADS]
                    act.activation(gate, gate, ACT.Sigmoid).then_inc(ph["gates_done"], 1)

            @block.vector
            def _(dve):
                def four(q, last=False):
                    for u in range(4):
                        if not (last and u >= 2):
                            ph.lo(dve, q + (u + 2) // 4, (u + 2) % 4, D)
                ph.lo(dve, 0, 0, D)
                ph.lo(dve, 0, 1, D)
                with dve.Fori(0, HT // 4 - 1) as q:
                    four(q)
                four(HT // 4 - 1, last=True)
                for b in range(QB):
                    dve.wait_ge(ph["tok_done"], b + 1)
                    dve.tensor_copy(m.tok[:, b], c.ps[:, 4 + b, 0:TW]).then_inc(ph["tok_out"], 1)
        ph.end()


def mixer_preparation(c, m, l):
    nc, d = c.nc, c.dram
    W = A_WORK + 64 * KB
    t1 = c.at("rope_sin", [P, 2, SEQ], F32, W)
    t2 = c.at("rope_cos", [P, 2, SEQ], F32, W + 4 * KB)
    uq = c.at("uq_w", [P, 2, HEADS * 96], F32, W + 8 * KB)
    ukv = c.at("ukv_w", [P, 2, HEADS * HD], F32, W + 11 * KB)
    c1 = c.at("cmp_w1", [P, 2, 16, HD], F32, W + 13 * KB)
    c2 = c.at("cmp_w2", [64, 192], F32, W + 21 * KB)
    sq = c.at("lat_sq", [P, 3, SEQ], F32, W + 22 * KB)
    std = c.at("lat_std", [P, 2, SEQ], F32, W + 28 * KB)
    rstd = c.at("lat_rstd", [P, 2, SEQ], F32, W + 32 * KB)
    win = c.at("cmp_win", [P, 2, SEQ], F32, A_XL + 4 * KB)
    hid = c.at("cmp_hid", [64, 2, NCMP], F32, A_XL + 13 * KB)
    ropes = [(m.h[:, t], "sw64", c.cos64, c.sin64, 0, P) for t in (NSAQ, NSAQ + 1, KCMP, KSLC, KWIN, DSAQ, DSAQ + 1, DSAK)]
    ropes = [(m.h[:, t], "sw32", c.cos32, c.sin32, 0, P) for t in (KROPE, IDXQ, IDXQ + 1, IDXK)] + ropes
    kcmp_rope = 4 + 2
    ropes += [(m.qm[:, h], "sw32", c.cos32, c.sin32, 64, 96) for h in range(HEADS)]
    nh = len(ropes) - HEADS
    with ExitStack() as ctx:
        ph = Phase(c, ctx, "prep", "w_in c1_in c2_in swap_done cos_done sin_done rope_done sq_done sum_done std_done rstd_done "
                   "lat_done uq_done qm_done uk_done km_done kpe_done uv_done vm_done win_done hid_done gelu_done kv_done cmp_done ukv_in")
        with nc.Block() as block:
            @block.sync
            def _(sp):
                sp.dma_start(uq[:], d["mla_uq"][l].rearrange("p (t n) -> p t n", t=2)).then_inc(ph["w_in"], 16)
                sp.dma_start(ukv[:], d["mla_ukv"][l].rearrange("p (t n) -> p t n", t=2)).then_inc(ph["ukv_in"], 16)
                sp.dma_start(c1[:], d["cmp1"][l].rearrange("p (a j n) -> p a j n", a=2, j=16)).then_inc(ph["c1_in"], 16)
                sp.dma_start(c2[:], d["cmp2"][l]).then_inc(ph["c2_in"], 16)

            @block.tensor
            def _(pe):
                def swap(r):
                    src, sw, _, _, _, hi = ropes[r]
                    n = P if hi == P else 96
                    if r >= 2:
                        pe.wait_ge(ph["sin_done"], r - 1)
                    pe.matmul(c.ps[0:n, r % 2], c.k[sw][0:n, 0:n], src[0:n], start=True, stop=True).then_inc(ph["swap_done"], 1)

                swap(0)
                swap(1)
                pe.wait_ge(ph["sq_done"], 3)
                for t in range(3):
                    mm = pe.matmul(c.ps[:, 2 + t // 2], c.k["ones"], sq[:, t], start=t != 1, stop=t != 0)
                mm.then_inc(ph["sum_done"], 1)
                for r in range(2, nh):
                    swap(r)
                pe.wait_ge(ph["w_in"], 16)
                pe.wait_ge(ph["lat_done"], 3)
                for h in range(HEADS):
                    for t in range(2):
                        mm = pe.matmul(c.ps[0:96, 4 + h], uq[:, t, h * 96:(h + 1) * 96], m.h[:, CQ + t], start=t == 0, stop=t == 1)
                    mm.then_inc(ph["uq_done"], 1)
                for h in range(HEADS):
                    pe.wait_ge(ph["qm_done"], h + 1)
                    swap(nh + h)
                pe.wait_ge(ph["ukv_in"], 16)
                for h in range(HEADS):
                    pe.matmul(c.ps[0:64, 4 + h], ukv[:, 0, h * HD:(h + 1) * HD], m.h[:, CKV], start=True, stop=True).then_inc(ph["uk_done"], 1)
                pe.wait_ge(ph["std_done"], 2)
                for b in range(QB):
                    mm = pe.matmul(c.ps[:, 2 + b // 2, (b % 2) * 256:(b % 2) * 256 + 256], m.h[:, CKV, b * P:(b + 1) * P], ukv[:, 1],
                                   start=True, stop=True)
                mm.then_inc(ph["uv_done"], 1)
                pe.wait_ge(ph["c1_in"], 16)
                pe.wait_ge(ph["c2_in"], 16)
                pe.wait_ge(ph["win_done"], 4)
                pe.wait_ge(ph["km_done"], HEADS)
                for a in range(2):
                    for j in range(16):
                        mm = pe.matmul(c.ps[0:64, 4 + a, 0:NCMP], c1[:, a, j], win[:, a, j:j + 16 * (NCMP - 1) + 1:16], start=j == 0, stop=j == 15)
                mm.then_inc(ph["hid_done"], 1)
                pe.wait_ge(ph["gelu_done"], 2)
                pe.matmul(c.ps[:, 6, 0:NCMP], c2[:, 0:P], hid[:, 0], start=True, stop=True)
                pe.matmul(c.ps[0:NCMP, 7, 0:HD], hid[:, 1], c2[:, P:P + HD], start=True, stop=True).then_inc(ph["kv_done"], 1)

            @block.scalar
            def _(act):
                for t in range(3):
                    act.activation(sq[:, t], m.h[:, CQ + t], ACT.Square).then_inc(ph["sq_done"], 1)
                act.wait_ge(ph["sum_done"], 1)
                act.activation(std[:, 0], c.ps[:, 2], ACT.Sqrt, scale=1.0 / 256, bias=c.eps_rms).then_inc(ph["std_done"], 1)
                act.activation(std[:, 1], c.ps[:, 3], ACT.Sqrt, scale=1.0 / 128, bias=c.eps_rms).then_inc(ph["std_done"], 1)
                for h in range(HEADS):
                    act.wait_ge(ph["uq_done"], h + 1)
                    act.activation(m.qm[:, h], c.ps[0:96, 4 + h], ACT.Copy).then_inc(ph["qm_done"], 1)
                for h in range(HEADS):
                    act.wait_ge(ph["uk_done"], h + 1)
                    act.activation(m.km[0:64, h], c.ps[0:64, 4 + h], ACT.Copy).then_inc(ph["km_done"], 1)
                act.wait_ge(ph["uv_done"], 1)
                for b in range(2):
                    act.activation(m.vm[:, 2 * b:2 * b + 2], c.ps[:, 2 + b].rearrange("p (b n) -> p b n", b=2), ACT.Copy).then_inc(ph["vm_done"], 1)
                act.wait_ge(ph["hid_done"], 1)
                for a in range(2):
                    act.activation(hid[:, a], c.ps[0:64, 4 + a, 0:NCMP], ACT.Gelu_apprx_tanh).then_inc(ph["gelu_done"], 1)
                act.wait_ge(ph["kv_done"], 1)
                act.activation(m.kc[:], c.ps[:, 6, 0:NCMP], ACT.Copy).then_inc(ph["cmp_done"], 1)
                act.activation(m.vc[:], c.ps[0:NCMP, 7, 0:HD], ACT.Copy).then_inc(ph["cmp_done"], 1)

            @block.gpsimd
            def _(pool):
                for r, (src, _, cos, _, lo, hi) in enumerate(ropes):
                    if r >= 2:
                        pool.wait_ge(ph["rope_done"], r - 1)
                    if r >= nh:
                        pool.wait_ge(ph["qm_done"], r - nh + 1)
                        pool.wait_ge(ph["kpe_done"], HEADS)
                    pool.tensor_tensor(t2[lo:hi, r % 2], src[lo:hi], cos[lo:hi], ALU.mult).then_inc(ph["cos_done"], 1)
                    if r == nh - 1:
                        pool.wait_ge(ph["cos_done"], nh)
                        for h in range(HEADS):
                            pool.tensor_copy(m.km[64:96, h], m.h[64:96, KROPE]).then_inc(ph["kpe_done"], 1)

            @block.vector
            def _(dve):
                def rope(r):
                    src, _, _, sin, lo, hi = ropes[r]
                    dve.wait_ge(ph["swap_done"], r + 1)
                    dve.tensor_tensor(t1[lo:hi, r % 2], c.ps[lo:hi, r % 2], sin[lo:hi], ALU.mult).then_inc(ph["sin_done"], 1)
                    dve.wait_ge(ph["sin_done"], r + 1)
                    dve.wait_ge(ph["cos_done"], r + 1)
                    dve.tensor_tensor(src[lo:hi], t1[lo:hi, r % 2], t2[lo:hi, r % 2], ALU.add).then_inc(ph["rope_done"], 1)

                rope(0)
                rope(1)
                for n in range(2):
                    dve.wait_ge(ph["std_done"], n + 1)
                    dve.reciprocal(rstd[:, n], std[:, n]).then_inc(ph["rstd_done"], 1)
                dve.wait_ge(ph["rstd_done"], 2)
                for t in range(3):
                    g = c.par[:, PQN + t:PQN + t + 1]
                    dve.scalar_tensor_tensor(m.h[:, CQ + t], m.h[:, CQ + t], g, rstd[:, t // 2], ALU.mult, ALU.mult).then_inc(ph["lat_done"], 1)
                for r in range(2, nh):
                    rope(r)
                for a, t in enumerate((KCMP, VCMP)):
                    for lo in (0, 64):
                        off = 16 * (lo // 64)
                        pos = c.par[lo:lo + 64, PPOS:PPOS + 16].unsqueeze(1).broadcast_to([64, NCMP, 16])
                        src = m.h[lo:lo + 64, t, off:off + 16 * NCMP].rearrange("p (n j) -> p n j", j=16)
                        if a == 0:
                            dve.wait_ge(ph["rope_done"], kcmp_rope + 1)
                        dve.tensor_tensor(win[lo:lo + 64, a, 0:16 * NCMP].rearrange("p (n j) -> p n j", j=16), src, pos,
                                          ALU.add).then_inc(ph["win_done"], 1)
                for r in range(nh, len(ropes)):
                    rope(r)
        ph.end()


def attention_units(m, c):
    units = []

    def rows(tile, h):
        return tile[64 * (h % 2):64 * (h % 2) + 64]

    for h in range(HEADS):
        for b in range(QB):
            units.append(dict(q=m.qm[:, h, b * P:(b + 1) * P], k=m.km[:, h, 0:(b + 1) * P], mask=c.kb["negd"], at=b * P, width=(b + 1) * P,
                              scale=96 ** -0.5, v=[m.vm[:, j, h * HD:(h + 1) * HD] for j in range(b + 1)], gate=None, mixer=0, h=h, b=b,
                              first=True, clamp=False))
    for h in range(HEADS):
        for b in range(QB):
            q = rows(m.h[:, NSAQ + h // 2], h)[:, b * P:(b + 1) * P]
            units.append(dict(q=q, k=rows(m.kc, h), mask=c.kb["cmpm"][:, b * NCMP:(b + 1) * NCMP], at=0, width=NCMP, scale=HD ** -0.5,
                              v=[m.vc[:]], gate=m.tok[:, b, GATE + h:GATE + h + 1], mixer=1, h=h, b=b, first=True, clamp=True))
            for br, (kt, vt) in enumerate(((KSLC, VSLC), (KWIN, VWIN))):
                g = GATE + (br + 1) * HEADS + h
                units.append(dict(q=q, k=rows(m.h[:, kt], h)[:, 0:(b + 1) * P], mask=c.kb["negd"], at=b * P, width=(b + 1) * P,
                                  scale=HD ** -0.5, v=[m.tok[:, j, vt:vt + HD] for j in range(b + 1)], gate=m.tok[:, b, g:g + 1],
                                  mixer=1, h=h, b=b, first=False, clamp=False))
    return units


def dsa_units(m, c, allowed):
    units = []
    for h in range(HEADS):
        lo = 64 * (h % 2)
        for b in range(QB):
            mask = c.kb["negd"] if b == 0 else allowed[b]
            units.append(dict(q=m.h[lo:lo + 64, DSAQ + h // 2, b * P:(b + 1) * P], k=m.h[lo:lo + 64, DSAK, 0:(b + 1) * P], mask=mask, at=0,
                              width=(b + 1) * P, scale=HD ** -0.5, v=[m.tok[:, j, DSAV:DSAV + HD] for j in range(b + 1)], gate=None,
                              mixer=2, h=h, b=b, first=True, clamp=False))
    return units


def mixer_attention(c, m, l):
    nc = c.nc
    W = A_WORK + 64 * KB
    p = c.at("att_p", [P, 3, SEQ], F32, W)
    pt = c.at("att_pt", [P, 2, SEQ], F32, W + 6 * KB)
    rel = c.at("idx_rel", [P, 4, SEQ], F32, W + 10 * KB)
    sizes = {b: (b + 1) * P for b in range(1, QB)}
    picked, allowed, off = {}, {}, W + 18 * KB
    for b in range(1, QB):
        picked[b] = c.at(f"idx_score{b}", [P, sizes[b]], F32, off)[:]
        off += sizes[b] * 4
    for b in range(1, QB):
        allowed[b] = c.at(f"idx_allowed{b}", [P, sizes[b]], BF16, off)[:]
        off += sizes[b] * 2
    stat = c.at("att_stat", [P, 4, 8], F32, off)
    top8 = c.at("idx_top", [P, 8], F32, off + 128)[:]
    units = attention_units(m, c)
    n_dsa = len(units)
    units += dsa_units(m, c, allowed)
    n = len(units)
    rels = [(b, h) for b in range(1, QB) for h in range(IDXH)]
    rounds = [(b, r) for b in range(1, QB) for r in range(TOPK // 8)]
    per_unit = -(-len(rounds) // (n_dsa - 4))
    with ExitStack() as ctx:
        ph = Phase(c, ctx, "att", "rel_done relu_done acc_done scores_done max_done nmax_done exp_done sum_done rinv_done scale_done t_done "
                   "pt_done pv_done y_done top_done took_done choice_done")
        with nc.Block() as block:
            @block.tensor
            def _(pe):
                def index_scores(i):
                    b, h = rels[i]
                    lo = 32 * (h % 4)
                    if i >= 4:
                        pe.wait_ge(ph["relu_done"], i - 3)
                    pe.matmul(c.ps[:, 4 + i % 4, 0:sizes[b]], m.h[lo:lo + 32, IDXQ + h // 4, b * P:(b + 1) * P],
                              m.h[lo:lo + 32, IDXK, 0:sizes[b]], start=True, stop=True).then_inc(ph["rel_done"], 1)

                def scores(u):
                    x = units[u]
                    if u >= 4:
                        pe.wait_ge(ph["exp_done"], u - 3)
                    if u == n_dsa:
                        pe.wait_ge(ph["choice_done"], QB - 1)
                    s = c.ps[:, u % 4]
                    mw = x["mask"].shape[-1]
                    pe.matmul(s[:, 0:x["width"]], x["q"], x["k"], start=True, stop=False)
                    pe.matmul(s[:, x["at"]:x["at"] + mw], c.kb["ident"], x["mask"], start=False, stop=True).then_inc(ph["scores_done"], 1)

                def transposes(u):
                    x = units[u]
                    pe.wait_ge(ph["exp_done"], u + 1)
                    if u >= 2:
                        pe.wait_ge(ph["pt_done"], u - 1)
                    for j in range(len(x["v"])):
                        w = min(P, x["width"])
                        mm = pe.transpose(c.ps[0:w, 6 + u % 2, j * P:(j + 1) * P], p[:, u % 3, j * P:j * P + w], c.k["ident"])
                    mm.then_inc(ph["t_done"], 1)

                def values(u):
                    x = units[u]
                    pe.wait_ge(ph["pt_done"], u + 1)
                    if u >= 2:
                        pe.wait_ge(ph["y_done"], u - 1)
                    w = min(P, x["width"])
                    for j, v in enumerate(x["v"]):
                        mm = pe.matmul(c.ps[:, 4 + u % 2, 0:HD], pt[0:w, u % 2, j * P:(j + 1) * P], v, start=j == 0, stop=j == len(x["v"]) - 1)
                    mm.then_inc(ph["pv_done"], 1)

                for u in range(3):
                    scores(u)
                for i in range(len(rels)):
                    index_scores(i)
                pe.wait_ge(ph["relu_done"], len(rels))
                for u in range(n):
                    if u + 3 < n:
                        scores(u + 3)
                    transposes(u)
                    if u >= 1:
                        values(u - 1)
                values(n - 1)

            @block.scalar
            def _(act):
                for i, (b, h) in enumerate(rels):
                    act.wait_ge(ph["rel_done"], i + 1)
                    if i >= 4:
                        act.wait_ge(ph["acc_done"], i - 3)
                    act.activation(rel[:, i % 4, 0:sizes[b]], c.ps[:, 4 + i % 4, 0:sizes[b]], ACT.Relu,
                                   scale=(IDXH * 32) ** -0.5).then_inc(ph["relu_done"], 1)

                def exponentials(u):
                    x = units[u]
                    act.wait_ge(ph["nmax_done"], u + 1)
                    if u >= 3:
                        act.wait_ge(ph["t_done"], u - 2)
                    act.activation(p[:, u % 3, 0:x["width"]], c.ps[:, u % 4, 0:x["width"]], ACT.Exp, scale=x["scale"],
                                   bias=stat[:, u % 4, 1:2], accum_out=stat[:, u % 4, 2:3]).then_inc(ph["exp_done"], 1)

                def copy_transposed(u):
                    x = units[u]
                    act.wait_ge(ph["t_done"], u + 1)
                    if u >= 2:
                        act.wait_ge(ph["pv_done"], u - 1)
                    w = min(P, x["width"])
                    act.activation(pt[0:w, u % 2, 0:len(x["v"]) * P], c.ps[0:w, 6 + u % 2, 0:len(x["v"]) * P], ACT.Copy).then_inc(ph["pt_done"], 1)

                exponentials(0)
                for u in range(n):
                    if u + 1 < n:
                        exponentials(u + 1)
                    copy_transposed(u)

            @block.vector
            def _(dve):
                took = [0]

                def choose(k):
                    for b, r in rounds[took[0]:took[0] + k]:
                        w = picked[b]
                        if r == 0:
                            dve.wait_ge(ph["acc_done"], len(rels) + QB - 1)
                        dve.max(top8, w).then_inc(ph["top_done"], 1)
                        dve.wait_ge(ph["top_done"], took[0] + 1)
                        dve.match_replace(w, top8, w, TAKEN).then_inc(ph["took_done"], 1)
                        took[0] += 1
                        dve.wait_ge(ph["took_done"], took[0])
                        if r == TOPK // 8 - 1:
                            dve.tensor_scalar(allowed[b], w, TAKEN, NEG, ALU.not_equal, ALU.mult).then_inc(ph["choice_done"], 1)

                def maximum(u):
                    x = units[u]
                    s = u % 4
                    dve.wait_ge(ph["scores_done"], u + 1)
                    dve.reduce_max(stat[:, s, 0:1], c.ps[:, u % 4, 0:x["width"]], AXX).then_inc(ph["max_done"], 1)
                    dve.wait_ge(ph["max_done"], u + 1)
                    dve.tensor_scalar(stat[:, s, 1:2], stat[:, s, 0:1], -x["scale"], 1e27, ALU.mult, ALU.min).then_inc(ph["nmax_done"], 1)

                def finish(u):
                    x = units[u]
                    s = u % 4
                    total, rinv, scale = stat[:, s, 2:3], stat[:, s, 3:4], stat[:, s, 4:5]
                    dve.wait_ge(ph["exp_done"], u + 1)
                    if x["clamp"]:
                        dve.tensor_scalar(total, total, 1e-30, None, ALU.max).then_inc(ph["sum_done"], 1)
                        dve.wait_ge(ph["sum_done"], sum(y["clamp"] for y in units[:u + 1]))
                    dve.reciprocal(rinv, total).then_inc(ph["rinv_done"], 1)
                    dve.wait_ge(ph["rinv_done"], u + 1)
                    if x["gate"] is None:
                        scale = rinv
                    else:
                        dve.tensor_tensor(scale, rinv, x["gate"], ALU.mult).then_inc(ph["scale_done"], 1)
                        dve.wait_ge(ph["scale_done"], sum(y["gate"] is not None for y in units[:u + 1]))
                    dve.wait_ge(ph["pv_done"], u + 1)
                    col = x["mixer"] * HEADS * HD + x["h"] * HD
                    out = m.y[:, x["b"], col:col + HD]
                    if x["first"]:
                        dve.tensor_scalar(out, c.ps[:, 4 + u % 2, 0:HD], scale, None, ALU.mult).then_inc(ph["y_done"], 1)
                    else:
                        dve.wait_ge(ph["y_done"], u)
                        dve.scalar_tensor_tensor(out, c.ps[:, 4 + u % 2, 0:HD], scale, out, ALU.mult, ALU.add).then_inc(ph["y_done"], 1)

                maximum(0)
                maximum(1)
                for i, (b, h) in enumerate(rels):
                    dve.wait_ge(ph["relu_done"], i + 1)
                    wt = m.tok[:, b, IDXW + h:IDXW + h + 1]
                    src = rel[:, i % 4, 0:sizes[b]]
                    if h == 0:
                        dve.tensor_scalar(picked[b], src, wt, None, ALU.mult).then_inc(ph["acc_done"], 1)
                    else:
                        dve.wait_ge(ph["acc_done"], i)
                        dve.scalar_tensor_tensor(picked[b], src, wt, picked[b], ALU.mult, ALU.add).then_inc(ph["acc_done"], 1)
                dve.wait_ge(ph["acc_done"], len(rels))
                for b in range(1, QB):
                    own = picked[b][:, b * P:(b + 1) * P]
                    dve.tensor_tensor(own, own, c.k["negd"], ALU.add).then_inc(ph["acc_done"], 1)
                for u in range(n):
                    if u + 2 < n:
                        maximum(u + 2)
                    if u >= 1:
                        finish(u - 1)
                    choose(per_unit)
                finish(n - 1)
        ph.end()


def mixer_stick_breaking(c, m, l):
    nc = c.nc
    W = A_WORK + 64 * KB
    sp_ = c.at("sb_sp", [P, 2, QB, SEQ], F32, W)
    e = c.at("sb_e", [P, 3, SEQ], F32, W + 16 * KB)
    a = c.at("sb_a", [P, 2, SEQ], F32, W + 22 * KB)
    units = [(h, b) for h in range(HEADS) for b in reversed(range(QB))]
    n = len(units)
    with ExitStack() as ctx:
        ph = Phase(c, ctx, "stick", "q_done z_done abs_done e_done l_done spraw_done sp_done after_done a_done pv_done y_out")
        with nc.Block() as block:
            @block.tensor
            def _(pe):
                def scores(u):
                    h, b = units[u]
                    r = slice(64 * (h % 2), 64 * (h % 2) + 64)
                    if u >= 4:
                        pe.wait_ge(ph["a_done"], u - 3)
                    pe.matmul(c.ps[:, u % 4, b * P:SEQ], m.h[r, SBK + h // 2, b * P:(b + 1) * P], m.h[r, SBQ + h // 2, b * P:SEQ],
                              start=True, stop=True, skip_group_check=True).then_inc(ph["z_done"], 1)

                def after(u):
                    h, b = units[u]
                    pe.wait_ge(ph["sp_done"], u + 1)
                    for j in range(b, QB):
                        pe.matmul(c.ps[:, u % 4, j * P:SEQ], c.k["ntri" if j == b else "nones"], sp_[:, h % 2, j, j * P:SEQ],
                                  start=False, stop=True, skip_group_check=True)
                    pe.matmul(c.ps[:, u % 4, b * P:(b + 1) * P], c.kb["ident"], c.kb["negs"], start=False, stop=True,
                              skip_group_check=True).then_inc(ph["after_done"], 1)

                def values(u):
                    h, b = units[u]
                    pe.wait_ge(ph["a_done"], u + 1)
                    if h >= 2 and b == QB - 1:
                        pe.wait_ge(ph["y_out"], h - 1)
                    for j in reversed(range(b, QB)):
                        mm = pe.matmul(c.ps[:, 4 + h % 2, j * HD:(j + 1) * HD], a[:, u % 2, j * P:(j + 1) * P],
                                       m.tok[:, b, SBV + h * HD:SBV + (h + 1) * HD], start=b == QB - 1 and j == QB - 1, stop=True, skip_group_check=True)
                    mm.then_inc(ph["pv_done"], 1)

                pe.wait_ge(ph["q_done"], 2)
                scores(0)
                scores(1)
                for u in range(n):
                    if u + 2 < n:
                        scores(u + 2)
                    after(u)
                    if u >= 1:
                        values(u - 1)
                values(n - 1)

            @block.scalar
            def _(act):
                for t in range(2):
                    act.activation(m.h[:, SBQ + t], m.h[:, SBQ + t], ACT.Copy, scale=HD ** -0.5).then_inc(ph["q_done"], 1)

                def softplus_part(u):
                    h, b = units[u]
                    s = slice(b * P, SEQ)
                    act.wait_ge(ph["z_done"], u + 1)
                    if u >= 3:
                        act.wait_ge(ph["spraw_done"], u - 2)
                    act.activation(e[:, u % 3, s], c.ps[:, u % 4, s], ACT.Abs).then_inc(ph["abs_done"], 1)
                    act.wait_ge(ph["abs_done"], u + 1)
                    act.activation(e[:, u % 3, s], e[:, u % 3, s], ACT.Exp, scale=-1.0).then_inc(ph["e_done"], 1)
                    act.wait_ge(ph["e_done"], u + 1)
                    act.activation(e[:, u % 3, s], e[:, u % 3, s], ACT.Ln, bias=1.0).then_inc(ph["l_done"], 1)

                def weights(u):
                    h, b = units[u]
                    act.wait_ge(ph["after_done"], u + 1)
                    if u >= 2:
                        act.wait_ge(ph["pv_done"], u - 1)
                    act.activation(a[:, u % 2, b * P:SEQ], c.ps[:, u % 4, b * P:SEQ], ACT.Exp).then_inc(ph["a_done"], 1)

                act.preload_act_table_set("natural_log_exp_and_others")
                softplus_part(0)
                softplus_part(1)
                for u in range(n):
                    if u + 2 < n:
                        softplus_part(u + 2)
                    weights(u)

            @block.vector
            def _(dve):
                def softplus(u):
                    h, b = units[u]
                    s = slice(b * P, SEQ)
                    out = sp_[:, h % 2, b]
                    dve.wait_ge(ph["l_done"], u + 1)
                    if h >= 2 and b == QB - 1:
                        dve.wait_ge(ph["after_done"], QB * (h - 1))
                    dve.scalar_tensor_tensor(out[:, s], c.ps[:, u % 4, s], 0.0, e[:, u % 3, s], ALU.max, ALU.add).then_inc(ph["spraw_done"], 1)
                    dve.wait_ge(ph["spraw_done"], u + 1)
                    own = out[:, b * P:(b + 1) * P]
                    dve.tensor_tensor(own, own, c.k["strict"], ALU.mult).then_inc(ph["sp_done"], 1)

                def head_out(h):
                    col = 3 * HEADS * HD + h * HD
                    dve.wait_ge(ph["pv_done"], QB * (h + 1))
                    dve.tensor_copy(m.y[:, :, col:col + HD], c.ps[:, 4 + h % 2, 0:QB * HD].rearrange("p (b n) -> p b n", b=QB)).then_inc(ph["y_out"], 1)

                for u in range(n):
                    softplus(u)
                    if u >= 2 and units[u - 2][1] == 0:
                        head_out(units[u - 2][0])
                head_out(HEADS - 1)
        ph.end()


def mixer_output(c, m, l):
    nc, d = c.nc, c.dram
    W = A_WORK + 64 * KB
    GW = HEADS * HD
    sq = c.at("gn_sq", [P, GW], F32, W)
    ssum = c.at("gn_sum", [P, 4, QB], F32, W + 1 * KB)
    std = c.at("gn_std", [P, 4, QB], F32, W + 1 * KB + 64)
    rstd = c.at("gn_rstd", [P, 4, QB], F32, W + 1 * KB + 128)
    with ExitStack() as ctx:
        ph = Phase(c, ctx, "mout", "gsq_done gstd_done grstd_done yg_done yt_done yh_done yl_done res_done bank_free " + NORM_SEMS)
        norm = Norm(ph, c, ph["res_done"], True, PG2, PB2)
        with nc.Block() as block:
            @block.sync
            def _(sp):
                for u in range(4):
                    ph.load(sp, 0, u, d["mix_out"][l, u], D, fresh=True)
                for u in range(4):
                    ph.load(sp, 1, u, d["mix_out"][l, 4 + u], D)

            @block.tensor
            def _(pe):
                for g in range(4):
                    pe.wait_ge(ph["yg_done"], QB * (g + 1))
                    for t in (2 * g, 2 * g + 1):
                        if t >= 4:
                            pe.wait_ge(ph["yl_done"], t - 3)
                        for b in range(QB):
                            mm = pe.transpose(c.ps[:, t % 4, b * P:(b + 1) * P], m.y[:, b, t * P:(t + 1) * P], c.k["ident"])
                        mm.then_inc(ph["yt_done"], 1)
                for t in range(DT):
                    if t >= 2:
                        pe.wait_ge(ph["res_done"], t - 1)
                    ph.products(pe, t // 4, t % 4, c.ps[:, 4 + t % 2], c.xh, c.xl, 0, DT, True, True, ready=ph["yl_done"] if t == 0 else None)
                norm.pe(pe)

            @block.scalar
            def _(act):
                for g in range(4):
                    for b in range(QB):
                        n = g * QB + b
                        if n >= 1:
                            act.wait_ge(ph["gsq_done"], n)
                        act.activation(sq[:], m.y[:, b, g * GW:(g + 1) * GW], ACT.Square, accum_out=ssum[:, g, b:b + 1]).then_inc(ph["gsq_done"], 1)
                    act.wait_ge(ph["gsq_done"], QB * (g + 1))
                    act.activation(std[:, g], ssum[:, g], ACT.Sqrt, scale=1.0 / GW, bias=c.eps_rms).then_inc(ph["gstd_done"], 1)
                ph.hi(act, 0, 0, D)
                ph.hi(act, 0, 1, D)
                for t in range(DT):
                    act.wait_ge(ph["yt_done"], t + 1)
                    act.activation(c.xh[:, t], c.ps[:, t % 4], ACT.Copy, scale=c.par[:, PGN + t:PGN + t + 1]).then_inc(ph["yh_done"], 1)
                for t in range(DT - 2):
                    act.wait_ge(ph["slot_used"], t + 1)
                    ph.hi(act, (t + 2) // 4, (t + 2) % 4, D)
                norm.act(act)

            @block.vector
            def _(dve):
                for g in range(4):
                    dve.wait_ge(ph["gstd_done"], g + 1)
                    dve.reciprocal(rstd[:, g], std[:, g]).then_inc(ph["grstd_done"], 1)
                    dve.wait_ge(ph["grstd_done"], g + 1)
                    for b in range(QB):
                        y = m.y[:, b, g * GW:(g + 1) * GW]
                        dve.tensor_scalar(y, y, rstd[:, g, b:b + 1], None, ALU.mult).then_inc(ph["yg_done"], 1)
                ph.lo(dve, 0, 0, D)
                ph.lo(dve, 0, 1, D)
                for t in range(DT):
                    dve.wait_ge(ph["yh_done"], t + 1)
                    dve.scalar_tensor_tensor(c.xl[:, t], c.ps[:, t % 4], c.par[:, PGN + t:PGN + t + 1], c.xh[:, t].bitcast(F32), ALU.mult,
                                             ALU.subtract).then_inc(ph["yl_done"], 1)
                for t in range(DT):
                    if t < DT - 2:
                        ph.lo(dve, (t + 2) // 4, (t + 2) % 4, D)
                    dve.wait_ge(ph["slot_used"], t + 1)
                    dve.scalar_tensor_tensor(c.x[:, t], c.x[:, t], ALPHA, c.ps[:, 4 + t % 2], ALU.mult, ALU.add).then_inc(ph["res_done"], 1)
                norm.dve(dve)
        ph.end()


def mixer(c, m, l):
    mixer_projections(c, m, l)
    mixer_preparation(c, m, l)
    mixer_attention(c, m, l)
    mixer_stick_breaking(c, m, l)
    mixer_output(c, m, l)


SSM_G = 4
SSM_SLOTS = 12
CH = SEQ // P
LRU_T = 10


class Second:

    def __init__(self, c):
        W = A_WORK
        self.ys = c.at("ssm_y", [P, 16, SEQ], F32, W)
        self.gs = c.at("ssm_gate", [P, DT, SEQ], F32, W + 32 * KB)
        self.mix = c.at("branch_sum", [P, DT, SEQ], F32, W + 80 * KB)
        self.dt = c.at("dt_rows", [P, CH, 32], F32, W + 96 * KB)
        self.da = c.at("da_rows", [P, CH, 32], F32, W + 96 * KB + 512)
        self.state = c.at("ssm_state", [P, 8 * HD], F32, W + 97 * KB)
        self.lh = c.at("lru_h", [P, LRU_T, SEQ], F32R, W)
        self.ll = c.at("lru_l", [P, LRU_T, SEQ], F32R, W + 20 * KB)


def second_head(c, s):
    nc, d = c.nc, c.dram
    W = A_WORK + 32 * KB
    v = c.at("dt_raw", [32, SEQ], F32, W)
    e = c.at("dt_e", [32, SEQ], F32, W + 2 * KB)
    da = c.at("dt_a", [32, SEQ], F32, W + 4 * KB)
    lam = c.at("lam", [P, 2, LRU_T], F32, W + 6 * KB)
    ea = c.at("ea", [32, 1], F32, W + 7 * KB)
    with ExitStack() as ctx:
        ph = Phase(c, ctx, "head", "par_in x_ready v_done abs_done e_done l_done ea_done dtf_done daf_done turned lam_done coef_done rows_done " + NORM_SEMS)
        norm = Norm(ph, c, ph["x_ready"], False, RN1)
        with nc.Block() as block:
            @block.sync
            def _(sp):
                sp.nop().then_inc(ph["x_ready"], DT)
                sp.dma_start(c.par[:, 0:NPAR2], d["pars2"]).then_inc(ph["par_in"], 16)
                ph.load(sp, 0, 0, d["ssm_dt"], D, fresh=True)

            @block.tensor
            def _(pe):
                norm.pe(pe)
                pe.wait_ge(ph["xl_done"], DT)
                ph.products(pe, 0, 0, c.ps[:, 0], c.xh, c.xl, 0, DT, True, True)
                pe.wait_ge(ph["dtf_done"], 1)
                for k in range(CH):
                    pe.transpose(c.ps[:, 1, k * 32:(k + 1) * 32], v[:, k * P:(k + 1) * P], c.k["ident"][0:32, 0:32])
                pe.wait_ge(ph["daf_done"], 1)
                for k in range(CH):
                    t = pe.transpose(c.ps[:, 1, (CH + k) * 32:(CH + k + 1) * 32], da[:, k * P:(k + 1) * P], c.k["ident"][0:32, 0:32])
                t.then_inc(ph["turned"], 1)

            @block.scalar
            def _(act):
                act.wait_ge(ph["par_in"], 16)
                ph.hi(act, 0, 0, D)
                norm.act(act)
                lo, hi = c.par[:, RLAM:RLAM + LRU_T], lam[:, 0]
                act.activation(hi, lo, ACT.Abs).then_inc(ph["lam_done"], 1)
                act.wait_ge(ph["lam_done"], 1)
                act.activation(hi, hi, ACT.Exp, scale=-1.0).then_inc(ph["lam_done"], 1)
                act.wait_ge(ph["lam_done"], 2)
                act.activation(hi, hi, ACT.Ln, bias=1.0).then_inc(ph["lam_done"], 1)
                act.activation(ea[:], c.par[0:32, RALOG:RALOG + 1], ACT.Exp).then_inc(ph["ea_done"], 1)
                act.wait_ge(ph["slot_used"], 1)
                act.activation(v[:], c.ps[0:32, 0], ACT.Identity, bias=c.par[0:32, RDTB:RDTB + 1]).then_inc(ph["v_done"], 1)
                act.wait_ge(ph["v_done"], 1)
                act.activation(e[:], v[:], ACT.Abs).then_inc(ph["abs_done"], 1)
                act.wait_ge(ph["abs_done"], 1)
                act.activation(e[:], e[:], ACT.Exp, scale=-1.0).then_inc(ph["e_done"], 1)
                act.wait_ge(ph["e_done"], 1)
                act.activation(e[:], e[:], ACT.Ln, bias=1.0).then_inc(ph["l_done"], 1)

            @block.vector
            def _(dve):
                dve.wait_ge(ph["par_in"], 16)
                ph.lo(dve, 0, 0, D)
                norm.dve(dve)
                lo, hi = c.par[:, RLAM:RLAM + LRU_T], lam[:, 1]
                dve.wait_ge(ph["lam_done"], 3)
                dve.tensor_scalar(hi, lo, -1.0, 0.0, ALU.mult, ALU.max).then_inc(ph["coef_done"], 1)
                dve.wait_ge(ph["coef_done"], 1)
                dve.tensor_tensor(hi, hi, lam[:, 0], ALU.add).then_inc(ph["coef_done"], 1)
                dve.wait_ge(ph["coef_done"], 2)
                dve.tensor_scalar(lo, hi, -8.0, None, ALU.mult).then_inc(ph["coef_done"], 1)
                dve.wait_ge(ph["l_done"], 1)
                dve.scalar_tensor_tensor(v[:], v[:], 0.0, e[:], ALU.max, ALU.add).then_inc(ph["dtf_done"], 1)
                dve.wait_ge(ph["dtf_done"], 1)
                dve.wait_ge(ph["ea_done"], 1)
                dve.tensor_scalar(da[:], v[:], ea[:, 0:1], -1.0, ALU.mult, ALU.mult).then_inc(ph["daf_done"], 1)
                dve.wait_ge(ph["turned"], 1)
                dve.tensor_copy(s.dt[:], c.ps[:, 1, 0:CH * 32].rearrange("p (c h) -> p c h", h=32)).then_inc(ph["rows_done"], 1)
                dve.tensor_copy(s.da[:], c.ps[:, 1, CH * 32:2 * CH * 32].rearrange("p (c h) -> p c h", h=32)).then_inc(ph["rows_done"], 1)
        ph.end()


def ssm_group(c, s, g):
    nc, d = c.nc, c.dram
    W = A_WORK + 48 * KB
    PADW = SEQ + 4
    up = c.at("conv_in", [P, 6, PADW], F32, W)
    lm = c.at("ssm_m", [P, 8, P], F32, W)
    ce = c.at("ssm_ce", [P, 8, P], F32, W + 4 * KB)
    e2 = c.at("ssm_e2", [P, 8, P], F32, W + 8 * KB)
    xs = c.at("conv_out", [P, 6, SEQ], F32, W + 6 * PADW * 4)
    z = c.at("ssm_z", [P, 4, SEQ], F32, W + 6 * PADW * 4 + 12 * KB)
    o = W + 6 * PADW * 4 + 20 * KB
    xdt = c.at("ssm_xdt", [P, 8 * HD], F32, o)
    xdd = c.at("ssm_xdd", [P, 8 * HD], F32, o + 2 * KB)
    first = c.at("ssm_first", [P, 272], F32, o + 4 * KB)
    cb, bt, cs, tot = first[:, 0:P], first[:, P:2 * P], first[:, 256:264], first[:, 264:272]
    o += 64
    sm = c.at("ssm_small", [P, 4, 8], F32, o + 5 * KB)
    pg = c.at("ssm_par", [P, NPG], F32, o + 5 * KB + 128)
    dag = c.at("ssm_da_g", [P, CH, 8], F32, o + 5 * KB + 384)
    dtg = c.at("ssm_dt_g", [P, CH, 8], F32, o + 5 * KB + 512)
    sq = xs[:, 0:4]
    std, rstd = c.at("ssm_std", [P, SEQ], F32, W), c.at("ssm_rstd", [P, SEQ], F32, W + 2 * KB)
    with ExitStack() as ctx:
        ph = Phase(c, ctx, "ssm", "par_in pad_done evac_done conv_step conv_done silu_done z_done first_done e2_done masked_done cb_done ncs_done dd_done "
                   "dec_done xdt_done xdd_done l_done m_done ce_done y_done s_done yout_done hdec_done state_done gated_done sq_done sum_done "
                   "std_done rstd_done norm_done g_done")
        with nc.Block() as block:
            @block.sync
            def _(sp):
                sp.dma_start(pg[:], d["pars_g"][g]).then_inc(ph["par_in"], 16)
                for k in range(SSM_SLOTS):
                    ph.load(sp, k // 4, k % 4, d["ssm_in"][g, k], D, fresh=k < 4)

            @block.tensor
            def _(pe):
                def project(k):
                    if k >= 2:
                        pe.wait_ge(ph["evac_done"], k - 1)
                    ph.products(pe, k // 4, k % 4, c.ps[:, k % 2], c.xh, c.xl, 0, DT, True, True)

                def chunk_first(k):
                    ch = slice(k * P, (k + 1) * P)
                    pe.matmul(c.ps[:, 2, 0:P], xs[:, 0, ch], xs[:, 1, ch], start=True, stop=True)
                    pe.transpose(c.ps[:, 2, P:2 * P], xs[:, 0, ch], c.k["ident"])
                    pe.matmul(c.ps[:, 2, 256:264], c.k["triu"], dag[:, k], start=True, stop=True)
                    pe.matmul(c.ps[:, 2, 264:272], c.k["ones"], dag[:, k], start=True, stop=True)
                    if k >= 1:
                        pe.wait_ge(ph["xdt_done"], k)
                    for j in range(4):
                        pe.transpose(c.ps[:, 3, j * P:(j + 1) * P], xs[:, 2 + j, ch], c.k["ident"])
                    for h in range(8):
                        mm = pe.matmul(c.ps[:, 4 + h // 4, (h % 4) * P:(h % 4 + 1) * P], dag[:, k, h:h + 1].broadcast_to([P, P]), c.k["triu"],
                                       start=h % 4 == 0, stop=True, skip_group_check=True)
                    mm.then_inc(ph["first_done"], 1)
                    for b in range(2):
                        pe.wait_ge(ph["e2_done"], 2 * k + b + 1)
                        pe.matmul(c.ps[:, 4 + b].rearrange("p (h l) -> p h l", h=4), c.kb["ident"], c.kb["negl"].unsqueeze(1).broadcast_to([P, 4, P]),
                                  start=False, stop=True, skip_group_check=True).then_inc(ph["masked_done"], 1)

                def chunk_second(k):
                    pe.wait_ge(ph["xdd_done"], k + 1)
                    if k >= 1:
                        pe.wait_ge(ph["state_done"], k)
                    pe.wait_ge(ph["cb_done"], k + 1)
                    pe.matmul(c.ps[:, 7], bt, xdd[:], start=True, stop=True).then_inc(ph["s_done"], 1)
                    pe.wait_ge(ph["m_done"], 2 * k + 2)
                    pe.wait_ge(ph["ce_done"], 2 * k + 2)
                    if k == 0:
                        pe.wait_ge(ph["pad_done"], 2)
                    if k >= 1:
                        pe.wait_ge(ph["yout_done"], 4 * k)
                    for h in range(8):
                        lo = 64 * (h % 2)
                        out = c.ps[lo:lo + 64, 6, (h // 2) * P:(h // 2 + 1) * P]
                        pe.matmul(out, xdt[:, h * HD:(h + 1) * HD], lm[:, h], start=True, stop=False)
                        mm = pe.matmul(out, s.state[:, h * HD:(h + 1) * HD], ce[:, h], start=False, stop=True)
                    mm.then_inc(ph["y_done"], 1)

                for k in range(6):
                    project(k)
                pe.wait_ge(ph["silu_done"], 6)
                pe.wait_ge(ph["g_done"], 2)
                for k in range(CH):
                    chunk_first(k)
                    if k < 3:
                        project(6 + 2 * k)
                        project(7 + 2 * k)
                    chunk_second(k)
                for j in range(4):
                    pe.wait_ge(ph["sq_done"], j + 1)
                    mm = pe.matmul(c.ps[:, 3], c.k["ones"], sq[:, j], start=j == 0, stop=j == 3)
                mm.then_inc(ph["sum_done"], 1)

            @block.scalar
            def _(act):
                act.wait_ge(ph["par_in"], 16)
                act.wait_ge(ph["pad_done"], 1)
                ph.hi(act, 0, 0, D)
                ph.hi(act, 0, 1, D)

                def evacuate(k):
                    act.wait_ge(ph["slot_used"], k + 1)
                    src = c.ps[:, k % 2]
                    if k < 6:
                        act.activation(up[:, k, 4:4 + SEQ], src, ACT.Copy).then_inc(ph["evac_done"], 1)
                    elif k < 10:
                        act.activation(z[:, k - 6], src, ACT.Silu).then_inc(ph["evac_done"], 1)
                    else:
                        t = g * 2 + (k - 10)
                        act.activation(s.gs[:, t], src, ACT.Sigmoid, bias=pg[:, GN + 4 + k - 10:GN + 5 + k - 10]).then_inc(ph["evac_done"], 1)
                    if k + 2 < SSM_SLOTS:
                        ph.hi(act, (k + 2) // 4, (k + 2) % 4, D)

                for k in range(6):
                    evacuate(k)
                for k in range(6):
                    act.wait_ge(ph["conv_done"], k + 1)
                    act.activation(xs[:, k], xs[:, k], ACT.Silu).then_inc(ph["silu_done"], 1)
                for k in range(CH):
                    act.wait_ge(ph["first_done"], k + 1)
                    for b in range(2):
                        if k >= 1:
                            act.wait_ge(ph["ce_done"], 2 * k)
                        act.activation(e2[:, 4 * b:4 * b + 4], c.ps[:, 4 + b].rearrange("p (h l) -> p h l", h=4), ACT.Exp).then_inc(ph["e2_done"], 1)
                    if k >= 1:
                        act.wait_ge(ph["y_done"], k)
                        act.wait_ge(ph["s_done"], k)
                        act.wait_ge(ph["state_done"], k)
                    act.activation(first[:], c.ps[:, 2, 0:272], ACT.Copy).then_inc(ph["cb_done"], 1)
                    act.wait_ge(ph["cb_done"], k + 1)
                    act.activation(sm[:, 3], tot, ACT.Exp).then_inc(ph["dec_done"], 1)
                    act.wait_ge(ph["dd_done"], k + 1)
                    act.activation(sm[:, 2], sm[:, 1], ACT.Exp).then_inc(ph["dec_done"], 1)
                    for b in range(2):
                        act.wait_ge(ph["masked_done"], 2 * k + b + 1)
                        for h in range(4 * b, 4 * b + 4):
                            e = act.activation(lm[:, h], c.ps[:, 4 + b, (h % 4) * P:(h % 4 + 1) * P], ACT.Exp, bias=sm[:, 0, h:h + 1])
                        e.then_inc(ph["l_done"], 1)
                    if k < 3:
                        evacuate(6 + 2 * k)
                        evacuate(7 + 2 * k)
                for j in range(4):
                    act.wait_ge(ph["gated_done"], j + 1)
                    act.activation(sq[:, j], s.ys[:, g * 4 + j], ACT.Square).then_inc(ph["sq_done"], 1)
                act.wait_ge(ph["sum_done"], 1)
                act.activation(std[:], c.ps[:, 3], ACT.Sqrt, scale=1.0 / 512, bias=c.eps_rms).then_inc(ph["std_done"], 1)

            @block.vector
            def _(dve):
                dve.memset(up[:, :, 0:4], 0.0).then_inc(ph["pad_done"], 1)
                dve.memset(s.state[:], 0.0).then_inc(ph["pad_done"], 1)
                dve.tensor_copy(dag[:], s.da[:, :, bass.ds(g * 8, 8)]).then_inc(ph["g_done"], 1)
                dve.tensor_copy(dtg[:], s.dt[:, :, bass.ds(g * 8, 8)]).then_inc(ph["g_done"], 1)
                dve.wait_ge(ph["g_done"], 2)
                dve.wait_ge(ph["par_in"], 16)
                ph.lo(dve, 0, 0, D)
                ph.lo(dve, 0, 1, D)
                for k in range(6):
                    dve.wait_ge(ph["evac_done"], k + 1)
                    tap = lambda i: pg[:, GCW + 4 * k + i:GCW + 4 * k + i + 1]
                    dve.tensor_scalar(xs[:, k], up[:, k, 4:4 + SEQ], tap(3), pg[:, GCB + k:GCB + k + 1], ALU.mult, ALU.add).then_inc(ph["conv_step"], 1)
                    for i in range(3):
                        dve.wait_ge(ph["conv_step"], 3 * k + i + 1)
                        dve.scalar_tensor_tensor(xs[:, k], up[:, k, 1 + i:1 + i + SEQ], tap(i), xs[:, k], ALU.mult,
                                                 ALU.add).then_inc(ph["conv_step" if i < 2 else "conv_done"], 1)
                    ph.lo(dve, (k + 2) // 4, (k + 2) % 4, D)

                for k in range(CH):
                    ch = slice(k * P, (k + 1) * P)
                    dve.wait_ge(ph["cb_done"], k + 1)
                    if k >= 1:
                        dve.wait_ge(ph["l_done"], 2 * k)
                    dve.tensor_scalar(sm[:, 0], cs, -1.0, None, ALU.mult).then_inc(ph["ncs_done"], 1)
                    dve.wait_ge(ph["ncs_done"], k + 1)
                    dve.tensor_tensor(sm[:, 1], sm[:, 0], tot, ALU.add).then_inc(ph["dd_done"], 1)
                    if k >= 1:
                        dve.wait_ge(ph["y_done"], k)
                        dve.wait_ge(ph["s_done"], k)
                    heads = "p (h d) -> p h d"
                    dve.tensor_tensor(xdt[:].rearrange(heads, d=HD), c.ps[:, 3].rearrange(heads, d=HD),
                                      dtg[:, k].unsqueeze(2).broadcast_to([P, 8, HD]), ALU.mult).then_inc(ph["xdt_done"], 1)
                    dve.wait_ge(ph["xdt_done"], k + 1)
                    dve.wait_ge(ph["dec_done"], 2 * k + 2)
                    dve.tensor_tensor(xdd[:].rearrange(heads, d=HD), xdt[:].rearrange(heads, d=HD),
                                      sm[:, 2].unsqueeze(2).broadcast_to([P, 8, HD]), ALU.mult).then_inc(ph["xdd_done"], 1)
                    for b in range(2):
                        hs = slice(4 * b, 4 * b + 4)
                        dve.wait_ge(ph["e2_done"], 2 * k + b + 1)
                        dve.tensor_tensor(ce[:, hs], e2[:, hs], xs[:, 1, ch].unsqueeze(1).broadcast_to([P, 4, P]), ALU.mult).then_inc(ph["ce_done"], 1)
                    for b in range(2):
                        hs = slice(4 * b, 4 * b + 4)
                        dve.wait_ge(ph["l_done"], 2 * k + b + 1)
                        dve.tensor_tensor(lm[:, hs], lm[:, hs], cb.unsqueeze(1).broadcast_to([P, 4, P]), ALU.mult).then_inc(ph["m_done"], 1)
                    if k < 3:
                        for j in (8 + 2 * k, 9 + 2 * k):
                            if j < SSM_SLOTS:
                                ph.lo(dve, j // 4, j % 4, D)
                    dve.wait_ge(ph["y_done"], k + 1)
                    for j in range(4):
                        dve.scalar_tensor_tensor(s.ys[:, g * 4 + j, ch], xs[:, 2 + j, ch], pg[:, GD + j:GD + j + 1], c.ps[:, 6, j * P:(j + 1) * P],
                                                 ALU.mult, ALU.add).then_inc(ph["yout_done"], 1)
                    st = s.state[:].rearrange(heads, d=HD)
                    dve.tensor_tensor(st, st, sm[:, 3].unsqueeze(2).broadcast_to([P, 8, HD]), ALU.mult).then_inc(ph["hdec_done"], 1)
                    dve.wait_ge(ph["hdec_done"], k + 1)
                    dve.wait_ge(ph["s_done"], k + 1)
                    dve.tensor_tensor(s.state[:], s.state[:], c.ps[:, 7], ALU.add).then_inc(ph["state_done"], 1)
                dve.wait_ge(ph["yout_done"], 4 * CH)
                dve.wait_ge(ph["evac_done"], 10)
                for j in range(4):
                    y = s.ys[:, g * 4 + j]
                    dve.tensor_tensor(y, y, z[:, j], ALU.mult).then_inc(ph["gated_done"], 1)
                dve.wait_ge(ph["std_done"], 1)
                dve.reciprocal(rstd[:], std[:]).then_inc(ph["rstd_done"], 1)
                dve.wait_ge(ph["rstd_done"], 1)
                dve.wait_ge(ph["gated_done"], 4)
                for j in range(4):
                    y = s.ys[:, g * 4 + j]
                    dve.scalar_tensor_tensor(y, y, pg[:, GN + j:GN + j + 1], rstd[:], ALU.mult, ALU.mult).then_inc(ph["norm_done"], 1)
        ph.end()


def ssm_output(c, s):
    nc, d = c.nc, c.dram
    yh = c.at("ssm_yh", [P, 16, SEQ], F32R, A_WORK + 48 * KB)
    yl = c.at("ssm_yl", [P, 16, SEQ], F32R, A_WORK)
    with ExitStack() as ctx:
        ph = Phase(c, ctx, "sout", "yh_done yl_done bank_free")
        with nc.Block() as block:
            @block.sync
            def _(sp):
                for u in range(4):
                    ph.load(sp, 0, u, d["ssm_out"][u], D, fresh=True)
                with sp.Fori(1, 4) as q:
                    for u in range(4):
                        ph.load(sp, q, u, d["ssm_out"][4 * q + u], D)

            @block.tensor
            def _(pe):
                pe.wait_ge(ph["yl_done"], 16)
                with pe.Fori(0, 4) as q:
                    for u in range(4):
                        if u % 2 == 0:
                            pe.wait_ge(ph["bank_free"], 2 * q + u // 2 + 1)
                        ph.products(pe, q, u, c.ps[:, u // 2], yh, yl, 8 * (u % 2), 8, u % 2 == 0, u % 2 == 1)

            @block.scalar
            def _(act):
                ph.hi(act, 0, 0, D)
                ph.hi(act, 0, 1, D)
                for t in range(16):
                    act.activation(yh[:, t], s.ys[:, t], ACT.Copy).then_inc(ph["yh_done"], 1)

                def four(q, last=False):
                    for u in range(4):
                        if not (last and u >= 2):
                            act.wait_ge(ph["slot_used"], 4 * q + u + 1)
                            ph.hi(act, q + (u + 2) // 4, (u + 2) % 4, D)
                with act.Fori(0, 3) as q:
                    four(q)
                four(3, last=True)

            @block.vector
            def _(dve):
                ph.lo(dve, 0, 0, D)
                ph.lo(dve, 0, 1, D)
                for t in range(16):
                    dve.wait_ge(ph["yh_done"], t + 1)
                    dve.tensor_tensor(yl[:, t], s.ys[:, t], yh[:, t].bitcast(F32), ALU.subtract).then_inc(ph["yl_done"], 1)
                dve.nop().then_inc(ph["bank_free"], 2)

                def four(q, last=False):
                    for u in range(4):
                        if not (last and u >= 2):
                            ph.lo(dve, q + (u + 2) // 4, (u + 2) % 4, D)
                        if u % 2 == 1:
                            t = 2 * q + u // 2
                            dve.wait_ge(ph["slot_used"], 4 * q + u + 1)
                            dve.tensor_tensor(s.mix[:, t], s.gs[:, t], c.ps[:, u // 2], ALU.mult).then_inc(ph["bank_free"], 1)
                with dve.Fori(0, 3) as q:
                    four(q)
                four(3, last=True)
        ph.end()


def lru(c, s):
    nc, d = c.nc, c.dram
    W = A_WORK + 40 * KB
    PADW = SEQ + 4
    STEPS = LRU_T // 2
    names = "u r i a b gel".split()
    up = c.at("lru_pad", [P, 2, PADW], F32, W)
    B = {n: c.at("lru_" + n + "_t", [P, 2, SEQ], F32, W + 2 * PADW * 4 + 4 * KB * k) for k, n in enumerate(names)}
    wri = c.at("lru_w", [P, 2, 2, P], F32, W + 2 * PADW * 4 + 24 * KB)
    cols = c.at("lru_cols", [P, 2, 8], F32, W + 2 * PADW * 4 + 26 * KB)
    with ExitStack() as ctx:
        ph = Phase(c, ctx, "lru", "pad_done w_in0 w_in1 cols_in0 cols_in1 evac_done conv_step conv_done ri_done rsig_done isig_done tanh_done a_done "
                   "den_done rden_done b2_done sqrt_done iu_done b_done scan_done gel_done out_done lh_done ll_done")
        with nc.Block() as block:
            @block.sync
            def _(sp):
                def four(q, fresh=False):
                    for u in range(4):
                        ph.load(sp, q, u, d["lru_in"][4 * q + u], D, fresh)
                    for v in range(2):
                        if not fresh:
                            sp.wait_ge(ph["isig_done"], 2 * q)
                        sp.dma_start(wri[:, v], d["lru_ri"][2 * q + v].rearrange("p (a n) -> p a n", a=2)).then_inc(ph[f"w_in{v}"], 16)
                        sp.dma_start(cols[:, v], d["lru_cols"][2 * q + v]).then_inc(ph[f"cols_in{v}"], 16)
                four(0, fresh=True)
                with sp.Fori(1, STEPS) as q:
                    four(q)

            @block.tensor
            def _(pe):
                def gates(q, v):
                    pe.wait_ge(ph["conv_done"], 2 * q + v + 1)
                    pe.wait_ge(ph[f"w_in{v}"], 16 * q + 16)
                    for a in range(2):
                        if not isinstance(q, int):
                            pe.wait_ge(ph["isig_done" if a else "rsig_done"], 2 * q + v - 1)
                        pe.matmul(c.ps[:, 4 + 2 * a + v], wri[:, v, a], B["u"][:, v], start=True, stop=True).then_inc(ph["ri_done"], 1)

                def step(q):
                    for u in range(4):
                        if not isinstance(q, int):
                            pe.wait_ge(ph["gel_done" if u % 2 else "evac_done"], 2 * q + u // 2 - 1)
                        ph.products(pe, q, u, c.ps[:, u], c.xh, c.xl, 0, DT, True, True)
                        if u == 2:
                            gates(q, 0)
                    gates(q, 1)
                step(0)
                with pe.Fori(1, STEPS) as q:
                    step(q)

            @block.scalar
            def _(act):
                ph.hi(act, 0, 0, D)
                ph.hi(act, 0, 1, D)
                act.wait_ge(ph["pad_done"], 1)

                def step(q, front=True, tail=True, last=False):
                    def project(u):
                        if front:
                            act.wait_ge(ph["slot_used"], 4 * q + u + 1)
                            if u % 2 == 0:
                                act.activation(up[:, u // 2, 4:4 + SEQ], c.ps[:, u], ACT.Copy).then_inc(ph["evac_done"], 1)
                            if not (last and u >= 2):
                                ph.hi(act, q + (u + 2) // 4, (u + 2) % 4, D)

                    if tail:
                        for v in range(2):
                            act.wait_ge(ph["rsig_done"], 2 * q + v - 1)
                            act.activation(B["b"][:, v], B["r"][:, v], ACT.Tanh, scale=c.par[:, bass.ds(RLAM + 2 * q - 2 + v, 1)]).then_inc(ph["tanh_done"], 1)
                        for v in range(2):
                            act.activation(B["a"][:, v], B["r"][:, v], ACT.Exp, scale=c.par[:, bass.ds(RLAM + 2 * q - 2 + v, 1)]).then_inc(ph["a_done"], 1)
                        for v in range(2):
                            act.wait_ge(ph["tanh_done"], 2 * q + v - 1)
                            act.wait_ge(ph["a_done"], 2 * q + v - 1)
                            act.activation(B["r"][:, v], B["b"][:, v], ACT.Identity, scale=-1.0, bias=c.k["ones"][:, 0:1]).then_inc(ph["den_done"], 1)
                    project(0)
                    project(1)
                    project(2)
                    if tail:
                        for v in range(2):
                            act.wait_ge(ph["b2_done"], 2 * q + v - 1)
                            act.activation(B["b"][:, v], B["b"][:, v], ACT.Sqrt).then_inc(ph["sqrt_done"], 1)
                    project(3)
                    if tail:
                        for v in range(2):
                            act.wait_ge(ph["out_done"], 2 * q + v - 1)
                            act.activation(s.lh[:, 2 * q - 2 + v], B["gel"][:, v], ACT.Copy).then_inc(ph["lh_done"], 1)
                    if front:
                        for v in range(2):
                            if tail:
                                act.wait_ge(ph["ll_done"], 2 * q + v - 1)
                            act.activation(B["gel"][:, v], c.ps[:, 2 * v + 1], ACT.Gelu_apprx_tanh).then_inc(ph["gel_done"], 1)
                        for v in range(2):
                            act.wait_ge(ph[f"cols_in{v}"], 16 * q + 16)
                            act.wait_ge(ph["ri_done"], 4 * q + 2 * v + 2)
                            act.activation(B["r"][:, v], c.ps[:, 4 + v], ACT.Sigmoid, bias=cols[:, v, 5:6]).then_inc(ph["rsig_done"], 1)
                            act.activation(B["i"][:, v], c.ps[:, 6 + v], ACT.Sigmoid, bias=cols[:, v, 6:7]).then_inc(ph["isig_done"], 1)
                step(0, tail=False)
                with act.Fori(1, STEPS - 1) as q:
                    step(q)
                step(STEPS - 1, last=True)
                step(STEPS, front=False)

            @block.vector
            def _(dve):
                dve.memset(up[:, :, 0:4], 0.0).then_inc(ph["pad_done"], 1)
                ph.lo(dve, 0, 0, D)
                ph.lo(dve, 0, 1, D)

                def step(q, front=True, tail=True, last=False):
                    def low(u):
                        if front and not (last and u >= 4):
                            ph.lo(dve, q + u // 4, u % 4, D)

                    def conv(v):
                        if not front:
                            return
                        tap = lambda i: cols[:, v, i:i + 1]
                        dve.wait_ge(ph[f"cols_in{v}"], 16 * q + 16)
                        dve.wait_ge(ph["evac_done"], 2 * q + v + 1)
                        dve.tensor_scalar(B["u"][:, v], up[:, v, 4:4 + SEQ], tap(3), tap(4), ALU.mult, ALU.add).then_inc(ph["conv_step"], 1)
                        for i in range(3):
                            dve.wait_ge(ph["conv_step"], 6 * q + 3 * v + i + 1)
                            dve.scalar_tensor_tensor(B["u"][:, v], up[:, v, 1 + i:1 + i + SEQ], tap(i), B["u"][:, v], ALU.mult,
                                                     ALU.add).then_inc(ph["conv_step" if i < 2 else "conv_done"], 1)

                    def decay(v):
                        if not tail:
                            return
                        n = 2 * q + v - 1
                        t, r = B["b"][:, v], B["r"][:, v]
                        dve.wait_ge(ph["den_done"], n)
                        dve.reciprocal(r, r).then_inc(ph["rden_done"], 1)
                        dve.wait_ge(ph["rden_done"], n)
                        dve.scalar_tensor_tensor(t, t, -2.0, r, ALU.mult, ALU.mult).then_inc(ph["b2_done"], 1)

                    def scan(v):
                        if not tail:
                            return
                        n = 2 * q + v - 1
                        dve.wait_ge(ph["sqrt_done"], n)
                        dve.tensor_tensor(B["b"][:, v], B["b"][:, v], B["i"][:, v], ALU.mult).then_inc(ph["b_done"], 1)
                        dve.wait_ge(ph["b_done"], n)
                        dve.tensor_tensor_scan(B["i"][:, v], B["a"][:, v], B["b"][:, v], 0.0, ALU.mult, ALU.add).then_inc(ph["scan_done"], 1)
                        dve.wait_ge(ph["scan_done"], n)
                        dve.tensor_tensor(B["gel"][:, v], B["gel"][:, v], B["i"][:, v], ALU.mult).then_inc(ph["out_done"], 1)

                    conv(0)
                    low(2)
                    decay(0)
                    low(3)
                    decay(1)
                    conv(1)
                    low(4)
                    scan(0)
                    low(5)
                    scan(1)
                    if tail:
                        for v in range(2):
                            n = 2 * q + v - 1
                            dve.wait_ge(ph["lh_done"], n)
                            dve.tensor_tensor(s.ll[:, 2 * q - 2 + v], B["gel"][:, v], s.lh[:, 2 * q - 2 + v].bitcast(F32), ALU.subtract).then_inc(ph["ll_done"], 1)
                    if front:
                        for v in range(2):
                            dve.wait_ge(ph["isig_done"], 2 * q + v + 1)
                            dve.tensor_tensor(B["i"][:, v], B["i"][:, v], B["u"][:, v], ALU.mult).then_inc(ph["iu_done"], 1)
                            dve.wait_ge(ph["iu_done"], 2 * q + v + 1)
                step(0, tail=False)
                with dve.Fori(1, STEPS - 1) as q:
                    step(q)
                step(STEPS - 1, last=True)
                step(STEPS, front=False)
        ph.end()


def lru_output(c, s):
    nc, d = c.nc, c.dram
    gate = c.at("lout_gate", [P, 2, SEQ], F32, A_WORK + 44 * KB)
    LW = LRU_T * P
    with ExitStack() as ctx:
        ph = Phase(c, ctx, "lout", "gate_done gated_done bank_free sum_done")
        with nc.Block() as block:
            @block.sync
            def _(sp):
                def four(q, fresh=False):
                    for v in range(2):
                        ph.load(sp, q, 2 * v, d["lru_gate"][2 * q + v], D, fresh)
                        ph.load(sp, q, 2 * v + 1, d["lru_out"][2 * q + v], LW, fresh)
                four(0, fresh=True)
                with sp.Fori(1, 4) as q:
                    four(q)

            @block.tensor
            def _(pe):
                with pe.Fori(0, 4) as q:
                    for v in range(2):
                        pe.wait_ge(ph["bank_free"], 2 * q + v + 1)
                        ph.products(pe, q, 2 * v, c.ps[:, 2 * v], c.xh, c.xl, 0, DT, True, True)
                        ph.products(pe, q, 2 * v + 1, c.ps[:, 2 * v + 1], s.lh, s.ll, 0, LRU_T, True, True)

            @block.scalar
            def _(act):
                ph.hi(act, 0, 0, D)
                ph.hi(act, 0, 1, LW)

                def four(q, last=False):
                    for u in range(4):
                        act.wait_ge(ph["slot_used"], 4 * q + u + 1)
                        if u % 2 == 0:
                            v = u // 2
                            act.activation(gate[:, v], c.ps[:, u], ACT.Sigmoid, bias=c.par[:, bass.ds(RBG + 8 + 2 * q + v, 1)]).then_inc(ph["gate_done"], 1)
                        if not (last and u >= 2):
                            ph.hi(act, q + (u + 2) // 4, (u + 2) % 4, LW if u % 2 else D)
                with act.Fori(0, 3) as q:
                    four(q)
                four(3, last=True)

            @block.vector
            def _(dve):
                dve.nop().then_inc(ph["bank_free"], 2)
                ph.lo(dve, 0, 0, D)
                ph.lo(dve, 0, 1, LW)

                def four(q, last=False):
                    for u in range(4):
                        if not (last and u >= 2):
                            ph.lo(dve, q + (u + 2) // 4, (u + 2) % 4, LW if u % 2 else D)
                        if u % 2 == 1:
                            v = u // 2
                            t = 2 * q + v
                            dve.wait_ge(ph["slot_used"], 4 * q + u + 1)
                            dve.wait_ge(ph["gate_done"], t + 1)
                            dve.tensor_tensor(gate[:, v], gate[:, v], c.ps[:, u], ALU.mult).then_inc(ph["gated_done"], 1)
                            dve.wait_ge(ph["gated_done"], t + 1)
                            dve.tensor_tensor(s.mix[:, t], s.mix[:, t], gate[:, v], ALU.add).then_inc(ph["bank_free"], 1)
                with dve.Fori(0, 3) as q:
                    four(q)
                four(3, last=True)
        ph.end()


def second_output(c, s):
    nc, d = c.nc, c.dram
    with ExitStack() as ctx:
        ph = Phase(c, ctx, "bout", "mh_done ml_done res_done " + NORM_SEMS)
        norm = Norm(ph, c, ph["res_done"], False, RN2)
        with nc.Block() as block:
            @block.sync
            def _(sp):
                for t in range(DT):
                    ph.load(sp, t // 4, t % 4, d["b2_out"][t], D, fresh=t < 4)

            @block.tensor
            def _(pe):
                pe.wait_ge(ph["ml_done"], DT)
                for t in range(DT):
                    if t >= 2:
                        pe.wait_ge(ph["res_done"], t - 1)
                    ph.products(pe, t // 4, t % 4, c.ps[:, t % 2], c.xh, c.xl, 0, DT, True, True)
                norm.pe(pe)

            @block.scalar
            def _(act):
                ph.hi(act, 0, 0, D)
                ph.hi(act, 0, 1, D)
                for t in range(DT):
                    act.activation(c.xh[:, t], s.mix[:, t], ACT.Copy).then_inc(ph["mh_done"], 1)
                for t in range(DT - 2):
                    act.wait_ge(ph["slot_used"], t + 1)
                    ph.hi(act, (t + 2) // 4, (t + 2) % 4, D)
                act.wait_ge(ph["slot_used"], DT)
                norm.act(act)

            @block.vector
            def _(dve):
                ph.lo(dve, 0, 0, D)
                ph.lo(dve, 0, 1, D)
                for t in range(DT):
                    dve.wait_ge(ph["mh_done"], t + 1)
                    dve.tensor_tensor(c.xl[:, t], s.mix[:, t], c.xh[:, t].bitcast(F32), ALU.subtract).then_inc(ph["ml_done"], 1)
                for t in range(DT):
                    if t < DT - 2:
                        ph.lo(dve, (t + 2) // 4, (t + 2) % 4, D)
                    dve.wait_ge(ph["slot_used"], t + 1)
                    dve.tensor_tensor(c.x[:, t], c.x[:, t], c.ps[:, t % 2], ALU.add).then_inc(ph["res_done"], 1)
                norm.dve(dve)
        ph.end()


def program(nc, dram, outT):
    with ExitStack() as ctx:
        c = Core(nc, ctx, dram, outT)
        m = Mixer(c)
        setup_phase(c)
        with nc.Fori(0, DEPTH) as l:
            ffn_phase(c, "ffn1", l * 2, PG1, PB1, ALPHA, 0.5, True, par_src=dram["pars"][l])
            mixer(c, m, l)
            ffn_phase(c, "ffn2", l * 2 + 1, PG3, PB3, ALPHA, 0.5, True, par_src=dram["pars"][l])
        s = Second(c)
        second_head(c, s)
        with nc.Fori(0, SSM_G) as g:
            ssm_group(c, s, g)
        ssm_output(c, s)
        lru(c, s)
        lru_output(c, s)
        second_output(c, s)
        ffn_phase(c, "ffn3", 4, RNF, None, 1.0, 1.0, False, final=True, par_src=dram["pars2"])


def kernel(**inputs):
    import concourse.bacc as bacc
    from concourse.bass_utils import run_bass_kernel_spmd

    arrays = layout(inputs)
    nc = bacc.Bacc("TRN2", target_bir_lowering=False, num_devices=1)
    dram = {n: nc.dram_tensor("in_" + n, list(arrays[n].shape), F32, kind="ExternalInput").ap() for n in SHAPES}
    outT = nc.dram_tensor("outT", [D, SEQ], F32, kind="ExternalOutput").ap()
    program(nc, dram, outT)
    r = run_bass_kernel_spmd(nc, [{"in_" + n: arrays[n] for n in SHAPES}], core_ids=[0])
    return np.ascontiguousarray(r.results[0]["outT"].T).reshape(1, SEQ, D)
```

```python
from contextlib import ExitStack

import numpy as np

import concourse.bass as bass
from concourse import mybir

F32 = mybir.dt.float32
F32R = mybir.dt.float32r
BF16 = mybir.dt.bfloat16
ALU = mybir.AluOpType
ACT = mybir.ActivationFunctionType
AXX = mybir.AxisListType.X

P = 128
SEQ = 512
D = 1024
DT = D // P
FF = 2816
FT = FF // P
DEPTH = 2
ALPHA = (2.0 * DEPTH) ** 0.25
LN_EPS = 1e-5
RMS_EPS = 1e-6
NEG = -1e30
TAKEN = -3e38
HD = 64
HEADS = 4
QB = SEQ // P
TOPK = min(256, SEQ // 4)
NCMP = (SEQ - 32) // 16 + 1
IDXH = 8

RAW = 4
HALF = 2
SLOT = 11 * P

CQ, CKV, KROPE, NSAQ, KCMP, VCMP, KSLC, KWIN, DSAQ, DSAK, IDXQ, IDXK, SBQ, SBK = 0, 2, 3, 4, 6, 7, 8, 9, 10, 12, 13, 15, 16, 18
HT = 20
VSLC, VWIN, GATE, DSAV, IDXW, SBV = 0, 64, 128, 140, 204, 212
TW = 468

KB = 1024
A_X, A_XH, A_XL, A_RAW, A_WHI, A_WLO = 0, 16 * KB, 32 * KB, 48 * KB, 48 * KB + RAW * SLOT * 4, 48 * KB + (RAW + HALF) * SLOT * 4
A_CONST = A_RAW + (RAW + 2 * HALF) * SLOT * 4
CONST_NAMES = ["ident", "negd", "negs", "cmpm", "negl", "strict", "ntri", "nones", "ones", "sw64", "sw32", "triu"]
N_BF16 = 5
NCONST = len(CONST_NAMES) * P + 4 * SEQ + 8
A_PAR = A_CONST + NCONST * 4
PG1, PB1, PG2, PB2, PG3, PB3, PQN, PKVN, PGN, PPOS = 0, 8, 16, 24, 32, 40, 48, 50, 51, 59
NPAR = 75
RN1, RN2, RNF, RBG, RLAM, RDTB, RALOG = 0, 8, 16, 24, 40, 50, 51
NPAR2 = 52
GCW, GCB, GD, GN = 0, 24, 30, 34
NPG = 40
A_KB = A_PAR + 128 * 4
A_WORK = A_KB + N_BF16 * P * 2


def tiles_of(w):
    k, m = w.shape
    return w.reshape(k // P, P, m).transpose(1, 0, 2).reshape(P, -1)


def columns_of(v):
    return v.reshape(-1, P).T


def constants():
    i = np.arange(P)
    k, q = i[:, None], i[None, :]
    c = {}
    c["ident"] = (k == q) * 1.0
    c["negd"] = (q > k) * NEG
    c["strict"] = (k < q) * 1.0
    c["negs"] = (k >= q) * NEG
    c["ntri"] = (k >= q) * -1.0
    c["nones"] = -np.ones((P, P))
    c["ones"] = np.ones((P, P))
    c["sw64"] = ((k // 64 == q // 64) & ((k % 64 + 32) % 64 == q % 64)) * 1.0
    c["sw32"] = ((k // 32 == q // 32) & ((k % 32 + 16) % 32 == q % 32)) * 1.0
    n = np.arange(NCMP)
    m = np.zeros((P, P))
    for b in range(QB):
        m[:, b * NCMP:(b + 1) * NCMP] = (n[None, :] * 16 + 31 > (i + b * P)[:, None]) * NEG
    c["cmpm"] = m
    c["triu"] = (k <= q) * 1.0
    c["negl"] = (k > q) * NEG
    cols = [c[x].astype(np.float32) for x in CONST_NAMES]
    for dim in (64, 32):
        half = dim // 2
        inv = (np.float32(10000.0) ** (-np.arange(0, dim, 2, dtype=np.float32) / np.float32(dim))).astype(np.float32)
        ang = np.arange(SEQ, dtype=np.float32)[:, None] * inv[None, :]
        cos, sin = np.cos(ang).astype(np.float32).T, np.sin(ang).astype(np.float32).T
        reps = P // dim
        cols.append(np.tile(np.concatenate([cos, cos]), (reps, 1)))
        cols.append(np.tile(np.concatenate([-sin, sin]), (reps, 1)))
    eps = np.zeros((P, 8), np.float32)
    eps[:, 0], eps[:, 1] = LN_EPS, RMS_EPS
    cols.append(eps)
    return np.ascontiguousarray(np.concatenate(cols, axis=1))


def mixer_columns():
    widths = [256, 128, 32, 256, 64, 64, 64, 64, 64, 64, 12, 256, 64, 64, 256, 32, 8, 256, 256, 256]
    names = "cq ckv krope nq kc vc ks vs kw vw gate dq dk dv iq ik iw sq sk sv".split()
    at, off = {}, 0
    for n, w in zip(names, widths):
        at[n] = np.arange(off, off + w)
        off += w
    feat = [at["cq"], at["ckv"], *[at["krope"]] * 4, at["nq"]]
    for n in ("kc", "vc", "ks", "kw"):
        feat += [at[n]] * 2
    feat += [at["dq"], at["dk"], at["dk"], at["iq"], *[at["ik"]] * 4, at["sq"], at["sk"]]
    tok = [at[n] for n in ("vs", "vw", "gate", "dv", "iw", "sv")]
    return np.concatenate(feat), np.concatenate(tok)


def layout(a):
    a = {k: np.asarray(v) for k, v in a.items()}
    out = {"xT": np.ascontiguousarray(a["x"][0].T.reshape(DT, P, SEQ).transpose(1, 0, 2).reshape(P, -1))}
    out["consts"] = constants()
    ups, downs = [], []

    def ffn(w1, w3, w2):
        up = []
        for t in range(FT):
            up += [tiles_of(w1[:, t * P:(t + 1) * P]), tiles_of(w3[:, t * P:(t + 1) * P])]
        ups.append(np.stack(up))
        down = []
        for d in range(DT):
            w = w2[:, d * P:(d + 1) * P]
            down += [tiles_of(w[:11 * P]), tiles_of(w[11 * P:])]
        downs.append(np.stack(down))

    for l in range(DEPTH):
        ffn(a["ffn1_w1"][l], a["ffn1_w3"][l], a["ffn1_w2"][l])
        ffn(a["ffn2_w1"][l], a["ffn2_w3"][l], a["ffn2_w2"][l])
    wf = a["w_ffn_in_2"][0]
    ffn(wf[:, :FF], wf[:, FF:], a["w_ffn_out_2"][0])
    out["ffn_up"], out["ffn_down"] = np.stack(ups), np.stack(downs)

    def outs(w):
        return [tiles_of(w[:, d * P:(d + 1) * P]) for d in range(w.shape[1] // P)]

    feat, tok = mixer_columns()
    out["mix_in"] = np.stack([np.stack(outs(a["w_in"][l][:, feat])) for l in range(DEPTH)])
    out["mix_tok"] = np.stack([tiles_of(a["w_in"][l][:, tok]) for l in range(DEPTH)])
    out["mix_out"] = np.stack([np.stack(outs(a["w_out"][l])) for l in range(DEPTH)])
    out["mla_uq"] = np.stack([tiles_of(a["mla_w_uq"][l]) for l in range(DEPTH)])
    ukv = a["mla_w_ukv"].reshape(DEPTH, P, HEADS, 2, 64).transpose(0, 1, 3, 2, 4)
    out["mla_ukv"] = np.ascontiguousarray(ukv.reshape(DEPTH, P, 512))

    def cmp1(w):
        return w.reshape(2, 16, 64, 64).transpose(0, 2, 1, 3).reshape(P, 1024)

    out["cmp1"] = np.stack([np.concatenate([cmp1(a["nsa_cmp_wk1"][l]), cmp1(a["nsa_cmp_wv1"][l])], 1) for l in range(DEPTH)])
    out["cmp2"] = np.concatenate([a["nsa_cmp_wk2"], a["nsa_cmp_wk2"], a["nsa_cmp_wv2"]], 2)
    pars = []
    for l in range(DEPTH):
        c = [columns_of(a[n][l]) for n in ("ln1_g", "ln1_b", "ln2_g", "ln2_b", "ln3_g", "ln3_b", "mla_q_norm", "mla_kv_norm", "group_norm_g")]
        pos = a["nsa_cmp_pos"][l]
        c.append(np.concatenate([pos[:16].T, pos[16:].T]))
        pars.append(np.concatenate(c, 1))
    out["pars"] = np.stack(pars)
    w = a["w_in_2"][0]
    zo, xo, bo, co, to, lo, yo = 2048, 4096, 6144, 6656, 7168, 7200, 8480

    def tl(n):
        return tiles_of(w[:, n:n + P])

    out["w_dt"] = tiles_of(w[:, to:to + 32])
    groups, pars_g = [], []
    cw, cbias = a["ssm_conv_w_2"][0], a["ssm_conv_b_2"][0]
    for g in range(4):
        conv = [bo + g * P, co + g * P] + [xo + (4 * g + j) * P for j in range(4)]
        rest = [zo + (4 * g + j) * P for j in range(4)] + [(2 * g + j) * P for j in range(2)]
        groups.append(np.stack([tl(n) for n in conv + rest]))
        cols = [cw[:, n - xo:n - xo + P].T for n in conv]
        cols += [cbias[n - xo:n - xo + P, None] for n in conv]
        cols += [np.repeat(a["ssm_d_2"][0, 8 * g + 2 * j:8 * g + 2 * j + 2], HD)[:, None] for j in range(4)]
        cols += [a["ssm_norm_w_2"][0, (4 * g + j) * P:(4 * g + j + 1) * P, None] for j in range(4)]
        cols += [a["b_branch_gate_2"][0, (2 * g + j) * P:(2 * g + j + 1) * P, None] for j in range(2)]
        pars_g.append(np.concatenate(cols, 1))
    out["ssm_in"], out["pars_g"] = np.stack(groups), np.stack(pars_g)
    wo = a["w_out_ssm_2"][0]
    out["ssm_out"] = np.stack([tiles_of(wo[hf * D:(hf + 1) * D, t * P:(t + 1) * P]) for t in range(DT) for hf in range(2)])
    out["lru_in"] = np.stack([tl(n + t * P) for t in range(10) for n in (lo, yo)])
    out["lru_ri"] = np.concatenate([a["lru_w_r_2"][0], a["lru_w_i_2"][0]], 2)
    cols = [a["lru_conv_w_2"][0], a["lru_conv_b_2"], a["lru_b_r_2"], a["lru_b_i_2"], np.zeros((1, 1280), np.float32)]
    out["lru_cols"] = np.concatenate(cols, 0).reshape(8, 10, P).transpose(1, 2, 0)
    out["lru_gate"] = np.stack([tl(D + t * P) for t in range(DT)])
    out["lru_out"] = np.stack(outs(a["w_out_lru_2"][0]))
    out["b2_out"] = np.stack(outs(a["w_out_2"][0]))
    out["after_layer"] = np.stack([out["ffn_up"][2 * l, :4] for l in range(1, DEPTH)] + [out["ssm_in"][0, :4]])
    out["after_ssm"] = np.stack([out["ssm_in"][2, :4], out["ssm_out"][:4]])
    p2 = np.zeros((P, NPAR2), np.float32)
    for at, v in ((RN1, a["norm1_w_2"][0]), (RN2, a["norm2_w_2"][0]), (RNF, a["norm_f_w_2"]), (RBG, a["b_branch_gate_2"][0]), (RLAM, a["lru_lambda_2"][0])):
        p2[:, at:at + v.size // P] = columns_of(v)
    p2[0:32, RDTB], p2[0:32, RALOG] = a["ssm_dt_bias_2"][0], a["ssm_a_log_2"][0]
    out["pars2"] = p2
    return {k: np.ascontiguousarray(v) for k, v in out.items()}


SHAPES = {
    "xT": [P, DT * SEQ], "consts": [P, NCONST], "ffn_up": [5, 2 * FT, P, D], "ffn_down": [5, 2 * DT, P, SLOT],
    "mix_in": [DEPTH, HT, P, D], "mix_tok": [DEPTH, P, DT * TW], "mix_out": [DEPTH, DT, P, D],
    "mla_uq": [DEPTH, P, 768], "mla_ukv": [DEPTH, P, 512], "cmp1": [DEPTH, P, 2048], "cmp2": [DEPTH, 64, 192],
    "pars": [DEPTH, P, NPAR], "w_dt": [P, DT * 32], "after_layer": [DEPTH, 4, P, D], "after_ssm": [2, 4, P, D], "ssm_in": [4, 12, P, D], "pars_g": [4, P, NPG], "ssm_out": [16, P, D],
    "lru_in": [20, P, D], "lru_ri": [10, P, 2 * P], "lru_cols": [10, P, 8], "lru_gate": [DT, P, D], "lru_out": [DT, P, 10 * P],
    "b2_out": [DT, P, D], "pars2": [P, NPAR2],
}


class Core:

    def __init__(self, nc, ctx, dram, outT):
        self.nc, self.dram, self.outT = nc, dram, outT
        arena = ctx.enter_context(nc.sbuf_tensor("arena", [P, 212 * 1000 // 4], F32))
        self.base = 16512
        self.n = 0
        self.x = self.at("x", [P, DT, SEQ], F32, A_X)
        self.xh = self.at("xh", [P, DT, SEQ], F32R, A_XH)
        self.xl = self.at("xl", [P, DT, SEQ], F32R, A_XL)
        self.raw = self.at("raw", [P, RAW, SLOT], F32, A_RAW)
        self.whi = self.at("whi", [P, HALF, SLOT], F32R, A_WHI)
        self.wlo = self.at("wlo", [P, HALF, SLOT], F32R, A_WLO)
        self.consts = self.at("consts_sb", [P, NCONST], F32, A_CONST)
        self.par = self.at("par", [P, P], F32, A_PAR)
        self.k = {name: self.consts[:, n * P:(n + 1) * P] for n, name in enumerate(CONST_NAMES)}
        self.kb_all = self.at("consts_bf16", [P, N_BF16 * P], BF16, A_KB)
        self.kb = {name: self.kb_all[:, n * P:(n + 1) * P] for n, name in enumerate(CONST_NAMES[:N_BF16])}
        self.rstd = self.at("rstd", [P, SEQ], F32, A_WORK + 96 * KB)
        self.sides = [self.side(ctx, name) for name in "ab"]
        r = len(CONST_NAMES) * P
        self.cos64, self.sin64, self.cos32, self.sin32 = (self.consts[:, r + n * SEQ:r + (n + 1) * SEQ] for n in range(4))
        self.eps_ln, self.eps_rms = self.consts[:, NCONST - 8:NCONST - 7], self.consts[:, NCONST - 7:NCONST - 6]
        self.ps = ctx.enter_context(nc.psum_tensor("ps", [P, 8, SEQ], F32))

    def side(self, ctx, name):
        names = [f"raw_in{u}" for u in range(RAW)] + ["hi_done", "lo_done", "slot_used"]
        return {n: ctx.enter_context(self.nc.semaphore(f"ring_{name}_{n}")) for n in names}

    def at(self, name, shape, dtype, offset):
        return self.nc.alloc_sbuf_tensor_at(name, shape, dtype, offset=self.base + offset)


class Phase:

    def __init__(self, core, ctx, name, sems, side=None, slots=0, following=None):
        self.core, self.nc, self.name, self.slots, self.following = core, core.nc, name, slots, following
        self.handles, self.sems = [], {}
        for n in sems.split():
            h = ctx.enter_context(core.nc.semaphore(f"{name}_{n}"))
            self.handles.append(h)
            self.sems[n] = h
        if side is not None:
            self.sems.update(core.sides[side])
            self.handles += core.sides[side].values()
        self.next = core.sides[0 if side is None else 1 - side]

    def __getitem__(self, name):
        return self.sems[name]

    def end(self):
        nums = sorted(h.num for h in self.handles)
        starts = [n for n in nums if n - 1 not in nums]
        for n in starts:
            self.nc.all_engine_barrier(sems_to_clear=range(n, next(k for k in range(n, n + 200) if k not in nums)))

    def load(self, sp, q, u, src, width):
        sp.wait_ge(self["lo_done"], 4 * q + u - (RAW - 1))
        sp.dma_start(self.core.raw[:, u, 0:width], src).then_inc(self[f"raw_in{u}"], 16)

    def load_next(self, sp):
        for u, (src, width) in enumerate(self.following):
            if self.slots:
                sp.wait_ge(self["lo_done"], self.slots - (RAW - 1) + u)
            sp.dma_start(self.core.raw[:, u, 0:width], src).then_inc(self.next[f"raw_in{u}"], 16)

    def split_hi(self, act, sems, q, u, width):
        act.wait_ge(sems[f"raw_in{u}"], 16 * q + 16)
        act.activation(self.core.whi[:, u % HALF, 0:width], self.core.raw[:, u, 0:width], ACT.Copy).then_inc(sems["hi_done"], 1)

    def split_lo(self, dve, sems, q, u, width):
        dve.wait_ge(sems["hi_done"], 4 * q + u + 1)
        dve.tensor_tensor(self.core.wlo[:, u % HALF, 0:width], self.core.raw[:, u, 0:width],
                          self.core.whi[:, u % HALF, 0:width].bitcast(F32), ALU.subtract).then_inc(sems["lo_done"], 1)

    def hi(self, act, q, u, width, last=False):
        if not (last and u >= 2):
            self.split_hi(act, self, q + (u + 2) // 4, (u + 2) % 4, width)
        elif self.following:
            self.split_hi(act, self.next, 0, u - 2, self.following[u - 2][1])

    def lo(self, dve, q, u, width, last=False):
        if not (last and u >= 2):
            self.split_lo(dve, self, q + (u + 2) // 4, (u + 2) % 4, width)
        elif self.following:
            self.split_lo(dve, self.next, 0, u - 2, self.following[u - 2][1])

    def products(self, pe, q, u, out, xh, xl, k0, nk, first, last, ready=None):
        c = self.core
        pe.wait_ge(self["lo_done"], 4 * q + u + 1)
        for k in range(nk):
            w = slice(k * P, (k + 1) * P)
            h = u % HALF
            if ready is not None:
                pe.wait_ge(ready, k + 1)
            pe.matmul(out, c.whi[:, h, w], xh[:, k0 + k], start=first and k == 0, stop=False)
            pe.matmul(out, c.whi[:, h, w], xl[:, k0 + k], start=False, stop=False)
            mm = pe.matmul(out, c.wlo[:, h, w], xh[:, k0 + k], start=False, stop=last and k == nk - 1)
        mm.then_inc(self["slot_used"], 1)


def setup_phase(c, following):
    nc, d = c.nc, c.dram
    with ExitStack() as ctx:
        ph = Phase(c, ctx, "setup", "x_in consts_in kb_done ones_done", following=following)
        with nc.Block() as block:
            @block.sync
            def _(sp):
                sp.dma_start(c.x[:], d["xT"].rearrange("p (t n) -> p t n", t=DT)).then_inc(ph["x_in"], 16)
                ph.load_next(sp)
                sp.dma_start(c.consts[:], d["consts"]).then_inc(ph["consts_in"], 16)
                sp.wait_ge(ph["x_in"], 16)

            @block.scalar
            def _(act):
                for u in range(2):
                    ph.split_hi(act, ph.next, 0, u, D)
                act.wait_ge(ph["consts_in"], 16)
                act.activation(c.kb_all[:], c.consts[:, 0:N_BF16 * P], ACT.Copy).then_inc(ph["kb_done"], 1)

            @block.vector
            def _(dve):
                dve.memset(c.rstd[:], 1.0).then_inc(ph["ones_done"], 1)
                dve.memset(c.par[:, PG3:PG3 + DT], 1.0).then_inc(ph["ones_done"], 1)
                dve.memset(c.par[:, PB3:PB3 + DT], 0.0).then_inc(ph["ones_done"], 1)
                for u in range(2):
                    ph.split_lo(dve, ph.next, 0, u, D)
        ph.end()


NORM_SEMS = "xsum_done mean_done xc_done sq_done pair_done sq_used std_done rstd_done"
APPLY_SEMS = "xg_done x_done xh_done xl_done"


class Norm:

    def __init__(self, ph, c, x_done, layer):
        self.ph, self.c, self.x_done, self.layer = ph, c, x_done, layer
        self.sq = c.at(f"{ph.name}_sq", [P, 4, SEQ], F32, A_WORK)
        self.std = c.at(f"{ph.name}_std", [P, SEQ], F32, A_WORK + 8 * KB)
        self.xsum = c.rstd

    def pe(self, pe):
        ph, c = self.ph, self.c
        if self.layer:
            pe.wait_ge(ph["xsum_done"], DT + 1)
            pe.matmul(c.ps[:, 6], c.k["ones"], self.xsum[:], start=True, stop=True).then_inc(ph["mean_done"], 1)
        for j in range(DT // 2):
            pe.wait_ge(ph["pair_done"], j + 1)
            pe.matmul(c.ps[:, 7], c.k["ones"], self.sq[:, 2 * j % 4], start=j == 0, stop=j == DT // 2 - 1).then_inc(ph["sq_used"], 1)

    def act(self, act):
        ph, c = self.ph, self.c
        for t in range(DT):
            act.wait_ge(ph["xc_done"] if self.layer else self.x_done, t + 1)
            if t >= 4:
                act.wait_ge(ph["sq_used"], t // 2 - 1)
            act.activation(self.sq[:, t % 4], c.x[:, t], ACT.Square).then_inc(ph["sq_done"], 1)
        act.wait_ge(ph["sq_used"], DT // 2)
        act.activation(self.std[:], c.ps[:, 7], ACT.Sqrt, scale=1.0 / D,
                       bias=c.eps_ln if self.layer else c.eps_rms).then_inc(ph["std_done"], 1)

    def clear_sum(self, dve):
        dve.memset(self.xsum[:], 0.0).then_inc(self.ph["xsum_done"], 1)

    def sum_tile(self, dve, t):
        ph, c = self.ph, self.c
        dve.wait_ge(self.x_done, t + 1)
        dve.wait_ge(ph["xsum_done"], t + 1)
        dve.tensor_tensor(self.xsum[:], self.xsum[:], c.x[:, t], ALU.add).then_inc(ph["xsum_done"], 1)

    def dve(self, dve):
        ph, c = self.ph, self.c

        def pair(j):
            dve.wait_ge(ph["sq_done"], 2 * j + 2)
            a, b = self.sq[:, 2 * j % 4], self.sq[:, (2 * j + 1) % 4]
            dve.tensor_tensor(a, a, b, ALU.add).then_inc(ph["pair_done"], 1)

        if self.layer:
            dve.wait_ge(ph["mean_done"], 1)
            for t in range(DT):
                dve.scalar_tensor_tensor(c.x[:, t], c.ps[:, 6], -1.0 / D, c.x[:, t], ALU.mult, ALU.add).then_inc(ph["xc_done"], 1)
                if t % 2 == 1 and t >= 3:
                    pair(t // 2 - 1)
        for j in range(DT // 2 - 1 if self.layer else 0, DT // 2):
            pair(j)
        dve.wait_ge(ph["std_done"], 1)
        dve.reciprocal(c.rstd[:], self.std[:]).then_inc(ph["rstd_done"], 1)


class Apply:

    def __init__(self, ph, c, layer, g, b=None, keep=False, t_at=0):
        self.ph, self.c, self.layer, self.g, self.b, self.keep = ph, c, layer, g, b, keep
        self.t = None if layer else c.at(f"{ph.name}_t", [P, DT, SEQ], F32, A_WORK + t_at)

    def dst(self, t):
        return self.c.x[:, t] if self.layer else self.t[:, t]

    def act(self, act):
        ph, c = self.ph, self.c
        for t in range(DT + 1):
            if t < DT:
                act.wait_ge(ph["xg_done"], t + 1)
                if self.layer:
                    act.activation(c.xh[:, t], self.dst(t), ACT.Identity, bias=c.par[:, self.b + t:self.b + t + 1]).then_inc(ph["xh_done"], 1)
                else:
                    act.activation(c.xh[:, t], self.dst(t), ACT.Copy).then_inc(ph["xh_done"], 1)
            if t >= 1 and self.layer:
                act.wait_ge(ph["xl_done"], t)
                act.activation(c.x[:, t - 1], c.x[:, t - 1], ACT.Identity, bias=c.par[:, self.b + t - 1:self.b + t]).then_inc(ph["x_done"], 1)

    def dve(self, dve):
        ph, c = self.ph, self.c
        for t in range(DT + 1):
            if t < DT:
                dve.scalar_tensor_tensor(self.dst(t), c.x[:, t], c.par[:, self.g + t:self.g + t + 1], c.rstd[:],
                                         ALU.mult, ALU.mult).then_inc(ph["xg_done"], 1)
            if t >= 1 and not self.keep:
                k = t - 1
                dve.wait_ge(ph["xh_done"], k + 1)
                if self.layer:
                    dve.scalar_tensor_tensor(c.xl[:, k], c.x[:, k], c.par[:, self.b + k:self.b + k + 1], c.xh[:, k].bitcast(F32),
                                             ALU.add, ALU.subtract).then_inc(ph["xl_done"], 1)
                else:
                    dve.tensor_tensor(c.xl[:, k], self.dst(k), c.xh[:, k].bitcast(F32), ALU.subtract).then_inc(ph["xl_done"], 1)


def ffn_phase(c, name, f, before, res, half, side, following=None, par_src=None, final=None):
    nc, d = c.nc, c.dram
    UP, DOWN = 2 * FT, 2 * DT
    with ExitStack() as ctx:
        ph = Phase(c, ctx, name, "gate_done prod_done hh_done hl_done bank_free yb_done res_done par_in xo_done out_done " + NORM_SEMS + " " + APPLY_SEMS,
                   side=side, slots=UP + DOWN, following=following)
        hh = c.at(name + "_hh", [P, FT, SEQ], F32R, A_WORK)
        hl = c.at(name + "_hl", [P, FT, SEQ], F32R, A_WORK + FT * 2 * KB)
        gate = c.at(name + "_gate", [P, 2, SEQ], F32, A_WORK + FT * 4 * KB)
        layer = before[1] is not None
        apply = Apply(ph, c, layer, *before, t_at=64 * KB)
        norm = Norm(ph, c, ph["res_done"], layer)
        t_out = c.at(name + "_out", [P, DT, SEQ], F32, A_WORK + 8 * KB) if final else None
        with nc.Block() as block:
            @block.sync
            def _(sp):
                def up(q):
                    for u in range(4):
                        ph.load(sp, q, u, d["ffn_up"][f, 4 * q + u], D)

                def down(j):
                    for u in range(4):
                        ph.load(sp, j + UP // 4, u, d["ffn_down"][f, 4 * j + u], SLOT)

                up(1)
                if par_src is not None:
                    sp.wait_ge(ph["x_done"], DT)
                    sp.dma_start(c.par[:, 0:par_src.shape[-1]], par_src).then_inc(ph["par_in"], 16)
                    sp.wait_ge(ph["par_in"], 16)
                with sp.Fori(2, UP // 4) as q:
                    up(q)
                with sp.Fori(0, DOWN // 4) as j:
                    down(j)
                if following:
                    ph.load_next(sp)
                if final:
                    for t in range(DT):
                        sp.wait_ge(ph["xo_done"], t + 1)
                        sp.dma_start(c.outT[t * P:(t + 1) * P, :], t_out[:, t]).then_inc(ph["out_done"], 16)
                    sp.wait_ge(ph["out_done"], 16 * DT)

            @block.tensor
            def _(pe):
                def up(q):
                    for u in range(4):
                        pe.wait_ge(ph["bank_free"], 2 * q + u // 2 + 1)
                        ready = ph["xl_done"] if isinstance(q, int) and u == 0 else None
                        ph.products(pe, q, u, c.ps[:, u], c.xh, c.xl, 0, DT, True, True, ready)

                def down(j):
                    for u in range(4):
                        t = u // 2
                        if u % 2 == 0:
                            pe.wait_ge(ph["bank_free"], UP // 2 + 2 * j + t + 1)
                        ph.products(pe, j + UP // 4, u, c.ps[:, 4 + t], hh, hl, 11 * (u % 2), 11, u % 2 == 0, u % 2 == 1)

                up(0)
                with pe.Fori(1, UP // 4) as q:
                    up(q)
                pe.wait_ge(ph["hl_done"], FT)
                with pe.Fori(0, DOWN // 4) as j:
                    down(j)
                norm.pe(pe)

            @block.scalar
            def _(act):
                def evacuate_up(q, u):
                    act.wait_ge(ph["slot_used"], 4 * q + u + 1)
                    if u % 2 == 0:
                        act.activation(gate[:, u // 2], c.ps[:, u], ACT.Silu).then_inc(ph["gate_done"], 1)
                    else:
                        p = 2 * q + u // 2
                        act.wait_ge(ph["prod_done"], p + 1)
                        act.activation(hh[:, p], gate[:, u // 2], ACT.Copy).then_inc(ph["hh_done"], 1)

                def evacuate_down(j, u):
                    act.wait_ge(ph["slot_used"], 4 * j + u + 1 + UP)
                    if u % 2 == 1:
                        act.wait_ge(ph["bank_free"], UP // 2 + 2 * j + u // 2 + 1)
                        act.activation(gate[:, u // 2], c.ps[:, 4 + u // 2], ACT.Copy, scale=half).then_inc(ph["yb_done"], 1)

                def up(q, last=False):
                    for u in range(4):
                        evacuate_up(q, u)
                        ph.hi(act, q, u, SLOT if last and u >= 2 else D)

                def down(j, last=False):
                    for u in range(4):
                        evacuate_down(j, u)
                        ph.hi(act, j + UP // 4, u, SLOT, last)

                apply.act(act)
                with act.Fori(0, UP // 4 - 1) as q:
                    up(q)
                up(UP // 4 - 1, last=True)
                with act.Fori(0, DOWN // 4 - 1) as j:
                    down(j)
                down(DOWN // 4 - 1, last=True)
                norm.act(act)

            @block.vector
            def _(dve):
                def evacuate_up(q, u):
                    if u % 2 == 1:
                        p = 2 * q + u // 2
                        dve.wait_ge(ph["slot_used"], 4 * q + u + 1)
                        dve.wait_ge(ph["gate_done"], p + 1)
                        dve.tensor_tensor(gate[:, u // 2], gate[:, u // 2], c.ps[:, u], ALU.mult).then_inc(ph["prod_done"], 1)
                        dve.wait_ge(ph["hh_done"], p + 1)
                        dve.tensor_tensor(hl[:, p], gate[:, u // 2], hh[:, p].bitcast(F32), ALU.subtract).then_inc(ph["hl_done"], 1)
                        dve.wait_ge(ph["hl_done"], p + 1)
                        dve.nop().then_inc(ph["bank_free"], 1)

                def evacuate_down(j, u):
                    if u % 2 == 1:
                        t = 2 * j + u // 2
                        dve.wait_ge(ph["yb_done"], t + 1)
                        dve.scalar_tensor_tensor(c.x[:, t], c.x[:, t], res, gate[:, u // 2], ALU.mult, ALU.add).then_inc(ph["res_done"], 1)
                        if layer:
                            norm.sum_tile(dve, t)
                        dve.wait_ge(ph["res_done"], t + 1)
                        dve.nop().then_inc(ph["bank_free"], 1)

                def up(q, last=False):
                    for u in range(4):
                        evacuate_up(q, u)
                        ph.lo(dve, q, u, SLOT if last and u >= 2 else D)

                def down(j, last=False):
                    for u in range(4):
                        evacuate_down(j, u)
                        ph.lo(dve, j + UP // 4, u, SLOT, last)

                dve.nop().then_inc(ph["bank_free"], 2)
                apply.dve(dve)
                if layer:
                    norm.clear_sum(dve)
                with dve.Fori(0, UP // 4 - 1) as q:
                    up(q)
                up(UP // 4 - 1, last=True)
                if layer:
                    dve.wait_ge(ph["x_done"], DT)
                with dve.Fori(0, DOWN // 4 - 1) as j:
                    down(j)
                down(DOWN // 4 - 1, last=True)
                norm.dve(dve)
                if final:
                    dve.wait_ge(ph["rstd_done"], 1)
                    for t in range(DT):
                        dve.scalar_tensor_tensor(t_out[:, t], c.x[:, t], c.par[:, final + t:final + t + 1], c.rstd[:], ALU.mult,
                                                 ALU.mult).then_inc(ph["xo_done"], 1)
        ph.end()


def keep_clock(c, pe, bank, n):
    for _ in range(n):
        pe.matmul(c.ps[:, bank], c.kb["ident"], c.kb_all[:, 0:SEQ], start=True, stop=True, skip_group_check=True)


class Mixer:

    def __init__(self, c):
        W = A_WORK
        self.h = c.at("mix_h", [P, HT, SEQ], F32, W)
        self.hr = c.at("mix_h_split", [P, HT, SEQ], F32R, W)
        self.tok = c.at("mix_tok_sb", [P, QB, TW], F32, W + 40 * KB)
        self.y = c.at("mix_y", [P, QB, D], F32, W + 48 * KB)
        self.qm = c.at("mla_q", [96, HEADS, SEQ], F32, A_XH)
        self.km = c.at("mla_k", [96, HEADS, SEQ], F32, A_XH + 8 * KB)
        self.vm = c.at("mla_v", [P, QB, HEADS * HD], F32, A_XL)
        self.kc = c.at("cmp_k", [P, NCMP + 1], F32, A_XL + 12 * KB)
        self.kch = c.at("cmp_k_hi", [P, NCMP + 1], F32R, A_XL + 13 * KB)
        self.kcl = c.at("cmp_k_lo", [P, NCMP + 1], F32R, A_XL + 13 * KB + 128)
        xr = c.at("index_hi", [P, 4, SEQ], F32R, A_XL + 4 * KB)
        hi = {IDXQ: xr[:, 0], IDXQ + 1: xr[:, 1], IDXK: xr[:, 2], DSAK: xr[:, 3]}
        hi.update({t: self.hr[:, at] for t, at in ((NSAQ, 0), (NSAQ + 1, 1), (KSLC, 2), (KWIN, 3), (DSAQ, KCMP), (DSAQ + 1, VCMP))})
        self.split = {t: (hi[t], self.hr[:, t], self.h[:, t]) for t in (IDXQ, IDXQ + 1, IDXK, NSAQ, NSAQ + 1, KSLC, KWIN, DSAQ, DSAQ + 1, DSAK)}
        self.split["kc"] = (self.kch[:], self.kcl[:], self.kc[:])
        self.vc = c.at("cmp_v", [NCMP, HD], F32, A_XL + 12 * KB + 256)


def mixer_projections(c, m, l, following):
    nc, d = c.nc, c.dram
    with ExitStack() as ctx:
        ph = Phase(c, ctx, "proj", "bank_free tokw_in twh_done twl_done tok_done tok_out gates_done " + APPLY_SEMS, side=1, slots=HT, following=following)
        apply = Apply(ph, c, True, PG1, PB1)
        tw = c.at("tok_w", [P, DT, TW], F32, A_WORK + 64 * KB)
        twl = c.at("tok_w_lo", [P, DT, TW], F32R, A_WORK + 64 * KB)
        twh = c.at("tok_w_hi", [P, DT, TW], F32R, A_WORK + 80 * KB)
        with nc.Block() as block:
            @block.sync
            def _(sp):
                def four(q):
                    for u in range(4):
                        ph.load(sp, q, u, d["mix_in"][l, 4 * q + u], D)
                sp.dma_start(tw[:], d["mix_tok"][l].rearrange("p (t n) -> p t n", t=DT)).then_inc(ph["tokw_in"], 16)
                with sp.Fori(1, HT // 4) as q:
                    four(q)
                ph.load_next(sp)

            @block.tensor
            def _(pe):
                def four(q):
                    for u in range(4):
                        pe.wait_ge(ph["bank_free"], 4 * q + u + 1)
                        ready = ph["xl_done"] if isinstance(q, int) and u == 0 else None
                        ph.products(pe, q, u, c.ps[:, u], c.xh, c.xl, 0, DT, True, True, ready)
                four(0)
                with pe.Fori(1, HT // 4) as q:
                    four(q)
                pe.wait_ge(ph["twl_done"], DT)
                for b in range(QB):
                    out, at = c.ps[:, 4 + b, 0:TW], slice(b * P, (b + 1) * P)
                    for t in range(DT):
                        pe.matmul(out, c.xh[:, t, at], twh[:, t], start=t == 0, stop=False)
                        pe.matmul(out, c.xh[:, t, at], twl[:, t], start=False, stop=False)
                        mm = pe.matmul(out, c.xl[:, t, at], twh[:, t], start=False, stop=t == DT - 1)
                    mm.then_inc(ph["tok_done"], 1)

            @block.scalar
            def _(act):
                def four(q, last=False):
                    for u in range(4):
                        act.wait_ge(ph["slot_used"], 4 * q + u + 1)
                        act.activation(m.h[:, 4 * q + u], c.ps[:, u], ACT.Copy).then_inc(ph["bank_free"], 1)
                        ph.hi(act, q, u, D, last)
                act.nop().then_inc(ph["bank_free"], 4)
                apply.act(act)
                four(0)
                act.wait_ge(ph["tokw_in"], 16)
                for t in range(DT):
                    act.activation(twh[:, t], tw[:, t], ACT.Copy).then_inc(ph["twh_done"], 1)
                with act.Fori(1, HT // 4 - 1) as q:
                    four(q)
                four(HT // 4 - 1, last=True)
                for b in range(QB):
                    act.wait_ge(ph["tok_out"], b + 1)
                    gate = m.tok[:, b, GATE:GATE + 3 * HEADS]
                    act.activation(gate, gate, ACT.Sigmoid).then_inc(ph["gates_done"], 1)

            @block.vector
            def _(dve):
                def four(q, last=False):
                    for u in range(4):
                        ph.lo(dve, q, u, D, last)
                apply.dve(dve)
                four(0)
                for t in range(DT):
                    dve.wait_ge(ph["twh_done"], t + 1)
                    dve.tensor_tensor(twl[:, t], tw[:, t], twh[:, t].bitcast(F32), ALU.subtract).then_inc(ph["twl_done"], 1)
                with dve.Fori(1, HT // 4 - 1) as q:
                    four(q)
                four(HT // 4 - 1, last=True)
                for b in range(QB):
                    dve.wait_ge(ph["tok_done"], b + 1)
                    dve.tensor_copy(m.tok[:, b], c.ps[:, 4 + b, 0:TW]).then_inc(ph["tok_out"], 1)
        ph.end()


def mixer_preparation(c, m, l):
    nc, d = c.nc, c.dram
    W = A_WORK + 64 * KB
    t1 = c.at("rope_sin", [P, 2, SEQ], F32, W)
    t2 = c.at("rope_cos", [P, 2, SEQ], F32, W + 4 * KB)
    uq = c.at("uq_w", [P, 2, HEADS * 96], F32, W + 8 * KB)
    ukv = c.at("ukv_w", [P, 2, HEADS * HD], F32, W + 11 * KB)
    c1 = c.at("cmp_w1", [P, 2, 16, HD], F32, W + 13 * KB)
    c2 = c.at("cmp_w2", [64, 192], F32, W + 21 * KB)
    sq = c.at("lat_sq", [P, 3, SEQ], F32, W + 22 * KB)
    std = c.at("lat_std", [P, 2, SEQ], F32, W + 28 * KB)
    rstd = c.at("lat_rstd", [P, 2, SEQ], F32, W + 32 * KB)
    win = c.at("cmp_win", [P, 2, SEQ], F32, A_XL + 4 * KB)
    hid = c.at("cmp_hid", [64, 2, NCMP], F32, A_XL + 13 * KB)
    ropes = [(m.h[:, t], "sw64", c.cos64, c.sin64, 0, P) for t in (NSAQ, NSAQ + 1, KCMP, KSLC, KWIN, DSAQ, DSAQ + 1, DSAK)]
    ropes = [(m.h[:, t], "sw32", c.cos32, c.sin32, 0, P) for t in (KROPE, IDXQ, IDXQ + 1, IDXK)] + ropes
    kcmp_rope = 4 + 2
    ropes += [(m.qm[:, h], "sw32", c.cos32, c.sin32, 64, 96) for h in range(HEADS)]
    nh = len(ropes) - HEADS
    with ExitStack() as ctx:
        ph = Phase(c, ctx, "prep", "w_in c1_in c2_in swap_done cos_done sin_done rope_done sq_done sum_done std_done rstd_done "
                   "lat_done uq_done qm_done uk_done km_done kpe_done uv_done vm_done win_done hid_done gelu_done kv_done cmp_done pad_done ukv_in")
        with nc.Block() as block:
            @block.sync
            def _(sp):
                sp.dma_start(uq[:], d["mla_uq"][l].rearrange("p (t n) -> p t n", t=2)).then_inc(ph["w_in"], 16)
                sp.dma_start(ukv[:], d["mla_ukv"][l].rearrange("p (t n) -> p t n", t=2)).then_inc(ph["ukv_in"], 16)
                sp.dma_start(c1[:], d["cmp1"][l].rearrange("p (a j n) -> p a j n", a=2, j=16)).then_inc(ph["c1_in"], 16)
                sp.dma_start(c2[:], d["cmp2"][l]).then_inc(ph["c2_in"], 16)

            @block.tensor
            def _(pe):
                def swap(r):
                    src, sw, _, _, _, hi = ropes[r]
                    n = P if hi == P else 96
                    if r >= 2:
                        pe.wait_ge(ph["sin_done"], r - 1)
                    pe.matmul(c.ps[0:n, r % 2], c.k[sw][0:n, 0:n], src[0:n], start=True, stop=True).then_inc(ph["swap_done"], 1)

                swap(0)
                swap(1)
                pe.wait_ge(ph["sq_done"], 3)
                for t in range(3):
                    mm = pe.matmul(c.ps[:, 2 + t // 2], c.k["ones"], sq[:, t], start=t != 1, stop=t != 0)
                mm.then_inc(ph["sum_done"], 1)
                for r in range(2, nh):
                    swap(r)
                pe.wait_ge(ph["w_in"], 16)
                pe.wait_ge(ph["lat_done"], 3)
                for h in range(HEADS):
                    for t in range(2):
                        mm = pe.matmul(c.ps[0:96, 4 + h], uq[:, t, h * 96:(h + 1) * 96], m.h[:, CQ + t], start=t == 0, stop=t == 1)
                    mm.then_inc(ph["uq_done"], 1)
                for h in range(HEADS):
                    pe.wait_ge(ph["qm_done"], h + 1)
                    swap(nh + h)
                pe.wait_ge(ph["ukv_in"], 16)
                for h in range(HEADS):
                    pe.matmul(c.ps[0:64, 4 + h], ukv[:, 0, h * HD:(h + 1) * HD], m.h[:, CKV], start=True, stop=True).then_inc(ph["uk_done"], 1)
                pe.wait_ge(ph["std_done"], 2)
                for b in range(QB):
                    mm = pe.matmul(c.ps[:, 2 + b // 2, (b % 2) * 256:(b % 2) * 256 + 256], m.h[:, CKV, b * P:(b + 1) * P], ukv[:, 1],
                                   start=True, stop=True)
                mm.then_inc(ph["uv_done"], 1)
                pe.wait_ge(ph["c1_in"], 16)
                pe.wait_ge(ph["c2_in"], 16)
                pe.wait_ge(ph["win_done"], 4)
                pe.wait_ge(ph["km_done"], HEADS)
                for a in range(2):
                    for j in range(16):
                        mm = pe.matmul(c.ps[0:64, 4 + a, 0:NCMP], c1[:, a, j], win[:, a, j:j + 16 * (NCMP - 1) + 1:16], start=j == 0, stop=j == 15)
                mm.then_inc(ph["hid_done"], 1)
                pe.wait_ge(ph["gelu_done"], 2)
                pe.matmul(c.ps[:, 6, 0:NCMP], c2[:, 0:P], hid[:, 0], start=True, stop=True)
                pe.matmul(c.ps[0:NCMP, 7, 0:HD], hid[:, 1], c2[:, P:P + HD], start=True, stop=True).then_inc(ph["kv_done"], 1)

            @block.scalar
            def _(act):
                for t in range(3):
                    act.activation(sq[:, t], m.h[:, CQ + t], ACT.Square).then_inc(ph["sq_done"], 1)
                act.wait_ge(ph["sum_done"], 1)
                act.activation(std[:, 0], c.ps[:, 2], ACT.Sqrt, scale=1.0 / 256, bias=c.eps_rms).then_inc(ph["std_done"], 1)
                act.activation(std[:, 1], c.ps[:, 3], ACT.Sqrt, scale=1.0 / 128, bias=c.eps_rms).then_inc(ph["std_done"], 1)
                for h in range(HEADS):
                    act.wait_ge(ph["uq_done"], h + 1)
                    act.activation(m.qm[:, h], c.ps[0:96, 4 + h], ACT.Copy).then_inc(ph["qm_done"], 1)
                for h in range(HEADS):
                    act.wait_ge(ph["uk_done"], h + 1)
                    act.activation(m.km[0:64, h], c.ps[0:64, 4 + h], ACT.Copy).then_inc(ph["km_done"], 1)
                act.wait_ge(ph["uv_done"], 1)
                for b in range(2):
                    act.activation(m.vm[:, 2 * b:2 * b + 2], c.ps[:, 2 + b].rearrange("p (b n) -> p b n", b=2), ACT.Copy).then_inc(ph["vm_done"], 1)
                act.wait_ge(ph["hid_done"], 1)
                for a in range(2):
                    act.activation(hid[:, a], c.ps[0:64, 4 + a, 0:NCMP], ACT.Gelu_apprx_tanh).then_inc(ph["gelu_done"], 1)
                act.wait_ge(ph["kv_done"], 1)
                act.activation(m.kc[:, 0:NCMP], c.ps[:, 6, 0:NCMP], ACT.Copy).then_inc(ph["cmp_done"], 1)
                act.activation(m.vc[:], c.ps[0:NCMP, 7, 0:HD], ACT.Copy).then_inc(ph["cmp_done"], 1)

            @block.gpsimd
            def _(pool):
                for r, (src, _, cos, _, lo, hi) in enumerate(ropes):
                    if r >= 2:
                        pool.wait_ge(ph["rope_done"], r - 1)
                    if r >= nh:
                        pool.wait_ge(ph["qm_done"], r - nh + 1)
                        pool.wait_ge(ph["kpe_done"], HEADS)
                    pool.tensor_tensor(t2[lo:hi, r % 2], src[lo:hi], cos[lo:hi], ALU.mult).then_inc(ph["cos_done"], 1)
                    if r == nh - 1:
                        pool.wait_ge(ph["cos_done"], nh)
                        for h in range(HEADS):
                            pool.tensor_copy(m.km[64:96, h], m.h[64:96, KROPE]).then_inc(ph["kpe_done"], 1)

            @block.vector
            def _(dve):
                def rope(r):
                    src, _, _, sin, lo, hi = ropes[r]
                    dve.wait_ge(ph["swap_done"], r + 1)
                    dve.tensor_tensor(t1[lo:hi, r % 2], c.ps[lo:hi, r % 2], sin[lo:hi], ALU.mult).then_inc(ph["sin_done"], 1)
                    dve.wait_ge(ph["sin_done"], r + 1)
                    dve.wait_ge(ph["cos_done"], r + 1)
                    dve.tensor_tensor(src[lo:hi], t1[lo:hi, r % 2], t2[lo:hi, r % 2], ALU.add).then_inc(ph["rope_done"], 1)

                dve.memset(m.kc[:, NCMP:NCMP + 1], 0.0).then_inc(ph["pad_done"], 1)
                rope(0)
                rope(1)
                for n in range(2):
                    dve.wait_ge(ph["std_done"], n + 1)
                    dve.reciprocal(rstd[:, n], std[:, n]).then_inc(ph["rstd_done"], 1)
                dve.wait_ge(ph["rstd_done"], 2)
                for t in range(3):
                    g = c.par[:, PQN + t:PQN + t + 1]
                    dve.scalar_tensor_tensor(m.h[:, CQ + t], m.h[:, CQ + t], g, rstd[:, t // 2], ALU.mult, ALU.mult).then_inc(ph["lat_done"], 1)
                for r in range(2, nh):
                    rope(r)
                for a, t in enumerate((KCMP, VCMP)):
                    for lo in (0, 64):
                        off = 16 * (lo // 64)
                        pos = c.par[lo:lo + 64, PPOS:PPOS + 16].unsqueeze(1).broadcast_to([64, NCMP, 16])
                        src = m.h[lo:lo + 64, t, off:off + 16 * NCMP].rearrange("p (n j) -> p n j", j=16)
                        if a == 0:
                            dve.wait_ge(ph["rope_done"], kcmp_rope + 1)
                        dve.tensor_tensor(win[lo:lo + 64, a, 0:16 * NCMP].rearrange("p (n j) -> p n j", j=16), src, pos,
                                          ALU.add).then_inc(ph["win_done"], 1)
                for r in range(nh, len(ropes)):
                    rope(r)
        ph.end()


def attention_units(m, c):
    units = []

    def part(tile, h, at):
        return [x[64 * (h % 2):64 * (h % 2) + 64, at] for x in m.split[tile][:2]]

    for h in range(HEADS):
        for b in range(QB):
            units.append(dict(q=[m.qm[:, h, b * P:(b + 1) * P]], k=[m.km[:, h, 0:(b + 1) * P]], mask=c.kb["negd"], at=b * P, width=(b + 1) * P,
                              scale=96 ** -0.5, v=[m.vm[:, j, h * HD:(h + 1) * HD] for j in range(b + 1)], gate=None, mixer=0, h=h, b=b,
                              first=True, clamp=False))
    for h in range(HEADS):
        for b in range(QB):
            q = part(NSAQ + h // 2, h, slice(b * P, (b + 1) * P))
            units.append(dict(q=q, k=part("kc", h, slice(0, NCMP + 1)), mask=c.kb["cmpm"][:, b * NCMP:(b + 1) * NCMP], at=0, width=NCMP, scale=HD ** -0.5,
                              v=[m.vc[:]], gate=m.tok[:, b, GATE + h:GATE + h + 1], mixer=1, h=h, b=b, first=True, clamp=True))
            for br, (kt, vt) in enumerate(((KSLC, VSLC), (KWIN, VWIN))):
                g = GATE + (br + 1) * HEADS + h
                units.append(dict(q=q, k=part(kt, h, slice(0, (b + 1) * P)), mask=c.kb["negd"], at=b * P, width=(b + 1) * P,
                                  scale=HD ** -0.5, v=[m.tok[:, j, vt:vt + HD] for j in range(b + 1)], gate=m.tok[:, b, g:g + 1],
                                  mixer=1, h=h, b=b, first=False, clamp=False))
    return units


def dsa_units(m, c, allowed):
    units = []
    for h in range(HEADS):
        lo = 64 * (h % 2)
        for b in range(QB):
            mask = c.kb["negd"] if b == 0 else allowed[b]
            units.append(dict(q=[x[lo:lo + 64, b * P:(b + 1) * P] for x in m.split[DSAQ + h // 2][:2]],
                              k=[x[lo:lo + 64, 0:(b + 1) * P] for x in m.split[DSAK][:2]], mask=mask, at=0,
                              width=(b + 1) * P, scale=HD ** -0.5, v=[m.tok[:, j, DSAV:DSAV + HD] for j in range(b + 1)], gate=None,
                              mixer=2, h=h, b=b, first=True, clamp=False))
    return units


def mixer_attention(c, m, l):
    nc = c.nc
    W = A_WORK + 64 * KB
    p = c.at("att_p", [P, 3, SEQ], F32, W)
    pt = c.at("att_pt", [P, 2, SEQ], F32, W + 6 * KB)
    rel = c.at("idx_rel", [P, 4, SEQ], F32, W + 10 * KB)
    sizes = {b: (b + 1) * P for b in range(1, QB)}
    picked, allowed, off = {}, {}, W + 18 * KB
    for b in range(1, QB):
        picked[b] = c.at(f"idx_score{b}", [P, sizes[b]], F32, off)[:]
        off += sizes[b] * 4
    for b in range(1, QB):
        allowed[b] = c.at(f"idx_allowed{b}", [P, sizes[b]], BF16, off)[:]
        off += sizes[b] * 2
    stat = c.at("att_stat", [P, 4, 8], F32, off)
    top8 = c.at("idx_top", [P, 8], F32, off + 128)[:]
    units = attention_units(m, c)
    n_dsa = len(units)
    units += dsa_units(m, c, allowed)
    n = len(units)
    rels = [(b, h) for h in range(IDXH) for b in range(1, QB)]
    rounds = [(b, r) for b in range(1, QB) for r in range(TOPK // 8)]
    assert len(rounds) <= n_dsa - 4, "one round a unit"
    splits = list(m.split.values())
    n_index = 3
    with ExitStack() as ctx:
        ph = Phase(c, ctx, "att", "hi_done lo_done rel_done relu_done acc_done scores_done max_done nmax_done exp_done sum_done rinv_done scale_done t_done "
                   "pt_done pv_done y_done top_done took_done choice_done")
        with nc.Block() as block:
            @block.tensor
            def _(pe):
                def index_scores(i):
                    b, h = rels[i]
                    lo = 32 * (h % 4)
                    if i >= 4:
                        pe.wait_ge(ph["relu_done"], i - 3)
                    q = [x[lo:lo + 32, b * P:(b + 1) * P] for x in m.split[IDXQ + h // 4][:2]]
                    k = [x[lo:lo + 32, 0:sizes[b]] for x in m.split[IDXK][:2]]
                    out = c.ps[:, 4 + i % 4, 0:sizes[b]]
                    pe.matmul(out, q[0], k[0], start=True, stop=False)
                    pe.matmul(out, q[0], k[1], start=False, stop=False)
                    pe.matmul(out, q[1], k[0], start=False, stop=True).then_inc(ph["rel_done"], 1)

                def scores(u):
                    x = units[u]
                    if u >= 4:
                        pe.wait_ge(ph["exp_done"], u - 3)
                    if u == n_dsa:
                        pe.wait_ge(ph["choice_done"], QB - 1)
                    if len(x["q"]) == 2 and len(units[u - 1]["q"]) == 1:
                        pe.wait_ge(ph["lo_done"], len(splits))
                    s = c.ps[:, u % 4]
                    mw = x["mask"].shape[-1]
                    out = s[:, 0:x["k"][0].shape[-1]]
                    pe.matmul(out, x["q"][0], x["k"][0], start=True, stop=False)
                    if len(x["q"]) == 2:
                        pe.matmul(out, x["q"][0], x["k"][1], start=False, stop=False)
                        pe.matmul(out, x["q"][1], x["k"][0], start=False, stop=False)
                    pe.matmul(s[:, x["at"]:x["at"] + mw], c.kb["ident"], x["mask"], start=False, stop=True).then_inc(ph["scores_done"], 1)

                def transposes(u):
                    x = units[u]
                    if u >= 2:
                        pe.wait_ge(ph["pt_done"], u - 1)
                    keep_clock(c, pe, 6 + u % 2, 2)
                    pe.wait_ge(ph["exp_done"], u + 1)
                    for j in range(len(x["v"])):
                        w = min(P, x["width"])
                        mm = pe.transpose(c.ps[0:w, 6 + u % 2, j * P:(j + 1) * P], p[:, u % 3, j * P:j * P + w], c.k["ident"])
                    mm.then_inc(ph["t_done"], 1)

                def values(u):
                    x = units[u]
                    pe.wait_ge(ph["pt_done"], u + 1)
                    if u >= 2:
                        pe.wait_ge(ph["y_done"], u - 1)
                    w = min(P, x["width"])
                    for j, v in enumerate(x["v"]):
                        mm = pe.matmul(c.ps[:, 4 + u % 2, 0:HD], pt[0:w, u % 2, j * P:(j + 1) * P], v, start=j == 0, stop=j == len(x["v"]) - 1)
                    mm.then_inc(ph["pv_done"], 1)

                for u in range(3):
                    scores(u)
                pe.wait_ge(ph["lo_done"], n_index)
                for i in range(len(rels)):
                    index_scores(i)
                pe.wait_ge(ph["relu_done"], len(rels))
                for u in range(n):
                    if u + 3 < n:
                        scores(u + 3)
                    transposes(u)
                    if u >= 1:
                        values(u - 1)
                values(n - 1)

            @block.scalar
            def _(act):
                def hi(i):
                    act.activation(splits[i][0], splits[i][2], ACT.Copy).then_inc(ph["hi_done"], 1)

                for i in range(n_index):
                    hi(i)
                for i, (b, h) in enumerate(rels):
                    act.wait_ge(ph["rel_done"], i + 1)
                    if i >= 4:
                        act.wait_ge(ph["acc_done"], i - 3)
                    act.activation(rel[:, i % 4, 0:sizes[b]], c.ps[:, 4 + i % 4, 0:sizes[b]], ACT.Relu,
                                   scale=(IDXH * 32) ** -0.5).then_inc(ph["relu_done"], 1)

                def exponentials(u):
                    x = units[u]
                    act.wait_ge(ph["nmax_done"], u + 1)
                    if u >= 3:
                        act.wait_ge(ph["t_done"], u - 2)
                    act.activation(p[:, u % 3, 0:x["width"]], c.ps[:, u % 4, 0:x["width"]], ACT.Exp, scale=x["scale"],
                                   bias=stat[:, u % 4, 1:2], accum_out=stat[:, u % 4, 2:3]).then_inc(ph["exp_done"], 1)

                def copy_transposed(u):
                    x = units[u]
                    act.wait_ge(ph["t_done"], u + 1)
                    if u >= 2:
                        act.wait_ge(ph["pv_done"], u - 1)
                    w = min(P, x["width"])
                    act.activation(pt[0:w, u % 2, 0:len(x["v"]) * P], c.ps[0:w, 6 + u % 2, 0:len(x["v"]) * P], ACT.Copy).then_inc(ph["pt_done"], 1)

                exponentials(0)
                for u in range(n):
                    if u + 1 < n:
                        exponentials(u + 1)
                    if u < len(splits) - n_index:
                        hi(n_index + u)
                    copy_transposed(u)

            @block.vector
            def _(dve):
                took, allows = [0], [0]

                def largest():
                    if took[0] < len(rounds):
                        b, r = rounds[took[0]]
                        if took[0]:
                            dve.wait_ge(ph["took_done"], took[0])
                        else:
                            dve.wait_ge(ph["acc_done"], len(rels) + QB - 1)
                        dve.max(top8, picked[b]).then_inc(ph["top_done"], 1)

                def take():
                    if took[0] < len(rounds):
                        b, r = rounds[took[0]]
                        took[0] += 1
                        dve.wait_ge(ph["top_done"], took[0])
                        dve.match_replace(picked[b], top8, picked[b], TAKEN).then_inc(ph["took_done"], 1)

                def allow():
                    if took[0] and rounds[took[0] - 1][1] == TOPK // 8 - 1 and took[0] // (TOPK // 8) > allows[0]:
                        b = rounds[took[0] - 1][0]
                        allows[0] += 1
                        dve.wait_ge(ph["took_done"], took[0])
                        dve.tensor_scalar(allowed[b], picked[b], TAKEN, NEG, ALU.not_equal, ALU.mult).then_inc(ph["choice_done"], 1)

                def maximum(u):
                    x = units[u]
                    s = u % 4
                    dve.wait_ge(ph["scores_done"], u + 1)
                    dve.reduce_max(stat[:, s, 0:1], c.ps[:, u % 4, 0:x["width"]], AXX).then_inc(ph["max_done"], 1)

                def bias(u):
                    x = units[u]
                    s = u % 4
                    dve.wait_ge(ph["max_done"], u + 1)
                    dve.tensor_scalar(stat[:, s, 1:2], stat[:, s, 0:1], -x["scale"], 1e27, ALU.mult, ALU.min).then_inc(ph["nmax_done"], 1)

                def clamp_sum(u):
                    dve.wait_ge(ph["exp_done"], u + 1)
                    if units[u]["clamp"]:
                        total = stat[:, u % 4, 2:3]
                        dve.tensor_scalar(total, total, 1e-30, None, ALU.max).then_inc(ph["sum_done"], 1)

                def invert_sum(u):
                    if units[u]["clamp"]:
                        dve.wait_ge(ph["sum_done"], sum(y["clamp"] for y in units[:u + 1]))
                    dve.reciprocal(stat[:, u % 4, 3:4], stat[:, u % 4, 2:3]).then_inc(ph["rinv_done"], 1)

                def gate_scale(u):
                    dve.wait_ge(ph["rinv_done"], u + 1)
                    if units[u]["gate"] is not None:
                        dve.tensor_tensor(stat[:, u % 4, 4:5], stat[:, u % 4, 3:4], units[u]["gate"], ALU.mult).then_inc(ph["scale_done"], 1)

                def finish(u):
                    x = units[u]
                    scale = stat[:, u % 4, 3:4]
                    if x["gate"] is not None:
                        scale = stat[:, u % 4, 4:5]
                        dve.wait_ge(ph["scale_done"], sum(y["gate"] is not None for y in units[:u + 1]))
                    dve.wait_ge(ph["pv_done"], u + 1)
                    col = x["mixer"] * HEADS * HD + x["h"] * HD
                    out = m.y[:, x["b"], col:col + HD]
                    if x["first"]:
                        dve.tensor_scalar(out, c.ps[:, 4 + u % 2, 0:HD], scale, None, ALU.mult).then_inc(ph["y_done"], 1)
                    else:
                        dve.wait_ge(ph["y_done"], u)
                        dve.scalar_tensor_tensor(out, c.ps[:, 4 + u % 2, 0:HD], scale, out, ALU.mult, ALU.add).then_inc(ph["y_done"], 1)

                def lo(i):
                    dve.wait_ge(ph["hi_done"], i + 1)
                    dve.tensor_tensor(splits[i][1], splits[i][2], splits[i][0].bitcast(F32), ALU.subtract).then_inc(ph["lo_done"], 1)

                for i in range(n_index):
                    lo(i)
                for u in range(2):
                    maximum(u)
                    bias(u)
                for i, (b, h) in enumerate(rels):
                    dve.wait_ge(ph["relu_done"], i + 1)
                    wt = m.tok[:, b, IDXW + h:IDXW + h + 1]
                    src = rel[:, i % 4, 0:sizes[b]]
                    if h == 0:
                        dve.tensor_scalar(picked[b], src, wt, None, ALU.mult).then_inc(ph["acc_done"], 1)
                    else:
                        dve.wait_ge(ph["acc_done"], i - QB + 2)
                        dve.scalar_tensor_tensor(picked[b], src, wt, picked[b], ALU.mult, ALU.add).then_inc(ph["acc_done"], 1)
                dve.wait_ge(ph["acc_done"], len(rels))
                for b in range(1, QB):
                    own = picked[b][:, b * P:(b + 1) * P]
                    dve.tensor_tensor(own, own, c.k["negd"], ALU.add).then_inc(ph["acc_done"], 1)
                for u in range(n):
                    if u + 2 < n:
                        maximum(u + 2)
                    if u >= 1:
                        clamp_sum(u - 1)
                    largest()
                    if u + 2 < n:
                        bias(u + 2)
                    if u >= 1:
                        invert_sum(u - 1)
                    take()
                    if u >= 1:
                        gate_scale(u - 1)
                    allow()
                    if u >= 1:
                        finish(u - 1)
                    if u < len(splits) - n_index:
                        lo(n_index + u)
                for last in (clamp_sum, invert_sum, gate_scale, finish):
                    last(n - 1)
        ph.end()


def mixer_stick_breaking(c, m, l):
    nc = c.nc
    W = A_WORK + 64 * KB
    sp_ = c.at("sb_sp", [P, 2, QB, SEQ], F32, W)
    e = c.at("sb_e", [P, 3, SEQ], F32, W + 16 * KB)
    a = c.at("sb_a", [P, 2, SEQ], F32, W + 22 * KB)
    units = [(h, b) for h in range(HEADS) for b in reversed(range(QB))]
    n = len(units)
    splits = [(m.hr[:, DSAQ + i], m.hr[:, t], m.h[:, t], scale) for i, (t, scale) in
              enumerate(((SBQ, HD ** -0.5), (SBK, 1.0), (SBQ + 1, HD ** -0.5), (SBK + 1, 1.0)))]
    with ExitStack() as ctx:
        ph = Phase(c, ctx, "stick", "hi_done lo_done z_done abs_done e_done l_done spraw_done sp_done after_done a_done pv_done y_out")
        with nc.Block() as block:
            @block.tensor
            def _(pe):
                def scores(u):
                    h, b = units[u]
                    r = slice(64 * (h % 2), 64 * (h % 2) + 64)
                    if u >= 4:
                        pe.wait_ge(ph["a_done"], u - 3)
                    q = [x[r, b * P:SEQ] for x in splits[2 * (h // 2)][:2]]
                    k = [x[r, b * P:(b + 1) * P] for x in splits[2 * (h // 2) + 1][:2]]
                    out = c.ps[:, u % 4, b * P:SEQ]
                    if u in (0, 2 * QB):
                        pe.wait_ge(ph["lo_done"], 2 * (h // 2) + 2)
                    pe.matmul(out, k[0], q[0], start=True, stop=True, skip_group_check=True)
                    pe.matmul(out, k[0], q[1], start=False, stop=True, skip_group_check=True)
                    pe.matmul(out, k[1], q[0], start=False, stop=True, skip_group_check=True).then_inc(ph["z_done"], 1)

                def after(u):
                    h, b = units[u]
                    pe.wait_ge(ph["sp_done"], u + 1)
                    for j in range(b, QB):
                        pe.matmul(c.ps[:, u % 4, j * P:SEQ], c.k["ntri" if j == b else "nones"], sp_[:, h % 2, j, j * P:SEQ],
                                  start=False, stop=True, skip_group_check=True)
                    pe.matmul(c.ps[:, u % 4, b * P:(b + 1) * P], c.kb["ident"], c.kb["negs"], start=False, stop=True,
                              skip_group_check=True).then_inc(ph["after_done"], 1)

                def values(u):
                    h, b = units[u]
                    pe.wait_ge(ph["a_done"], u + 1)
                    if h >= 2 and b == QB - 1:
                        pe.wait_ge(ph["y_out"], h - 1)
                    for j in reversed(range(b, QB)):
                        mm = pe.matmul(c.ps[:, 4 + h % 2, j * HD:(j + 1) * HD], a[:, u % 2, j * P:(j + 1) * P],
                                       m.tok[:, b, SBV + h * HD:SBV + (h + 1) * HD], start=b == QB - 1 and j == QB - 1, stop=True, skip_group_check=True)
                    mm.then_inc(ph["pv_done"], 1)

                scores(0)
                scores(1)
                for u in range(n):
                    if u + 2 < n:
                        scores(u + 2)
                    after(u)
                    if u >= 1:
                        values(u - 1)
                values(n - 1)

            @block.scalar
            def _(act):
                for hi, _, src, scale in splits:
                    act.activation(hi, src, ACT.Copy, scale=scale).then_inc(ph["hi_done"], 1)

                def softplus_part(u):
                    h, b = units[u]
                    s = slice(b * P, SEQ)
                    act.wait_ge(ph["z_done"], u + 1)
                    if u >= 3:
                        act.wait_ge(ph["spraw_done"], u - 2)
                    act.activation(e[:, u % 3, s], c.ps[:, u % 4, s], ACT.Abs).then_inc(ph["abs_done"], 1)
                    act.wait_ge(ph["abs_done"], u + 1)
                    act.activation(e[:, u % 3, s], e[:, u % 3, s], ACT.Exp, scale=-1.0).then_inc(ph["e_done"], 1)
                    act.wait_ge(ph["e_done"], u + 1)
                    act.activation(e[:, u % 3, s], e[:, u % 3, s], ACT.Ln, bias=1.0).then_inc(ph["l_done"], 1)

                def weights(u):
                    h, b = units[u]
                    act.wait_ge(ph["after_done"], u + 1)
                    if u >= 2:
                        act.wait_ge(ph["pv_done"], u - 1)
                    act.activation(a[:, u % 2, b * P:SEQ], c.ps[:, u % 4, b * P:SEQ], ACT.Exp).then_inc(ph["a_done"], 1)

                act.preload_act_table_set("natural_log_exp_and_others")
                softplus_part(0)
                softplus_part(1)
                for u in range(n):
                    if u + 2 < n:
                        softplus_part(u + 2)
                    weights(u)

            @block.vector
            def _(dve):
                def softplus(u):
                    h, b = units[u]
                    s = slice(b * P, SEQ)
                    out = sp_[:, h % 2, b]
                    dve.wait_ge(ph["l_done"], u + 1)
                    if h >= 2 and b == QB - 1:
                        dve.wait_ge(ph["after_done"], QB * (h - 1))
                    dve.scalar_tensor_tensor(out[:, s], c.ps[:, u % 4, s], 0.0, e[:, u % 3, s], ALU.max, ALU.add).then_inc(ph["spraw_done"], 1)
                    dve.wait_ge(ph["spraw_done"], u + 1)
                    own = out[:, b * P:(b + 1) * P]
                    dve.tensor_tensor(own, own, c.k["strict"], ALU.mult).then_inc(ph["sp_done"], 1)

                def head_out(h):
                    col = 3 * HEADS * HD + h * HD
                    dve.wait_ge(ph["pv_done"], QB * (h + 1))
                    dve.tensor_copy(m.y[:, :, col:col + HD], c.ps[:, 4 + h % 2, 0:QB * HD].rearrange("p (b n) -> p b n", b=QB)).then_inc(ph["y_out"], 1)

                for i, (hi, lo, src, scale) in enumerate(splits):
                    dve.wait_ge(ph["hi_done"], i + 1)
                    dve.scalar_tensor_tensor(lo, src, scale, hi.bitcast(F32), ALU.mult, ALU.subtract).then_inc(ph["lo_done"], 1)
                for u in range(n):
                    softplus(u)
                    if u >= 2 and units[u - 2][1] == 0:
                        head_out(units[u - 2][0])
                head_out(HEADS - 1)
        ph.end()


def mixer_output(c, m, l, following):
    nc, d = c.nc, c.dram
    W = A_WORK + 64 * KB
    GW = HEADS * HD
    sq = c.at("gn_sq", [P, 4, GW], F32, W + 4 * KB)
    ssum = c.at("gn_sum", [P, 4, QB], F32, W + 1 * KB)
    std = c.at("gn_std", [P, 4, QB], F32, W + 1 * KB + 64)
    rstd = c.at("gn_rstd", [P, 4, QB], F32, W + 1 * KB + 128)
    with ExitStack() as ctx:
        ph = Phase(c, ctx, "mout", "gsq_done gstd_done grstd_done yg_done yt_done yh_done yl_done res_done " + NORM_SEMS, side=0, slots=DT, following=following)
        norm = Norm(ph, c, ph["res_done"], True)
        with nc.Block() as block:
            @block.sync
            def _(sp):
                for u in range(4):
                    ph.load(sp, 1, u, d["mix_out"][l, 4 + u], D)
                ph.load_next(sp)

            @block.tensor
            def _(pe):
                for g in range(4):
                    pe.wait_ge(ph["yg_done"], QB * (g + 1))
                    for t in (2 * g, 2 * g + 1):
                        if t >= 4:
                            pe.wait_ge(ph["yl_done"], t - 3)
                        for b in range(QB):
                            mm = pe.transpose(c.ps[:, t % 4, b * P:(b + 1) * P], m.y[:, b, t * P:(t + 1) * P], c.k["ident"])
                        mm.then_inc(ph["yt_done"], 1)
                for t in range(DT):
                    if t >= 2:
                        pe.wait_ge(ph["res_done"], t - 1)
                    ph.products(pe, t // 4, t % 4, c.ps[:, 4 + t % 2], c.xh, c.xl, 0, DT, True, True, ready=ph["yl_done"] if t == 0 else None)
                norm.pe(pe)

            @block.scalar
            def _(act):
                for g in range(4):
                    for b in range(QB):
                        n = g * QB + b
                        if n >= 4:
                            act.wait_ge(ph["gsq_done"], n - 3)
                        act.activation(sq[:, n % 4], m.y[:, b, g * GW:(g + 1) * GW], ACT.Square, accum_out=ssum[:, g, b:b + 1]).then_inc(ph["gsq_done"], 1)
                    act.wait_ge(ph["gsq_done"], QB * (g + 1))
                    act.activation(std[:, g], ssum[:, g], ACT.Sqrt, scale=1.0 / GW, bias=c.eps_rms).then_inc(ph["gstd_done"], 1)
                for t in range(DT):
                    act.wait_ge(ph["yt_done"], t + 1)
                    act.activation(c.xh[:, t], c.ps[:, t % 4], ACT.Copy, scale=c.par[:, PGN + t:PGN + t + 1]).then_inc(ph["yh_done"], 1)
                for t in range(DT):
                    act.wait_ge(ph["slot_used"], t + 1)
                    ph.hi(act, t // 4, t % 4, D, last=t >= 4)
                norm.act(act)

            @block.vector
            def _(dve):
                for g in range(4):
                    dve.wait_ge(ph["gstd_done"], g + 1)
                    dve.reciprocal(rstd[:, g], std[:, g]).then_inc(ph["grstd_done"], 1)
                    dve.wait_ge(ph["grstd_done"], g + 1)
                    for b in range(QB):
                        y = m.y[:, b, g * GW:(g + 1) * GW]
                        dve.tensor_scalar(y, y, rstd[:, g, b:b + 1], None, ALU.mult).then_inc(ph["yg_done"], 1)
                norm.clear_sum(dve)
                for t in range(DT):
                    dve.wait_ge(ph["yh_done"], t + 1)
                    dve.scalar_tensor_tensor(c.xl[:, t], c.ps[:, t % 4], c.par[:, PGN + t:PGN + t + 1], c.xh[:, t].bitcast(F32), ALU.mult,
                                             ALU.subtract).then_inc(ph["yl_done"], 1)
                for t in range(DT):
                    ph.lo(dve, t // 4, t % 4, D, last=t >= 4)
                    dve.wait_ge(ph["slot_used"], t + 1)
                    dve.scalar_tensor_tensor(c.x[:, t], c.x[:, t], ALPHA, c.ps[:, 4 + t % 2], ALU.mult, ALU.add).then_inc(ph["res_done"], 1)
                    norm.sum_tile(dve, t)
                norm.dve(dve)
        ph.end()


def mixer(c, m, l):
    d = c.dram
    mixer_projections(c, m, l, [(d["mix_out"][l, u], D) for u in range(4)])
    mixer_preparation(c, m, l)
    mixer_attention(c, m, l)
    mixer_stick_breaking(c, m, l)
    mixer_output(c, m, l, [(d["ffn_up"][2 * l + 1, u], D) for u in range(4)])


SSM_G = 4
SSM_SLOTS = 12
CH = SEQ // P
LRU_T = 10


class Second:

    def __init__(self, c):
        W = A_WORK
        self.ys = c.at("ssm_y", [P, 16, SEQ], F32, W)
        self.gs = c.at("ssm_gate", [P, DT, SEQ], F32, W + 32 * KB)
        self.mix = c.at("branch_sum", [P, DT, SEQ], F32, W + 80 * KB)
        self.dt = c.at("dt_rows", [P, CH, 32], F32, W + 96 * KB)
        self.da = c.at("da_rows", [P, CH, 32], F32, W + 96 * KB + 512)
        self.state = c.at("ssm_state", [P, 8 * HD], F32, W + 97 * KB)
        self.gates = c.at("lru_gates", [P, 4, SEQ], F32, W + 71 * KB)
        self.lh = c.at("lru_h", [P, LRU_T, SEQ], F32R, W)
        self.ll = c.at("lru_l", [P, LRU_T, SEQ], F32R, W + 20 * KB)


def second_head(c, s):
    nc, d = c.nc, c.dram
    W = A_WORK + 32 * KB
    v = c.at("dt_raw", [32, SEQ], F32, W)
    e = c.at("dt_e", [32, SEQ], F32, W + 2 * KB)
    da = c.at("dt_a", [32, SEQ], F32, W + 4 * KB)
    lam = c.at("lam", [P, 2, LRU_T], F32, W + 6 * KB)
    ea = c.at("ea", [32, 1], F32, W + 7 * KB)
    wdt = c.at("dt_w", [P, DT, 32], F32, W + 8 * KB)
    with ExitStack() as ctx:
        ph = Phase(c, ctx, "head", "par_in w_in dt_done nx_done nh_done nl_done v_done abs_done e_done l_done ea_done dtf_done daf_done turned lam_done coef_done rows_done " + NORM_SEMS + " " + APPLY_SEMS)
        before = Apply(ph, c, True, PG3, PB3)
        norm = Norm(ph, c, ph["x_done"], False)
        t_rms = c.at("head_t", [P, DT, SEQ], F32, A_WORK + 8 * KB)
        with nc.Block() as block:
            @block.sync
            def _(sp):
                sp.dma_start(wdt[:], d["w_dt"].rearrange("p (t n) -> p t n", t=DT)).then_inc(ph["w_in"], 16)
                sp.wait_ge(ph["x_done"], DT)
                sp.dma_start(c.par[:, 0:NPAR2], d["pars2"]).then_inc(ph["par_in"], 16)

            @block.tensor
            def _(pe):
                norm.pe(pe)
                pe.wait_ge(ph["w_in"], 16)
                for t in range(DT):
                    pe.wait_ge(ph["nx_done"], t + 1)
                    mm = pe.matmul(c.ps[0:32, 0], wdt[:, t], t_rms[:, t], start=t == 0, stop=t == DT - 1)
                mm.then_inc(ph["dt_done"], 1)
                pe.wait_ge(ph["dtf_done"], 1)
                for k in range(CH):
                    pe.transpose(c.ps[:, 1, k * 32:(k + 1) * 32], v[:, k * P:(k + 1) * P], c.k["ident"][0:32, 0:32])
                pe.wait_ge(ph["daf_done"], 1)
                for k in range(CH):
                    t = pe.transpose(c.ps[:, 1, (CH + k) * 32:(CH + k + 1) * 32], da[:, k * P:(k + 1) * P], c.k["ident"][0:32, 0:32])
                t.then_inc(ph["turned"], 1)

            @block.scalar
            def _(act):
                before.act(act)
                norm.act(act)
                for t in range(DT):
                    act.wait_ge(ph["nx_done"], t + 1)
                    act.activation(c.xh[:, t], t_rms[:, t], ACT.Copy).then_inc(ph["nh_done"], 1)
                act.wait_ge(ph["par_in"], 16)
                lo, hi = c.par[:, RLAM:RLAM + LRU_T], lam[:, 0]
                act.activation(hi, lo, ACT.Abs).then_inc(ph["lam_done"], 1)
                act.wait_ge(ph["lam_done"], 1)
                act.activation(hi, hi, ACT.Exp, scale=-1.0).then_inc(ph["lam_done"], 1)
                act.wait_ge(ph["lam_done"], 2)
                act.activation(hi, hi, ACT.Ln, bias=1.0).then_inc(ph["lam_done"], 1)
                act.activation(ea[:], c.par[0:32, RALOG:RALOG + 1], ACT.Exp).then_inc(ph["ea_done"], 1)
                act.wait_ge(ph["dt_done"], 1)
                act.activation(v[:], c.ps[0:32, 0], ACT.Identity, bias=c.par[0:32, RDTB:RDTB + 1]).then_inc(ph["v_done"], 1)
                act.wait_ge(ph["v_done"], 1)
                act.activation(e[:], v[:], ACT.Abs).then_inc(ph["abs_done"], 1)
                act.wait_ge(ph["abs_done"], 1)
                act.activation(e[:], e[:], ACT.Exp, scale=-1.0).then_inc(ph["e_done"], 1)
                act.wait_ge(ph["e_done"], 1)
                act.activation(e[:], e[:], ACT.Ln, bias=1.0).then_inc(ph["l_done"], 1)

            @block.vector
            def _(dve):
                before.dve(dve)
                norm.dve(dve)
                dve.wait_ge(ph["par_in"], 16)
                dve.wait_ge(ph["rstd_done"], 1)
                for t in range(DT + 1):
                    if t < DT:
                        dve.scalar_tensor_tensor(t_rms[:, t], c.x[:, t], c.par[:, RN1 + t:RN1 + t + 1], c.rstd[:], ALU.mult,
                                                 ALU.mult).then_inc(ph["nx_done"], 1)
                    if t >= 1:
                        dve.wait_ge(ph["nh_done"], t)
                        dve.tensor_tensor(c.xl[:, t - 1], t_rms[:, t - 1], c.xh[:, t - 1].bitcast(F32), ALU.subtract).then_inc(ph["nl_done"], 1)
                lo, hi = c.par[:, RLAM:RLAM + LRU_T], lam[:, 1]
                dve.wait_ge(ph["lam_done"], 3)
                dve.tensor_scalar(hi, lo, -1.0, 0.0, ALU.mult, ALU.max).then_inc(ph["coef_done"], 1)
                dve.wait_ge(ph["coef_done"], 1)
                dve.tensor_tensor(hi, hi, lam[:, 0], ALU.add).then_inc(ph["coef_done"], 1)
                dve.wait_ge(ph["coef_done"], 2)
                dve.tensor_scalar(lo, hi, -8.0, None, ALU.mult).then_inc(ph["coef_done"], 1)
                dve.wait_ge(ph["l_done"], 1)
                dve.scalar_tensor_tensor(v[:], v[:], 0.0, e[:], ALU.max, ALU.add).then_inc(ph["dtf_done"], 1)
                dve.wait_ge(ph["dtf_done"], 1)
                dve.wait_ge(ph["ea_done"], 1)
                dve.tensor_scalar(da[:], v[:], ea[:, 0:1], -1.0, ALU.mult, ALU.mult).then_inc(ph["daf_done"], 1)
                dve.wait_ge(ph["turned"], 1)
                dve.tensor_copy(s.dt[:], c.ps[:, 1, 0:CH * 32].rearrange("p (c h) -> p c h", h=32)).then_inc(ph["rows_done"], 1)
                dve.tensor_copy(s.da[:], c.ps[:, 1, CH * 32:2 * CH * 32].rearrange("p (c h) -> p c h", h=32)).then_inc(ph["rows_done"], 1)
        ph.end()


def ssm_group(c, s, g, side, following):
    nc, d = c.nc, c.dram
    W = A_WORK + 48 * KB
    PADW = SEQ + 4
    up = c.at("conv_in", [P, 6, PADW], F32, W)
    lm = c.at("ssm_m", [P, 8, P], F32, W)
    ce = c.at("ssm_ce", [P, 8, P], F32, W + 4 * KB)
    e2 = c.at("ssm_e2", [P, 8, P], F32, W + 8 * KB)
    xs = c.at("conv_out", [P, 6, SEQ], F32, W + 6 * PADW * 4)
    z = c.at("ssm_z", [P, 4, SEQ], F32, W + 6 * PADW * 4 + 12 * KB)
    o = W + 6 * PADW * 4 + 20 * KB
    xdt = c.at("ssm_xdt", [P, 8 * HD], F32, o)
    xdd = c.at("ssm_xdd", [P, 8 * HD], F32, o + 2 * KB)
    first = c.at("ssm_first", [P, 272], F32, o + 4 * KB)
    cb, bt, cs, tot = first[:, 0:P], first[:, P:2 * P], first[:, 256:264], first[:, 264:272]
    o += 64
    sm = c.at("ssm_small", [P, 4, 8], F32, o + 5 * KB)
    pg = c.at("ssm_par", [P, NPG], F32, o + 5 * KB + 128)
    dag = c.at("ssm_da_g", [P, CH, 8], F32, o + 5 * KB + 384)
    dtg = c.at("ssm_dt_g", [P, CH, 8], F32, o + 5 * KB + 512)
    sq = xs[:, 0:4]
    std, rstd = c.at("ssm_std", [P, SEQ], F32, W), c.at("ssm_rstd", [P, SEQ], F32, W + 2 * KB)
    with ExitStack() as ctx:
        ph = Phase(c, ctx, "ssm", "par_in pad_done evac_done conv_step conv_done silu_done z_done first_done e2_done masked_done cb_done ncs_done dd_done "
                   "dec_done xdt_done xdd_done l_done m_done ce_done y_done s_done yout_done hdec_done state_done gated_done sq_done sum_done "
                   "std_done rstd_done norm_done g_done", side=side, slots=SSM_SLOTS, following=following)
        with nc.Block() as block:
            @block.sync
            def _(sp):
                sp.dma_start(pg[:], d["pars_g"][g]).then_inc(ph["par_in"], 16)
                for k in range(4, SSM_SLOTS):
                    ph.load(sp, k // 4, k % 4, d["ssm_in"][g, k], D)
                ph.load_next(sp)

            @block.tensor
            def _(pe):
                def project(k):
                    if k >= 2:
                        pe.wait_ge(ph["evac_done"], k - 1)
                    ph.products(pe, k // 4, k % 4, c.ps[:, k % 2], c.xh, c.xl, 0, DT, True, True)

                def chunk_first(k):
                    ch = slice(k * P, (k + 1) * P)
                    pe.matmul(c.ps[:, 2, 0:P], xs[:, 0, ch], xs[:, 1, ch], start=True, stop=True)
                    pe.transpose(c.ps[:, 2, P:2 * P], xs[:, 0, ch], c.k["ident"])
                    pe.matmul(c.ps[:, 2, 256:264], c.k["triu"], dag[:, k], start=True, stop=True)
                    pe.matmul(c.ps[:, 2, 264:272], c.k["ones"], dag[:, k], start=True, stop=True)
                    if k >= 1:
                        pe.wait_ge(ph["xdt_done"], k)
                    for j in range(4):
                        pe.transpose(c.ps[:, 3, j * P:(j + 1) * P], xs[:, 2 + j, ch], c.k["ident"])
                    for h in range(8):
                        mm = pe.matmul(c.ps[:, 4 + h // 4, (h % 4) * P:(h % 4 + 1) * P], dag[:, k, h:h + 1].broadcast_to([P, P]), c.k["triu"],
                                       start=h % 4 == 0, stop=True, skip_group_check=True)
                    mm.then_inc(ph["first_done"], 1)
                    for b in range(2):
                        pe.wait_ge(ph["e2_done"], 2 * k + b + 1)
                        pe.matmul(c.ps[:, 4 + b].rearrange("p (h l) -> p h l", h=4), c.kb["ident"], c.kb["negl"].unsqueeze(1).broadcast_to([P, 4, P]),
                                  start=False, stop=True, skip_group_check=True).then_inc(ph["masked_done"], 1)

                def chunk_second(k):
                    pe.wait_ge(ph["xdd_done"], k + 1)
                    if k >= 1:
                        pe.wait_ge(ph["state_done"], k)
                    pe.wait_ge(ph["cb_done"], k + 1)
                    pe.matmul(c.ps[:, 7], bt, xdd[:], start=True, stop=True).then_inc(ph["s_done"], 1)
                    pe.wait_ge(ph["m_done"], 2 * k + 2)
                    pe.wait_ge(ph["ce_done"], 2 * k + 2)
                    if k == 0:
                        pe.wait_ge(ph["pad_done"], 2)
                    if k >= 1:
                        pe.wait_ge(ph["yout_done"], 4 * k)
                    for h in range(8):
                        lo = 64 * (h % 2)
                        out = c.ps[lo:lo + 64, 6, (h // 2) * P:(h // 2 + 1) * P]
                        pe.matmul(out, xdt[:, h * HD:(h + 1) * HD], lm[:, h], start=True, stop=False)
                        mm = pe.matmul(out, s.state[:, h * HD:(h + 1) * HD], ce[:, h], start=False, stop=True)
                    mm.then_inc(ph["y_done"], 1)

                for k in range(7):
                    project(k)
                pe.wait_ge(ph["silu_done"], 6)
                pe.wait_ge(ph["g_done"], 2)
                for k in range(CH):
                    chunk_first(k)
                    project(7 + k)
                    chunk_second(k)
                project(11)
                for j in range(4):
                    pe.wait_ge(ph["sq_done"], j + 1)
                    mm = pe.matmul(c.ps[:, 3], c.k["ones"], sq[:, j], start=j == 0, stop=j == 3)
                mm.then_inc(ph["sum_done"], 1)

            @block.scalar
            def _(act):
                act.wait_ge(ph["par_in"], 16)
                act.wait_ge(ph["pad_done"], 1)

                def evacuate(k):
                    act.wait_ge(ph["slot_used"], k + 1)
                    src = c.ps[:, k % 2]
                    if k < 6:
                        act.activation(up[:, k, 4:4 + SEQ], src, ACT.Copy).then_inc(ph["evac_done"], 1)
                    elif k < 10:
                        act.activation(z[:, k - 6], src, ACT.Silu).then_inc(ph["evac_done"], 1)
                    else:
                        t = g * 2 + (k - 10)
                        act.activation(s.gs[:, t], src, ACT.Sigmoid, bias=pg[:, GN + 4 + k - 10:GN + 5 + k - 10]).then_inc(ph["evac_done"], 1)
                    ph.hi(act, k // 4, k % 4, D, last=k >= 8)

                def silu(k):
                    act.wait_ge(ph["conv_done"], k + 1)
                    act.activation(xs[:, k], xs[:, k], ACT.Silu).then_inc(ph["silu_done"], 1)

                for k in range(7):
                    evacuate(k)
                    if k >= 3:
                        silu(k - 3)
                silu(4)
                silu(5)
                for k in range(CH):
                    act.wait_ge(ph["first_done"], k + 1)
                    for b in range(2):
                        if k >= 1:
                            act.wait_ge(ph["ce_done"], 2 * k)
                        act.activation(e2[:, 4 * b:4 * b + 4], c.ps[:, 4 + b].rearrange("p (h l) -> p h l", h=4), ACT.Exp).then_inc(ph["e2_done"], 1)
                    if k >= 1:
                        act.wait_ge(ph["y_done"], k)
                        act.wait_ge(ph["s_done"], k)
                        act.wait_ge(ph["state_done"], k)
                    act.activation(first[:], c.ps[:, 2, 0:272], ACT.Copy).then_inc(ph["cb_done"], 1)
                    act.wait_ge(ph["cb_done"], k + 1)
                    act.activation(sm[:, 3], tot, ACT.Exp).then_inc(ph["dec_done"], 1)
                    act.wait_ge(ph["dd_done"], k + 1)
                    act.activation(sm[:, 2], sm[:, 1], ACT.Exp).then_inc(ph["dec_done"], 1)
                    for b in range(2):
                        act.wait_ge(ph["masked_done"], 2 * k + b + 1)
                        for h in range(4 * b, 4 * b + 4):
                            e = act.activation(lm[:, h], c.ps[:, 4 + b, (h % 4) * P:(h % 4 + 1) * P], ACT.Exp, bias=sm[:, 0, h:h + 1])
                        e.then_inc(ph["l_done"], 1)
                    evacuate(7 + k)
                for j in range(4):
                    act.wait_ge(ph["gated_done"], j + 1)
                    act.activation(sq[:, j], s.ys[:, g * 4 + j], ACT.Square).then_inc(ph["sq_done"], 1)
                evacuate(11)
                act.wait_ge(ph["sum_done"], 1)
                act.activation(std[:], c.ps[:, 3], ACT.Sqrt, scale=1.0 / 512, bias=c.eps_rms).then_inc(ph["std_done"], 1)

            @block.vector
            def _(dve):
                dve.memset(up[:, :, 0:4], 0.0).then_inc(ph["pad_done"], 1)
                dve.memset(s.state[:], 0.0).then_inc(ph["pad_done"], 1)
                dve.tensor_copy(dag[:], s.da[:, :, bass.ds(g * 8, 8)]).then_inc(ph["g_done"], 1)
                dve.tensor_copy(dtg[:], s.dt[:, :, bass.ds(g * 8, 8)]).then_inc(ph["g_done"], 1)
                dve.wait_ge(ph["g_done"], 2)
                dve.wait_ge(ph["par_in"], 16)
                for k in range(6):
                    dve.wait_ge(ph["evac_done"], k + 1)
                    tap = lambda i: pg[:, GCW + 4 * k + i:GCW + 4 * k + i + 1]
                    dve.tensor_scalar(xs[:, k], up[:, k, 4:4 + SEQ], tap(3), pg[:, GCB + k:GCB + k + 1], ALU.mult, ALU.add).then_inc(ph["conv_step"], 1)
                    for i in range(3):
                        dve.wait_ge(ph["conv_step"], 3 * k + i + 1)
                        dve.scalar_tensor_tensor(xs[:, k], up[:, k, 1 + i:1 + i + SEQ], tap(i), xs[:, k], ALU.mult,
                                                 ALU.add).then_inc(ph["conv_step" if i < 2 else "conv_done"], 1)
                    ph.lo(dve, k // 4, k % 4, D)
                ph.lo(dve, 1, 2, D)

                for k in range(CH):
                    ch = slice(k * P, (k + 1) * P)
                    dve.wait_ge(ph["cb_done"], k + 1)
                    if k >= 1:
                        dve.wait_ge(ph["l_done"], 2 * k)
                    dve.tensor_scalar(sm[:, 0], cs, -1.0, None, ALU.mult).then_inc(ph["ncs_done"], 1)
                    dve.wait_ge(ph["ncs_done"], k + 1)
                    dve.tensor_tensor(sm[:, 1], sm[:, 0], tot, ALU.add).then_inc(ph["dd_done"], 1)
                    if k >= 1:
                        dve.wait_ge(ph["y_done"], k)
                        dve.wait_ge(ph["s_done"], k)
                    heads = "p (h d) -> p h d"
                    dve.tensor_tensor(xdt[:].rearrange(heads, d=HD), c.ps[:, 3].rearrange(heads, d=HD),
                                      dtg[:, k].unsqueeze(2).broadcast_to([P, 8, HD]), ALU.mult).then_inc(ph["xdt_done"], 1)
                    dve.wait_ge(ph["xdt_done"], k + 1)
                    dve.wait_ge(ph["dec_done"], 2 * k + 2)
                    dve.tensor_tensor(xdd[:].rearrange(heads, d=HD), xdt[:].rearrange(heads, d=HD),
                                      sm[:, 2].unsqueeze(2).broadcast_to([P, 8, HD]), ALU.mult).then_inc(ph["xdd_done"], 1)
                    for b in range(2):
                        hs = slice(4 * b, 4 * b + 4)
                        dve.wait_ge(ph["e2_done"], 2 * k + b + 1)
                        dve.tensor_tensor(ce[:, hs], e2[:, hs], xs[:, 1, ch].unsqueeze(1).broadcast_to([P, 4, P]), ALU.mult).then_inc(ph["ce_done"], 1)
                    for b in range(2):
                        hs = slice(4 * b, 4 * b + 4)
                        dve.wait_ge(ph["l_done"], 2 * k + b + 1)
                        dve.tensor_tensor(lm[:, hs], lm[:, hs], cb.unsqueeze(1).broadcast_to([P, 4, P]), ALU.mult).then_inc(ph["m_done"], 1)
                    ph.lo(dve, (7 + k) // 4, (7 + k) % 4, D, last=k >= 1)
                    dve.wait_ge(ph["y_done"], k + 1)
                    for j in range(4):
                        dve.scalar_tensor_tensor(s.ys[:, g * 4 + j, ch], xs[:, 2 + j, ch], pg[:, GD + j:GD + j + 1], c.ps[:, 6, j * P:(j + 1) * P],
                                                 ALU.mult, ALU.add).then_inc(ph["yout_done"], 1)
                    st = s.state[:].rearrange(heads, d=HD)
                    dve.tensor_tensor(st, st, sm[:, 3].unsqueeze(2).broadcast_to([P, 8, HD]), ALU.mult).then_inc(ph["hdec_done"], 1)
                    dve.wait_ge(ph["hdec_done"], k + 1)
                    dve.wait_ge(ph["s_done"], k + 1)
                    dve.tensor_tensor(s.state[:], s.state[:], c.ps[:, 7], ALU.add).then_inc(ph["state_done"], 1)
                dve.wait_ge(ph["yout_done"], 4 * CH)
                dve.wait_ge(ph["evac_done"], 10)
                for j in range(4):
                    y = s.ys[:, g * 4 + j]
                    dve.tensor_tensor(y, y, z[:, j], ALU.mult).then_inc(ph["gated_done"], 1)
                ph.lo(dve, 2, 3, D, last=True)
                dve.wait_ge(ph["std_done"], 1)
                dve.reciprocal(rstd[:], std[:]).then_inc(ph["rstd_done"], 1)
                dve.wait_ge(ph["rstd_done"], 1)
                dve.wait_ge(ph["gated_done"], 4)
                for j in range(4):
                    y = s.ys[:, g * 4 + j]
                    dve.scalar_tensor_tensor(y, y, pg[:, GN + j:GN + j + 1], rstd[:], ALU.mult, ALU.mult).then_inc(ph["norm_done"], 1)
        ph.end()


def ssm_output(c, s, following):
    nc, d = c.nc, c.dram
    yh = c.at("ssm_yh", [P, 16, SEQ], F32R, A_WORK + 48 * KB)
    yl = c.at("ssm_yl", [P, 16, SEQ], F32R, A_WORK)
    with ExitStack() as ctx:
        ph = Phase(c, ctx, "sout", "yh_done yl0_done yl1_done bank_free", side=0, slots=16, following=following)
        with nc.Block() as block:
            @block.sync
            def _(sp):
                with sp.Fori(1, 4) as q:
                    for u in range(4):
                        ph.load(sp, q, u, d["ssm_out"][4 * q + u], D)
                ph.load_next(sp)

            @block.tensor
            def _(pe):
                def four(q):
                    for u in range(4):
                        if u % 2 == 0:
                            pe.wait_ge(ph["bank_free"], 2 * q + u // 2 + 1)
                        ready = ph[f"yl{u}_done"] if isinstance(q, int) and u < 2 else None
                        ph.products(pe, q, u, c.ps[:, u // 2], yh, yl, 8 * (u % 2), 8, u % 2 == 0, u % 2 == 1, ready)
                four(0)
                with pe.Fori(1, 4) as q:
                    four(q)

            @block.scalar
            def _(act):
                for t in range(16):
                    act.activation(yh[:, t], s.ys[:, t], ACT.Copy).then_inc(ph["yh_done"], 1)

                def four(q, last=False):
                    for u in range(4):
                        act.wait_ge(ph["slot_used"], 4 * q + u + 1)
                        ph.hi(act, q, u, D, last)
                with act.Fori(0, 3) as q:
                    four(q)
                four(3, last=True)

            @block.vector
            def _(dve):
                for t in range(16):
                    dve.wait_ge(ph["yh_done"], t + 1)
                    dve.tensor_tensor(yl[:, t], s.ys[:, t], yh[:, t].bitcast(F32), ALU.subtract).then_inc(ph[f"yl{t // 8}_done"], 1)
                dve.nop().then_inc(ph["bank_free"], 2)

                def four(q, last=False):
                    for u in range(4):
                        ph.lo(dve, q, u, D, last)
                        if u % 2 == 1:
                            t = 2 * q + u // 2
                            dve.wait_ge(ph["slot_used"], 4 * q + u + 1)
                            dve.tensor_tensor(s.mix[:, t], s.gs[:, t], c.ps[:, u // 2], ALU.mult).then_inc(ph["bank_free"], 1)
                with dve.Fori(0, 3) as q:
                    four(q)
                four(3, last=True)
        ph.end()


def lru(c, s, following):
    nc, d = c.nc, c.dram
    W = A_WORK + 40 * KB
    PADW = SEQ + 4
    STEPS = LRU_T // 2
    names = "u r i a b gel".split()
    up = c.at("lru_pad", [P, 2, PADW], F32, W)
    B = {n: c.at("lru_" + n + "_t", [P, 2, SEQ], F32, W + 2 * PADW * 4 + 4 * KB * k) for k, n in enumerate(names)}
    wri = c.at("lru_w", [P, 2, 2, P], F32, W + 2 * PADW * 4 + 24 * KB)
    cols = c.at("lru_cols", [P, 2, 8], F32, W + 2 * PADW * 4 + 26 * KB)
    with ExitStack() as ctx:
        ph = Phase(c, ctx, "lru", "pad_done w_in0 w_in1 cols_in0 cols_in1 evac_done conv_step conv_done ri_done rsig_done isig_done tanh_done a_done "
                   "den_done rden_done b2_done sqrt_done iu_done b_done scan_done gel_done out_done lh_done ll_done gate_done", side=1, slots=2 * LRU_T + 4, following=following)
        with nc.Block() as block:
            @block.sync
            def _(sp):
                def four(q, first=False):
                    if not first:
                        for u in range(4):
                            ph.load(sp, q, u, d["lru_in"][4 * q + u], D)
                    for v in range(2):
                        if not first:
                            sp.wait_ge(ph["isig_done"], 2 * q)
                        sp.dma_start(wri[:, v], d["lru_ri"][2 * q + v].rearrange("p (a n) -> p a n", a=2)).then_inc(ph[f"w_in{v}"], 16)
                        sp.dma_start(cols[:, v], d["lru_cols"][2 * q + v]).then_inc(ph[f"cols_in{v}"], 16)
                four(0, first=True)
                with sp.Fori(1, STEPS) as q:
                    four(q)
                for u in range(4):
                    ph.load(sp, STEPS, u, d["lru_gate"][u], D)
                ph.load_next(sp)

            @block.tensor
            def _(pe):
                def gates(q, v):
                    pe.wait_ge(ph["conv_done"], 2 * q + v + 1)
                    pe.wait_ge(ph[f"w_in{v}"], 16 * q + 16)
                    for a in range(2):
                        if not isinstance(q, int):
                            pe.wait_ge(ph["isig_done" if a else "rsig_done"], 2 * q + v - 1)
                        pe.matmul(c.ps[:, 4 + 2 * a + v], wri[:, v, a], B["u"][:, v], start=True, stop=True).then_inc(ph["ri_done"], 1)

                def step(q):
                    for u in range(4):
                        if not isinstance(q, int):
                            pe.wait_ge(ph["gel_done" if u % 2 else "evac_done"], 2 * q + u // 2 - 1)
                        ph.products(pe, q, u, c.ps[:, u], c.xh, c.xl, 0, DT, True, True)
                        if u == 2:
                            gates(q, 0)
                    gates(q, 1)
                step(0)
                with pe.Fori(1, STEPS) as q:
                    step(q)
                for u in range(4):
                    pe.wait_ge(ph["gel_done" if u % 2 else "evac_done"], 2 * STEPS + u // 2 - 1)
                    ph.products(pe, STEPS, u, c.ps[:, u], c.xh, c.xl, 0, DT, True, True)

            @block.scalar
            def _(act):
                act.wait_ge(ph["pad_done"], 1)

                def step(q, front=True, tail=True):
                    def project(u):
                        if not front:
                            act.wait_ge(ph["slot_used"], 4 * q + u + 1)
                            act.activation(s.gates[:, u], c.ps[:, u], ACT.Sigmoid, bias=c.par[:, RBG + 8 + u:RBG + 9 + u]).then_inc(ph["gate_done"], 1)
                            ph.hi(act, q, u, D, last=True)
                        else:
                            act.wait_ge(ph["slot_used"], 4 * q + u + 1)
                            if u % 2 == 0:
                                act.activation(up[:, u // 2, 4:4 + SEQ], c.ps[:, u], ACT.Copy).then_inc(ph["evac_done"], 1)
                            ph.hi(act, q, u, D)

                    if tail:
                        for v in range(2):
                            act.wait_ge(ph["rsig_done"], 2 * q + v - 1)
                            act.activation(B["b"][:, v], B["r"][:, v], ACT.Tanh, scale=c.par[:, bass.ds(RLAM + 2 * q - 2 + v, 1)]).then_inc(ph["tanh_done"], 1)
                        for v in range(2):
                            act.activation(B["a"][:, v], B["r"][:, v], ACT.Exp, scale=c.par[:, bass.ds(RLAM + 2 * q - 2 + v, 1)]).then_inc(ph["a_done"], 1)
                        for v in range(2):
                            act.wait_ge(ph["tanh_done"], 2 * q + v - 1)
                            act.wait_ge(ph["a_done"], 2 * q + v - 1)
                            act.activation(B["r"][:, v], B["b"][:, v], ACT.Identity, scale=-1.0, bias=c.k["ones"][:, 0:1]).then_inc(ph["den_done"], 1)
                    project(0)
                    project(1)
                    project(2)
                    if tail:
                        for v in range(2):
                            act.wait_ge(ph["b2_done"], 2 * q + v - 1)
                            act.activation(B["b"][:, v], B["b"][:, v], ACT.Sqrt).then_inc(ph["sqrt_done"], 1)
                    project(3)
                    if tail:
                        for v in range(2):
                            act.wait_ge(ph["out_done"], 2 * q + v - 1)
                            act.activation(s.lh[:, 2 * q - 2 + v], B["gel"][:, v], ACT.Copy).then_inc(ph["lh_done"], 1)
                    if front:
                        for v in range(2):
                            if tail:
                                act.wait_ge(ph["ll_done"], 2 * q + v - 1)
                            act.activation(B["gel"][:, v], c.ps[:, 2 * v + 1], ACT.Gelu_apprx_tanh).then_inc(ph["gel_done"], 1)
                        for v in range(2):
                            act.wait_ge(ph[f"cols_in{v}"], 16 * q + 16)
                            act.wait_ge(ph["ri_done"], 4 * q + 2 * v + 2)
                            act.activation(B["r"][:, v], c.ps[:, 4 + v], ACT.Sigmoid, bias=cols[:, v, 5:6]).then_inc(ph["rsig_done"], 1)
                            act.activation(B["i"][:, v], c.ps[:, 6 + v], ACT.Sigmoid, bias=cols[:, v, 6:7]).then_inc(ph["isig_done"], 1)
                step(0, tail=False)
                with act.Fori(1, STEPS) as q:
                    step(q)
                step(STEPS, front=False)

            @block.vector
            def _(dve):
                dve.memset(up[:, :, 0:4], 0.0).then_inc(ph["pad_done"], 1)

                def step(q, front=True, tail=True):
                    def low(u):
                        ph.lo(dve, q, u, D, last=not front)

                    def conv(v):
                        if not front:
                            return
                        tap = lambda i: cols[:, v, i:i + 1]
                        dve.wait_ge(ph[f"cols_in{v}"], 16 * q + 16)
                        dve.wait_ge(ph["evac_done"], 2 * q + v + 1)
                        dve.tensor_scalar(B["u"][:, v], up[:, v, 4:4 + SEQ], tap(3), tap(4), ALU.mult, ALU.add).then_inc(ph["conv_step"], 1)
                        for i in range(3):
                            dve.wait_ge(ph["conv_step"], 6 * q + 3 * v + i + 1)
                            dve.scalar_tensor_tensor(B["u"][:, v], up[:, v, 1 + i:1 + i + SEQ], tap(i), B["u"][:, v], ALU.mult,
                                                     ALU.add).then_inc(ph["conv_step" if i < 2 else "conv_done"], 1)

                    def decay(v):
                        if not tail:
                            return
                        n = 2 * q + v - 1
                        t, r = B["b"][:, v], B["r"][:, v]
                        dve.wait_ge(ph["den_done"], n)
                        dve.reciprocal(r, r).then_inc(ph["rden_done"], 1)
                        dve.wait_ge(ph["rden_done"], n)
                        dve.scalar_tensor_tensor(t, t, -2.0, r, ALU.mult, ALU.mult).then_inc(ph["b2_done"], 1)

                    def scan(v):
                        if not tail:
                            return
                        n = 2 * q + v - 1
                        dve.wait_ge(ph["sqrt_done"], n)
                        dve.tensor_tensor(B["b"][:, v], B["b"][:, v], B["i"][:, v], ALU.mult).then_inc(ph["b_done"], 1)
                        dve.wait_ge(ph["b_done"], n)
                        dve.tensor_tensor_scan(B["i"][:, v], B["a"][:, v], B["b"][:, v], 0.0, ALU.mult, ALU.add).then_inc(ph["scan_done"], 1)
                        dve.wait_ge(ph["scan_done"], n)
                        dve.tensor_tensor(B["gel"][:, v], B["gel"][:, v], B["i"][:, v], ALU.mult).then_inc(ph["out_done"], 1)

                    conv(0)
                    low(0)
                    decay(0)
                    low(1)
                    decay(1)
                    conv(1)
                    low(2)
                    scan(0)
                    low(3)
                    scan(1)
                    if tail:
                        for v in range(2):
                            n = 2 * q + v - 1
                            dve.wait_ge(ph["lh_done"], n)
                            dve.tensor_tensor(s.ll[:, 2 * q - 2 + v], B["gel"][:, v], s.lh[:, 2 * q - 2 + v].bitcast(F32), ALU.subtract).then_inc(ph["ll_done"], 1)
                    if front:
                        for v in range(2):
                            dve.wait_ge(ph["isig_done"], 2 * q + v + 1)
                            dve.tensor_tensor(B["i"][:, v], B["i"][:, v], B["u"][:, v], ALU.mult).then_inc(ph["iu_done"], 1)
                            dve.wait_ge(ph["iu_done"], 2 * q + v + 1)
                step(0, tail=False)
                with dve.Fori(1, STEPS) as q:
                    step(q)
                step(STEPS, front=False)
        ph.end()


def lru_output(c, s, following):
    nc, d = c.nc, c.dram
    LW = LRU_T * P
    widths = [LW, D, LW]
    with ExitStack() as ctx:
        ph = Phase(c, ctx, "lout", "gate_done gated_done sum_done", side=0, slots=12, following=following)
        with nc.Block() as block:
            @block.sync
            def _(sp):
                for q, name in ((1, "lru_gate"), (2, "lru_out")):
                    for u in range(4):
                        ph.load(sp, q, u, d[name][4 + u], widths[q])
                ph.load_next(sp)

            @block.tensor
            def _(pe):
                for u in range(4):
                    ph.products(pe, 0, u, c.ps[:, u], s.lh, s.ll, 0, LRU_T, True, True)
                for u in range(4):
                    ph.products(pe, 1, u, c.ps[:, 4 + u], c.xh, c.xl, 0, DT, True, True)
                for u in range(4):
                    pe.wait_ge(ph["gated_done"], u + 1)
                    ph.products(pe, 2, u, c.ps[:, u], s.lh, s.ll, 0, LRU_T, True, True)

            @block.scalar
            def _(act):
                for q in range(3):
                    for u in range(4):
                        act.wait_ge(ph["slot_used"], 4 * q + u + 1)
                        if q == 1:
                            act.wait_ge(ph["sum_done"], u + 1)
                            act.activation(s.gates[:, u], c.ps[:, 4 + u], ACT.Sigmoid, bias=c.par[:, RBG + 12 + u:RBG + 13 + u]).then_inc(ph["gate_done"], 1)
                        ph.hi(act, q, u, widths[min(2, q + (u + 2) // 4)], last=q == 2)

            @block.vector
            def _(dve):
                for q in range(3):
                    for u in range(4):
                        ph.lo(dve, q, u, widths[min(2, q + (u + 2) // 4)], last=q == 2)
                        if q != 1:
                            n = 2 * q + u + 1
                            dve.wait_ge(ph["slot_used"], 4 * q + u + 1)
                            if q == 2:
                                dve.wait_ge(ph["gate_done"], u + 1)
                            t = 2 * q + u
                            dve.tensor_tensor(s.gates[:, u], s.gates[:, u], c.ps[:, u], ALU.mult).then_inc(ph["gated_done"], 1)
                            dve.wait_ge(ph["gated_done"], n)
                            dve.tensor_tensor(s.mix[:, t], s.mix[:, t], s.gates[:, u], ALU.add).then_inc(ph["sum_done"], 1)
        ph.end()


def second_output(c, s, following):
    nc, d = c.nc, c.dram
    with ExitStack() as ctx:
        ph = Phase(c, ctx, "bout", "mh_done ml_done res_done " + NORM_SEMS, side=1, slots=DT, following=following)
        norm = Norm(ph, c, ph["res_done"], False)
        with nc.Block() as block:
            @block.sync
            def _(sp):
                for t in range(4, DT):
                    ph.load(sp, t // 4, t % 4, d["b2_out"][t], D)
                ph.load_next(sp)

            @block.tensor
            def _(pe):
                for t in range(DT):
                    if t >= 2:
                        pe.wait_ge(ph["res_done"], t - 1)
                    ph.products(pe, t // 4, t % 4, c.ps[:, t % 2], c.xh, c.xl, 0, DT, True, True, ready=ph["ml_done"] if t == 0 else None)
                norm.pe(pe)

            @block.scalar
            def _(act):
                for t in range(DT):
                    act.activation(c.xh[:, t], s.mix[:, t], ACT.Copy).then_inc(ph["mh_done"], 1)
                for t in range(DT):
                    act.wait_ge(ph["slot_used"], t + 1)
                    ph.hi(act, t // 4, t % 4, D, last=t >= 4)
                norm.act(act)

            @block.vector
            def _(dve):
                for t in range(DT):
                    dve.wait_ge(ph["mh_done"], t + 1)
                    dve.tensor_tensor(c.xl[:, t], s.mix[:, t], c.xh[:, t].bitcast(F32), ALU.subtract).then_inc(ph["ml_done"], 1)
                for t in range(DT):
                    ph.lo(dve, t // 4, t % 4, D, last=t >= 4)
                    dve.wait_ge(ph["slot_used"], t + 1)
                    dve.tensor_tensor(c.x[:, t], c.x[:, t], c.ps[:, t % 2], ALU.add).then_inc(ph["res_done"], 1)
                norm.dve(dve)
        ph.end()


def program(nc, dram, outT):
    with ExitStack() as ctx:
        c = Core(nc, ctx, dram, outT)
        m = Mixer(c)

        def four(name, *at):
            src = dram[name]
            for i in at:
                src = src[i]
            return [(src[u], D) for u in range(4)]

        setup_phase(c, four("ffn_up", 0))
        with nc.Fori(0, DEPTH) as l:
            ffn_phase(c, "ffn1", l * 2, (PG3, PB3), ALPHA, 0.5, 0, four("mix_in", l), par_src=dram["pars"][l])
            mixer(c, m, l)
            ffn_phase(c, "ffn2", l * 2 + 1, (PG2, PB2), ALPHA, 0.5, 1, four("after_layer", l))
        s = Second(c)
        second_head(c, s)
        with nc.Fori(0, SSM_G // 2) as i:
            ssm_group(c, s, 2 * i, 0, four("ssm_in", 2 * i + 1))
            ssm_group(c, s, 2 * i + 1, 1, four("after_ssm", i))
        ssm_output(c, s, four("lru_in"))
        lru(c, s, [(dram["lru_out"][u], LRU_T * P) for u in range(4)])
        lru_output(c, s, four("b2_out"))
        second_output(c, s, four("ffn_up", 4))
        ffn_phase(c, "ffn3", 4, (RN2, None), 1.0, 1.0, 0, final=RNF)


def kernel(**inputs):
    import concourse.bacc as bacc
    from concourse.bass_utils import run_bass_kernel_spmd

    arrays = layout(inputs)
    nc = bacc.Bacc("TRN2", target_bir_lowering=False, num_devices=1)
    dram = {n: nc.dram_tensor("in_" + n, list(arrays[n].shape), F32, kind="ExternalInput").ap() for n in SHAPES}
    outT = nc.dram_tensor("outT", [D, SEQ], F32, kind="ExternalOutput").ap()
    program(nc, dram, outT)
    r = run_bass_kernel_spmd(nc, [{"in_" + n: arrays[n] for n in SHAPES}], core_ids=[0])
    return np.ascontiguousarray(r.results[0]["outT"].T).reshape(1, SEQ, D)
```
